# Optimizing a Trainium2 kernel written in Bass

```python
import numpy as np
import jax, jax.numpy as jnp
from jax import lax
import math

D_MODEL = 1024
BATCH = 1
SEQ = 1024
DEPTH = 1

RET_HEADS = 4
RET_DK = 128
RET_DV = 256
RET_CHUNK = 128
NSA_HEADS = 8
NSA_KV_GROUPS = 2
NSA_GROUP_HEADS = NSA_HEADS // NSA_KV_GROUPS
NSA_DK = 64
CMP_BLOCK = 32
CMP_STRIDE = 16
CMP_HIDDEN = 256
SEL_BLOCK = 64
SEL_TOPK = 8
WINDOW = 512
D_FF = 2816
CONV_W = 3

EPS = 1e-6
NEG = -1e30
FORCE = 1e9

IN_SIZES = (RET_HEADS * RET_DK, RET_HEADS * RET_DK, RET_HEADS * RET_DV, RET_HEADS * RET_DV,
            NSA_HEADS * NSA_DK,
            NSA_KV_GROUPS * NSA_DK, NSA_KV_GROUPS * NSA_DK, NSA_KV_GROUPS * NSA_DK,
            NSA_KV_GROUPS * NSA_DK, NSA_KV_GROUPS * NSA_DK, NSA_KV_GROUPS * NSA_DK,
            3 * NSA_HEADS, D_MODEL, D_MODEL)
N_IN = sum(IN_SIZES)


def rmsnorm(x, g):
    xf = x.astype(jnp.float32)
    y = xf * lax.rsqrt(jnp.mean(xf * xf, axis=-1, keepdims=True) + EPS) * g.astype(jnp.float32)
    return y.astype(x.dtype)

def retention(q, k, v, g, gn_g):
    B, S = q.shape[0], q.shape[1]
    H, C = RET_HEADS, RET_CHUNK
    NCH = S // C
    lg = jnp.log1p(-jnp.exp2(-5.0 - jnp.arange(H, dtype=jnp.float32)))
    pos = jnp.arange(C, dtype=jnp.float32)
    diff = pos[:, None] - pos[None, :]
    dmask = jnp.where(diff >= 0, jnp.exp(lg[:, None, None] * jnp.maximum(diff, 0.0)), 0.0)
    zeta = jnp.exp(lg[:, None] * (C - 1 - pos))
    xi = jnp.exp(lg[:, None] * (pos + 1.0))

    def to_chunks(t):
        return t.reshape(B, NCH, C, H, t.shape[-1]).transpose(0, 3, 1, 2, 4)

    qc = to_chunks(q)
    kc = to_chunks(k) * (RET_DK ** -0.5)
    vc = to_chunks(v)
    inner = jnp.einsum('bhncd,bhnmd->bhncm', qc, kc) * dmask[:, None]
    o_inner = jnp.einsum('bhncm,bhnme->bhnce', inner, vc)
    kv = jnp.einsum('bhnmd,bhnme->nbhde', kc * zeta[:, None, :, None], vc)
    chunk_decay = jnp.exp(lg * C).astype(kv.dtype)[:, None, None]

    def step(R, kv_n):
        return chunk_decay * R + kv_n, R

    R0 = jnp.zeros(kv.shape[1:], kv.dtype)
    _, R_prev = lax.scan(step, R0, kv)
    o_cross = jnp.einsum('bhncd,nbhde->bhnce', qc * xi[:, None, :, None], R_prev)
    o = (o_inner + o_cross).transpose(0, 2, 3, 1, 4).reshape(B, S, H, RET_DV)
    of = o.astype(jnp.float32)
    mu = jnp.mean(of, axis=-1, keepdims=True)
    var = jnp.mean(jnp.square(of - mu), axis=-1, keepdims=True)
    on = ((of - mu) * lax.rsqrt(var + EPS)).reshape(B, S, H * RET_DV) * gn_g.astype(jnp.float32)
    return (jax.nn.silu(g.astype(jnp.float32)) * on).astype(q.dtype)

def compress(t, pos_emb, w1, b1, w2):
    B, G, S, dk = t.shape
    npc = CMP_BLOCK // CMP_STRIDE
    NP = S // CMP_STRIDE
    pieces = t.reshape(B, G, NP, CMP_STRIDE, dk)
    blocks = jnp.concatenate([pieces[:, :, i:NP - (npc - 1) + i] for i in range(npc)], axis=3)
    blocks = (blocks + pos_emb).reshape(B, G, NP - npc + 1, CMP_BLOCK * dk)
    return jax.nn.gelu(blocks @ w1 + b1) @ w2

def nsa(q, kcr, vcr, ks, vs, kw, vw, gates,
        cmp_pos_k, cmp_w1_k, cmp_b1_k, cmp_w2_k, cmp_pos_v, cmp_w1_v, cmp_b1_v, cmp_w2_v):
    B, S = q.shape[0], q.shape[1]
    G, R, dk, T = NSA_KV_GROUPS, NSA_GROUP_HEADS, NSA_DK, SEL_BLOCK
    NS = S // SEL_BLOCK
    NQ = S // T
    k_eff = min(SEL_TOPK, NS)
    scale = dk ** -0.5
    qh = q.reshape(B, S, G, R, dk).transpose(0, 2, 3, 1, 4)

    def kvh(t):
        return t.reshape(B, S, G, dk).transpose(0, 2, 1, 3)

    kcr, vcr, ks, vs, kw, vw = [kvh(t) for t in (kcr, vcr, ks, vs, kw, vw)]
    slopes = jnp.exp2(-(jnp.arange(NSA_HEADS, dtype=jnp.float32) + 1.0)).reshape(G, R)
    tpos = jnp.arange(S, dtype=jnp.float32)

    kcmp = compress(kcr, cmp_pos_k, cmp_w1_k, cmp_b1_k, cmp_w2_k)
    vcmp = compress(vcr, cmp_pos_v, cmp_w1_v, cmp_b1_v, cmp_w2_v)
    NC = kcmp.shape[2]
    c_start = jnp.arange(NC) * CMP_STRIDE
    c_end = (c_start + CMP_BLOCK - 1).astype(jnp.float32)
    dcmp = tpos[:, None] - c_end[None, :]
    cmask = dcmp >= 0
    s = jnp.einsum('bgrtd,bgcd->bgrtc', qh, kcmp).astype(jnp.float32) * scale
    s = jnp.where(cmask, s - slopes[None, :, :, None, None] * dcmp, NEG)
    p_cmp = jax.nn.softmax(s, axis=-1) * cmask
    o_cmp = jnp.einsum('bgrtc,bgcd->bgrtd', p_cmp.astype(vcmp.dtype), vcmp)

    j_start = jnp.arange(NS) * SEL_BLOCK
    overlap = ((c_start[:, None] < j_start[None, :] + SEL_BLOCK) &
               (c_start[:, None] + CMP_BLOCK > j_start[None, :])).astype(jnp.float32)
    imp = jnp.einsum('bgrtc,cj->bgtj', p_cmp, overlap)
    cur = (jnp.arange(S) // SEL_BLOCK)[:, None]
    jj = jnp.arange(NS)[None, :]
    imp = jnp.where((jj == 0) | (jj == cur) | (jj == cur - 1), FORCE, imp)
    imp = jnp.where(jj > cur, -FORCE, imp)
    _, sel_idx = lax.top_k(imp, k_eff)

    ks_blk = ks.reshape(B, G, NS, SEL_BLOCK, dk)
    vs_blk = vs.reshape(B, G, NS, SEL_BLOCK, dk)
    kw_pad = jnp.pad(kw, ((0, 0), (0, 0), (WINDOW, 0), (0, 0)))
    vw_pad = jnp.pad(vw, ((0, 0), (0, 0), (WINDOW, 0), (0, 0)))
    bi = jnp.arange(B)[:, None, None, None]
    gi = jnp.arange(G)[None, :, None, None]
    sl = slopes[None, :, :, None]

    def block_fn(n):
        t0 = n * T
        qb = lax.dynamic_slice_in_dim(qh, t0, T, axis=3)
        tb = t0 + jnp.arange(T)
        idb = lax.dynamic_slice_in_dim(sel_idx, t0, T, axis=2)
        kb = ks_blk[bi, gi, idb]
        vb = vs_blk[bi, gi, idb]
        kpos = idb[..., None] * SEL_BLOCK + jnp.arange(SEL_BLOCK)
        dsel = (tb[None, None, :, None, None] - kpos).astype(jnp.float32)[:, :, None]
        ss = jnp.einsum('bgrtd,bgtnsd->bgrtns', qb, kb).astype(jnp.float32) * scale
        ss = jnp.where(dsel >= 0, ss - sl[..., None, None] * dsel, NEG)
        ps = jax.nn.softmax(ss.reshape(B, G, R, T, -1), axis=-1).reshape(ss.shape)
        o_sel = jnp.einsum('bgrtns,bgtnsd->bgrtd', ps.astype(vb.dtype), vb)
        kwb = lax.dynamic_slice_in_dim(kw_pad, t0, WINDOW + T, axis=2)
        vwb = lax.dynamic_slice_in_dim(vw_pad, t0, WINDOW + T, axis=2)
        wpos = t0 - WINDOW + jnp.arange(WINDOW + T)
        dw = tb[:, None] - wpos[None, :]
        wmask = (dw >= 0) & (dw < WINDOW) & (wpos[None, :] >= 0)
        sw = jnp.einsum('bgrtd,bgsd->bgrts', qb, kwb).astype(jnp.float32) * scale
        sw = jnp.where(wmask, sw - sl[..., None] * dw.astype(jnp.float32), NEG)
        pw = jax.nn.softmax(sw, axis=-1)
        o_win = jnp.einsum('bgrts,bgsd->bgrtd', pw.astype(vwb.dtype), vwb)
        return o_sel, o_win

    o_sel, o_win = lax.map(block_fn, jnp.arange(NQ))
    o_sel = o_sel.transpose(1, 2, 3, 0, 4, 5).reshape(B, G, R, S, dk)
    o_win = o_win.transpose(1, 2, 3, 0, 4, 5).reshape(B, G, R, S, dk)

    gt = jax.nn.sigmoid(gates.reshape(B, S, 3, G, R).transpose(2, 0, 3, 4, 1))[..., None]
    o = gt[0] * o_cmp + gt[1] * o_sel + gt[2] * o_win
    return o.transpose(0, 3, 1, 2, 4).reshape(B, S, NSA_HEADS * dk).astype(q.dtype)

def conv_ffn(h, w_up, conv_w, conv_b, w_down):
    S = h.shape[1]
    a, b = jnp.split(h @ w_up, 2, axis=-1)
    a_pad = jnp.pad(a, ((0, 0), (CONV_W - 1, 0), (0, 0)))
    ac = conv_b + sum(conv_w[i] * a_pad[:, i:i + S] for i in range(CONV_W))
    return (jax.nn.gelu(ac) * b) @ w_down

def first_inputs(seed: int = 0) -> dict:
    key = jax.random.key(seed)
    ks = jax.random.split(key, 24)
    f32 = jnp.float32

    def nrm(k, shape, fan_in):
        return jax.random.normal(k, shape, f32) * (fan_in ** -0.5)

    def gain(k, shape):
        return 1.0 + 0.01 * jax.random.normal(k, shape, f32)

    L = DEPTH
    return {
        "x": jax.random.normal(ks[0], (BATCH, SEQ, D_MODEL), f32),
        "norm_mix": gain(ks[1], (L, D_MODEL)),
        "w_in": nrm(ks[2], (L, D_MODEL, N_IN), D_MODEL),
        "ret_gn_g": gain(ks[3], (L, RET_HEADS * RET_DV)),
        "cmp_pos_k": 0.02 * jax.random.normal(ks[4], (L, CMP_BLOCK, NSA_DK), f32),
        "cmp_w1_k": nrm(ks[5], (L, CMP_BLOCK * NSA_DK, CMP_HIDDEN), CMP_BLOCK * NSA_DK),
        "cmp_b1_k": 0.01 * jax.random.normal(ks[6], (L, CMP_HIDDEN), f32),
        "cmp_w2_k": nrm(ks[7], (L, CMP_HIDDEN, NSA_DK), CMP_HIDDEN),
        "cmp_pos_v": 0.02 * jax.random.normal(ks[8], (L, CMP_BLOCK, NSA_DK), f32),
        "cmp_w1_v": nrm(ks[9], (L, CMP_BLOCK * NSA_DK, CMP_HIDDEN), CMP_BLOCK * NSA_DK),
        "cmp_b1_v": 0.01 * jax.random.normal(ks[10], (L, CMP_HIDDEN), f32),
        "cmp_w2_v": nrm(ks[11], (L, CMP_HIDDEN, NSA_DK), CMP_HIDDEN),
        "w_ret_o": nrm(ks[12], (L, RET_HEADS * RET_DV, D_MODEL), RET_HEADS * RET_DV),
        "w_nsa_o": nrm(ks[13], (L, NSA_HEADS * NSA_DK, D_MODEL), NSA_HEADS * NSA_DK),
        "w_out": nrm(ks[14], (L, D_MODEL, D_MODEL), D_MODEL),
        "norm_ffn": gain(ks[15], (L, D_MODEL)),
        "w_up": nrm(ks[16], (L, D_MODEL, 2 * D_FF), D_MODEL),
        "conv_w": nrm(ks[17], (L, CONV_W, D_FF), CONV_W),
        "conv_b": 0.01 * jax.random.normal(ks[18], (L, D_FF), f32),
        "w_down": nrm(ks[19], (L, D_FF, D_MODEL), D_FF),
        "norm_final": gain(ks[20], (D_MODEL,)),
    }

def first_block(x, norm_mix, w_in, ret_gn_g, cmp_pos_k, cmp_w1_k, cmp_b1_k, cmp_w2_k,
              cmp_pos_v, cmp_w1_v, cmp_b1_v, cmp_w2_v, w_ret_o, w_nsa_o, w_out,
              norm_ffn, w_up, conv_w, conv_b, w_down, norm_final):
    B, S, _ = x.shape
    split_at = list(np.cumsum(IN_SIZES)[:-1])
    for l in range(DEPTH):
        h = rmsnorm(x, norm_mix[l])
        proj = h @ w_in[l]
        (rq, rk, rv, rg, nq, kcr, vcr, ksl, vsl, kwn, vwn, ngate,
         ga, gb) = jnp.split(proj, split_at, axis=-1)
        y_a = retention(rq.reshape(B, S, RET_HEADS, RET_DK), rk.reshape(B, S, RET_HEADS, RET_DK),
                        rv.reshape(B, S, RET_HEADS, RET_DV), rg, ret_gn_g[l]) @ w_ret_o[l]
        y_b = nsa(nq, kcr, vcr, ksl, vsl, kwn, vwn, ngate,
                  cmp_pos_k[l], cmp_w1_k[l], cmp_b1_k[l], cmp_w2_k[l],
                  cmp_pos_v[l], cmp_w1_v[l], cmp_b1_v[l], cmp_w2_v[l]) @ w_nsa_o[l]
        merged = jax.nn.sigmoid(ga) * y_a + jax.nn.sigmoid(gb) * y_b
        x = x + merged @ w_out[l]
        x = x + conv_ffn(rmsnorm(x, norm_ffn[l]), w_up[l], conv_w[l], conv_b[l], w_down[l])
    return rmsnorm(x, norm_final)


_first_inputs = first_inputs


def first_inputs(seed=0):
    import zlib

    import numpy as np

    out = dict(_first_inputs(seed))
    spreads = {}
    factors = {'norm_mix': 6.662,
     'ret_gn_g': 8.0,
     'cmp_pos_k': 8.0,
     'cmp_b1_k': 8.0,
     'cmp_pos_v': 8.0,
     'cmp_b1_v': 8.0,
     'norm_ffn': 7.606,
     'conv_b': 8.0,
     'norm_final': 5.894}
    for name, (base, spread) in spreads.items():
        noise = np.random.default_rng([zlib.crc32(name.encode()), seed]).standard_normal(out[name].shape)
        drawn = base * np.exp(spread * noise) if base else spread * noise
        out[name] = __import__('jax').numpy.asarray(drawn.astype(out[name].dtype))
    for name, factor in factors.items():
        out[name] = (out[name] * factor).astype(out[name].dtype)
    return out


_narrow_inputs = first_inputs


def first_inputs(seed=0):

    out = dict(_narrow_inputs(seed))
    wider = {'ret_gn_g': 5.19,
     'cmp_pos_k': 4.45,
     'cmp_b1_k': 8.22,
     'cmp_pos_v': 12.0,
     'cmp_b1_v': 12.0,
     'norm_ffn': 5.35,
     'conv_b': 6.98,
     'norm_final': 6.64}
    for name, times in wider.items():
        mean = out[name].mean()
        out[name] = (mean + times * (out[name] - mean)).astype(out[name].dtype)
    return out


D_MIX = D_MODEL
D_RWKV = D_MIX // 2
D_S5 = D_MIX - D_RWKV
RWKV_HEAD = 64
N_RWKV_HEADS = D_RWKV // RWKV_HEAD
LORA_W = 64
LORA_A = 64
LORA_G = 128
S5_CH = 16
N_S5_GROUPS = D_S5 // S5_CH
S5_STATE = 64
D_FF_2 = ((8 * D_MODEL // 3 + 255) // 256) * 256
D_SHIFT = 3 * D_RWKV + LORA_W + LORA_A + LORA_G
D_IN = D_SHIFT + D_S5
NORM_EPS = 1e-6
LNX_EPS = 64e-5
DT_MIN = 1e-3
DT_MAX = 1e-1


def rms_norm(x, eps=NORM_EPS):
    xf = x.astype(jnp.float32)
    y = xf * lax.rsqrt(jnp.mean(xf * xf, axis=-1, keepdims=True) + eps)
    return y.astype(x.dtype)

def modulate(h, shift, scale):
    return h * (1.0 + scale[:, None, :]) + shift[:, None, :]

def rwkv7_time_mix(z, w0, w2, a0, a2, g2, k_k, k_a, r_k, lnx_w, lnx_b):
    out_dtype = z.dtype
    z = z.astype(jnp.float32)
    bsz, seq = z.shape[0], z.shape[1]
    H, N = N_RWKV_HEADS, RWKV_HEAD
    o = 0
    r = z[..., o:o + D_RWKV]; o += D_RWKV
    k = z[..., o:o + D_RWKV]; o += D_RWKV
    v = z[..., o:o + D_RWKV]; o += D_RWKV
    w_lo = z[..., o:o + LORA_W]; o += LORA_W
    a_lo = z[..., o:o + LORA_A]; o += LORA_A
    g_lo = z[..., o:o + LORA_G]

    w = -jax.nn.softplus(-(w0 + jnp.tanh(w_lo) @ w2)) - 0.5
    decay = jnp.exp(-jnp.exp(w))
    a = jax.nn.sigmoid(a0 + a_lo @ a2)
    g = jax.nn.sigmoid(g_lo) @ g2
    kk = (k * k_k).reshape(bsz, seq, H, N)
    kk = kk / jnp.maximum(jnp.linalg.norm(kk, axis=-1, keepdims=True), 1e-12)
    k = k * (1.0 + (a - 1.0) * k_a)

    heads = lambda t: t.reshape(bsz, seq, H, N)
    r_h, k_h, v_h, w_h, a_h = heads(r), heads(k), heads(v), heads(decay), heads(a)
    tm = lambda t: jnp.transpose(t, (1, 0, 2, 3))
    xs = (tm(r_h), tm(w_h), tm(k_h), tm(v_h), tm(-kk), tm(kk * a_h))

    def step(S, inp):
        r_t, w_t, k_t, v_t, a_t, b_t = inp
        sa = jnp.einsum("bhvk,bhk->bhv", S, a_t)
        S = S * w_t[:, :, None, :] + sa[..., None] * b_t[:, :, None, :] + v_t[..., None] * k_t[:, :, None, :]
        y = jnp.einsum("bhvk,bhk->bhv", S, r_t)
        return S, y

    S0 = jnp.zeros((bsz, H, N, N), jnp.float32)
    _, y = lax.scan(step, S0, xs)
    y = jnp.transpose(y, (1, 0, 2, 3))

    mu = jnp.mean(y, axis=-1, keepdims=True)
    var = jnp.mean(jnp.square(y - mu), axis=-1, keepdims=True)
    y = (y - mu) * lax.rsqrt(var + LNX_EPS) * lnx_w.reshape(H, N) + lnx_b.reshape(H, N)
    y = y + jnp.sum(r_h * k_h * r_k, axis=-1, keepdims=True) * v_h
    return (y.reshape(bsz, seq, D_RWKV) * g).astype(out_dtype)

def _ssm_combine(e1, e2):
    ar1, ai1, br1, bi1 = e1
    ar2, ai2, br2, bi2 = e2
    ar = ar2 * ar1 - ai2 * ai1
    ai = ar2 * ai1 + ai2 * ar1
    br = ar2 * br1 - ai2 * bi1 + br2
    bi = ar2 * bi1 + ai2 * br1 + bi2
    return ar, ai, br, bi

def s5_mix(u, a_re, a_im, log_dt, b_re, b_im, c_re, c_im, d_skip, w_glu, b_glu, gain):
    out_dtype = u.dtype
    u = u.astype(jnp.float32)
    bsz, seq = u.shape[0], u.shape[1]
    G, P = N_S5_GROUPS, S5_STATE
    ug = u.reshape(bsz, seq, G, S5_CH)

    dt = jnp.exp(log_dt)[:, None]
    mag = jnp.exp(dt * a_re)
    abar_re = mag * jnp.cos(dt * a_im)
    abar_im = mag * jnp.sin(dt * a_im)
    den = a_re * a_re + a_im * a_im
    p, q = abar_re - 1.0, abar_im
    coef_re = (p * a_re + q * a_im) / den
    coef_im = (q * a_re - p * a_im) / den
    bbar_re = coef_re[..., None] * b_re - coef_im[..., None] * b_im
    bbar_im = coef_re[..., None] * b_im + coef_im[..., None] * b_re

    bu_re = jnp.einsum("gpc,btgc->tbgp", bbar_re, ug)
    bu_im = jnp.einsum("gpc,btgc->tbgp", bbar_im, ug)
    a_seq_re = jnp.broadcast_to(abar_re[None, None], (seq, 1, G, P))
    a_seq_im = jnp.broadcast_to(abar_im[None, None], (seq, 1, G, P))
    _, _, s_re, s_im = lax.associative_scan(_ssm_combine, (a_seq_re, a_seq_im, bu_re, bu_im), axis=0)

    y = (jnp.einsum("gcp,tbgp->btgc", c_re, s_re) - jnp.einsum("gcp,tbgp->btgc", c_im, s_im)
         + d_skip * ug).reshape(bsz, seq, D_S5)
    zz = jax.nn.gelu(y)
    out = zz * jax.nn.sigmoid(zz @ w_glu + b_glu)
    return (rms_norm(out) * gain).astype(out_dtype)

def second_inputs(seed: int = 0) -> dict:
    key = jax.random.key(seed)
    ks = jax.random.split(key, 40)
    L = DEPTH
    nrm = lambda k, shape, s: jax.random.normal(k, shape, jnp.float32) * s
    uni = lambda k, shape, lo, hi: jax.random.uniform(k, shape, jnp.float32, lo, hi)
    H, N, G, P = N_RWKV_HEADS, RWKV_HEAD, N_S5_GROUPS, S5_STATE
    return {
        "x": nrm(ks[0], (BATCH, SEQ, D_MODEL), 1.0),
        "c": nrm(ks[1], (BATCH, D_MODEL), 1.0),
        "w_ada": nrm(ks[2], (L, D_MODEL, 6 * D_MODEL), D_MODEL ** -0.5),
        "b_ada": nrm(ks[3], (L, 6 * D_MODEL), 0.01),
        "w_in": nrm(ks[4], (L, D_MODEL, D_IN), D_MODEL ** -0.5),
        "mu_shift": uni(ks[5], (L, D_SHIFT), 0.0, 1.0),
        "rw_w0": uni(ks[6], (L, D_RWKV), -6.0, 1.0),
        "rw_w2": nrm(ks[7], (L, LORA_W, D_RWKV), 0.5 * LORA_W ** -0.5),
        "rw_a0": nrm(ks[8], (L, D_RWKV), 0.1),
        "rw_a2": nrm(ks[9], (L, LORA_A, D_RWKV), 0.5 * LORA_A ** -0.5),
        "rw_g2": nrm(ks[10], (L, LORA_G, D_RWKV), LORA_G ** -0.5),
        "rw_k_k": 0.85 + nrm(ks[11], (L, D_RWKV), 0.05),
        "rw_k_a": 1.0 + nrm(ks[12], (L, D_RWKV), 0.05),
        "rw_r_k": nrm(ks[13], (L, H, N), 0.1),
        "rw_lnx_w": 1.0 + nrm(ks[14], (L, D_RWKV), 0.05),
        "rw_lnx_b": nrm(ks[15], (L, D_RWKV), 0.01),
        "s5_a_re": -0.5 + nrm(ks[16], (L, G, P), 0.01),
        "s5_a_im": math.pi * jnp.arange(P, dtype=jnp.float32)[None, None, :] + nrm(ks[17], (L, G, P), 0.01),
        "s5_log_dt": uni(ks[18], (L, G), math.log(DT_MIN), math.log(DT_MAX)),
        "s5_b_re": nrm(ks[19], (L, G, P, S5_CH), (2 * S5_CH) ** -0.5),
        "s5_b_im": nrm(ks[20], (L, G, P, S5_CH), (2 * S5_CH) ** -0.5),
        "s5_c_re": nrm(ks[21], (L, G, S5_CH, P), (2 * P) ** -0.5),
        "s5_c_im": nrm(ks[22], (L, G, S5_CH, P), (2 * P) ** -0.5),
        "s5_d": nrm(ks[23], (L, G, S5_CH), 1.0),
        "s5_w_glu": nrm(ks[24], (L, D_S5, D_S5), D_S5 ** -0.5),
        "s5_b_glu": nrm(ks[25], (L, D_S5), 0.01),
        "s5_gain": 1.0 + nrm(ks[26], (L, D_S5), 0.05),
        "w_out": nrm(ks[27], (L, D_MIX, D_MODEL), D_MIX ** -0.5),
        "ffn_w_gate": nrm(ks[28], (L, D_MODEL, D_FF_2), D_MODEL ** -0.5),
        "ffn_w_up": nrm(ks[29], (L, D_MODEL, D_FF_2), D_MODEL ** -0.5),
        "ffn_w_down": nrm(ks[30], (L, D_FF_2, D_MODEL), D_FF_2 ** -0.5),
        "final_gain": 1.0 + nrm(ks[31], (D_MODEL,), 0.05),
    }

def second_block(x, c, w_ada, b_ada, w_in, mu_shift, rw_w0, rw_w2, rw_a0, rw_a2, rw_g2,
              rw_k_k, rw_k_a, rw_r_k, rw_lnx_w, rw_lnx_b, s5_a_re, s5_a_im, s5_log_dt,
              s5_b_re, s5_b_im, s5_c_re, s5_c_im, s5_d, s5_w_glu, s5_b_glu, s5_gain,
              w_out, ffn_w_gate, ffn_w_up, ffn_w_down, final_gain):
    c_act = jax.nn.silu(c)
    for l in range(DEPTH):
        ada = c_act @ w_ada[l] + b_ada[l]
        sh_m, sc_m, g_m, sh_f, sc_f, g_f = jnp.split(ada, 6, axis=-1)

        h = modulate(rms_norm(x), sh_m, sc_m)
        proj = h @ w_in[l]
        z = proj[..., :D_SHIFT]
        u = proj[..., D_SHIFT:]
        z_prev = jnp.pad(z[:, :-1], ((0, 0), (1, 0), (0, 0)))
        z = z + mu_shift[l] * (z_prev - z)
        y_rwkv = rwkv7_time_mix(z, rw_w0[l], rw_w2[l], rw_a0[l], rw_a2[l], rw_g2[l],
                                rw_k_k[l], rw_k_a[l], rw_r_k[l], rw_lnx_w[l], rw_lnx_b[l])
        y_s5 = s5_mix(u, s5_a_re[l], s5_a_im[l], s5_log_dt[l], s5_b_re[l], s5_b_im[l],
                      s5_c_re[l], s5_c_im[l], s5_d[l], s5_w_glu[l], s5_b_glu[l], s5_gain[l])
        mix = jnp.concatenate([y_rwkv, y_s5], axis=-1) @ w_out[l]
        x = x + g_m[:, None, :] * mix

        h = modulate(rms_norm(x), sh_f, sc_f)
        ffn = (jax.nn.silu(h @ ffn_w_gate[l]) * (h @ ffn_w_up[l])) @ ffn_w_down[l]
        x = x + g_f[:, None, :] * ffn
    return rms_norm(x) * final_gain


def setup_inputs(seed=0):
    out = dict(first_inputs(seed))
    for name, value in second_inputs(seed + 1).items():
        if name != "x":
            out[name + "_2"] = value
    return out


def reference(
    x, norm_mix, w_in, ret_gn_g, cmp_pos_k, cmp_w1_k, cmp_b1_k, cmp_w2_k, cmp_pos_v, cmp_w1_v,
    cmp_b1_v, cmp_w2_v, w_ret_o, w_nsa_o, w_out, norm_ffn, w_up, conv_w, conv_b, w_down,
    norm_final, c_2, w_ada_2, b_ada_2, w_in_2, mu_shift_2, rw_w0_2, rw_w2_2, rw_a0_2, rw_a2_2,
    rw_g2_2, rw_k_k_2, rw_k_a_2, rw_r_k_2, rw_lnx_w_2, rw_lnx_b_2, s5_a_re_2, s5_a_im_2,
    s5_log_dt_2, s5_b_re_2, s5_b_im_2, s5_c_re_2, s5_c_im_2, s5_d_2, s5_w_glu_2, s5_b_glu_2,
    s5_gain_2, w_out_2, ffn_w_gate_2, ffn_w_up_2, ffn_w_down_2, final_gain_2,
):
    x = first_block(
        x, norm_mix, w_in, ret_gn_g, cmp_pos_k, cmp_w1_k, cmp_b1_k, cmp_w2_k, cmp_pos_v,
        cmp_w1_v, cmp_b1_v, cmp_w2_v, w_ret_o, w_nsa_o, w_out, norm_ffn, w_up, conv_w, conv_b,
        w_down, norm_final,
    )
    return second_block(
        x, c_2, w_ada_2, b_ada_2, w_in_2, mu_shift_2, rw_w0_2, rw_w2_2, rw_a0_2, rw_a2_2,
        rw_g2_2, rw_k_k_2, rw_k_a_2, rw_r_k_2, rw_lnx_w_2, rw_lnx_b_2, s5_a_re_2, s5_a_im_2,
        s5_log_dt_2, s5_b_re_2, s5_b_im_2, s5_c_re_2, s5_c_im_2, s5_d_2, s5_w_glu_2, s5_b_glu_2,
        s5_gain_2, w_out_2, ffn_w_gate_2, ffn_w_up_2, ffn_w_down_2, final_gain_2,
    )


_drawn_inputs = setup_inputs


def setup_inputs(seed=0):
    import zlib

    import numpy as np

    out = dict(_drawn_inputs(seed))
    spreads = {}
    factors = {'cmp_b1_v': 3.581,
     'b_ada_2': 8.0,
     'rw_w2_2': 8.0,
     'rw_a0_2': 8.0,
     'rw_a2_2': 4.957,
     'rw_k_k_2': 23.07,
     'rw_k_a_2': 7.902,
     'rw_lnx_w_2': 32.166,
     'rw_lnx_b_2': 200.0,
     's5_a_re_2': 64.0,
     's5_a_im_2': 64.0,
     's5_log_dt_2': 64.0,
     's5_b_re_2': 64.0,
     's5_b_im_2': 64.0,
     's5_c_re_2': 64.0,
     's5_c_im_2': 64.0,
     's5_b_glu_2': 28.746,
     's5_gain_2': 24.631}
    for name, (base, spread) in spreads.items():
        noise = np.random.default_rng([zlib.crc32(name.encode()), seed]).standard_normal(out[name].shape)
        drawn = base * np.exp(spread * noise) if base else spread * noise
        out[name] = __import__('jax').numpy.asarray(drawn.astype(out[name].dtype))
    for name, factor in factors.items():
        out[name] = (out[name] * factor).astype(out[name].dtype)
    return out
```

```python
from contextlib import ExitStack, contextmanager

import numpy as np
import concourse.bass as bass
from concourse import mybir

P = 128
F32 = mybir.dt.float32
F32R = mybir.dt.float32r
ACT = mybir.ActivationFunctionType
ALU = mybir.AluOpType
AX = mybir.AxisListType.X

S = 1024
D = 1024
KD = D // P
NT = S // P
HALF = 512
NH = S // HALF
FT = 2816 // P
EPS = 1e-6

RQ, RK, RV, RG, NQ = 0, 4, 8, 16, 24
KCR, VCR, KS, VS, KW, VW, GATE, GA, GB = 28, 29, 30, 31, 32, 33, 34, 35, 43
N_PROJ = 51
GATE_COL = 4352
N_GATE = 24
RET_H, RET_DK, RET_DV = 4, 128, 256
NSA_H, NSA_G, NSA_D = 8, 2, 64
NC_PAD, N_CMP = 64, 63
CMP_LEN, CMP_STRIDE, CMP_HID = 32, 16, 256
N_BLK, SEL_K = 16, 8
WINDOW = 512
NEG = -1e30
FORCE = 1e9

N_PROJ2 = 18
ZR, ZK, ZV, ZLO, ZG, UU = 0, 4, 8, 12, 13, 14

KB = 1024
ARENA = 17 * KB


class Memory:

    def __init__(self, nc):
        self.nc = nc

    def at(self, name, kib, shape, dtype=F32):
        return self.nc.alloc_sbuf_tensor_at(name, shape, dtype, offset=ARENA + int(kib * KB))


@contextmanager
def phase(nc, names, banks=()):
    with ExitStack() as ctx:
        sems = {n: nc.alloc_semaphore(name=f"{n}_{nc.next_id()}") for n in names.split()}
        psum = {n: ctx.enter_context(nc.psum_tensor(f"{n}_{nc.next_id()}", shape, dt)) for n, shape, dt in banks}
        with nc.Block() as block:
            yield block, sems, psum
        nc.clear_and_free_semaphores(list(sems.values()))
        nc.all_engine_barrier()


class Steps:

    def __init__(self, eng, sem, base=0):
        self.eng, self.sem, self.base, self.n = eng, sem, base, 0

    def do(self, ins):
        self.n += 1
        ins.then_inc(self.sem, 1)
        return ins

    def wait(self):
        self.eng.wait_ge(self.sem, self.base + self.n)

    def link(self, ins):
        self.do(ins)
        self.wait()


def both(names):
    return " ".join(f"{n}{b}" for n in names.split() for b in range(2)) + " "


def pairs(eng, n, body):
    if n >= 4:
        with eng.Fori(0, n // 2) as p:
            for b in range(2):
                body(p, b)
    else:
        for p in range(n // 2):
            for b in range(2):
                body(p, b)
    if n % 2:
        body(n // 2, 0)


def gemm(nc, mem, name, n_units, k_tiles, weight, rhs, epilogue, at, tiles=None, extra="", extra_banks=()):
    raw = [mem.at(f"{name}_raw{b}", at + 4 * b, [P, KD, P]) for b in range(2)]
    w_hi = [mem.at(f"{name}_whi{b}", at + 8 + 4 * b, [P, KD, P], F32R) for b in range(2)]
    w_lo = [mem.at(f"{name}_wlo{b}", at + 16 + 4 * b, [P, KD, P], F32R) for b in range(2)]
    names = "weight_loaded0 weight_loaded1 hi_done0 hi_done1 split_done0 split_done1 products_done0 products_done1 "
    names += "acc_read0 acc_read1 vector_step scalar_step stored0 stored1 loaded0 loaded1 epilogue_a0 epilogue_a1 epilogue_b0 epilogue_b1 " + extra
    banks = [("acc0", [P, NH, HALF], F32), ("acc1", [P, NH, HALF], F32), *extra_banks]
    hi, lo = rhs
    with phase(nc, names, banks) as (block, s, ps):
        acc = [ps["acc0"], ps["acc1"]]

        @block.sync
        def _(sp):
            def load(p, b):
                sp.wait_ge(s[f"split_done{b}"], p)
                sp.dma_start(raw[b][:, 0:k_tiles, :], weight(2 * p + b)).then_inc(s[f"weight_loaded{b}"], 16)

            pairs(sp, n_units, load)

        @block.gpsimd
        def _(pool):
            def split(p, b):
                pool.wait_ge(s[f"weight_loaded{b}"], 16 * p + 16)
                pool.wait_ge(s[f"products_done{b}"], p)
                pool_high(nc, w_hi[b][:, 0:k_tiles, :], raw[b][:, 0:k_tiles, :], mem.one).then_inc(s[f"hi_done{b}"], 1)
                pool.wait_ge(s[f"hi_done{b}"], p + 1)
                nc.gpsimd.tensor_tensor(w_lo[b][:, 0:k_tiles, :], raw[b][:, 0:k_tiles, :], w_hi[b][:, 0:k_tiles, :],
                                        ALU.subtract).then_inc(s[f"split_done{b}"], 1)

            pairs(pool, n_units, split)

        @block.tensor
        def _(pe):
            def products(p, b):
                pe.wait_ge(s[f"split_done{b}"], p + 1)
                pe.wait_ge(s[f"acc_read{b}"], p)
                three_pass(nc, acc[b], w_hi[b], w_lo[b], hi, lo, k_tiles).then_inc(s[f"products_done{b}"], 1)

            pairs(pe, n_units, products)

        epilogue(block, s, acc, ps)


def pool_high(nc, out, x, one):
    return nc.gpsimd.tensor_tensor(out, x, one.unsqueeze(2).broadcast_to(x.shape), ALU.mult)


def three_pass(nc, acc, w_hi, w_lo, hi, lo, k_tiles, w_cols=slice(0, P), k0=0):
    last = None
    for k in range(k_tiles):
        for i, (w, x) in enumerate(((w_hi, hi), (w_hi, lo), (w_lo, hi))):
            for t in range(NH):
                last = nc.tensor.matmul(acc[:, t, :], w[:, k, w_cols], x[:, k0 + k, t * HALF:(t + 1) * HALF],
                                        start=(k == 0 and i == 0), stop=(k == k_tiles - 1 and i == 2))
    return last


VECTORS = [("norm_mix", 8), ("ret_gn_g", 8), ("cmp_b1_k", 2), ("cmp_b1_v", 2), ("norm_ffn", 8), ("conv_w", 66),
           ("conv_b", 22), ("norm_final", 8), ("mu_shift_2", 14), ("rw_w0_2", 4), ("rw_a0_2", 4), ("rw_k_k_2", 4),
           ("rw_k_a_2", 4), ("rw_r_k_2", 4), ("rw_lnx_w_2", 4), ("rw_lnx_b_2", 4), ("s5_b_glu_2", 4), ("s5_gain_2", 4),
           ("s5_d_2", 4), ("final_gain_2", 8), ("c_2", 8), ("b_ada_2", 48)]
PRM = {}
_row = 0
for _name, _n in VECTORS:
    if _row // P != (_row + _n - 1) // P:
        _row = (_row // P + 1) * P
    PRM[_name] = _row
    _row += _n
ADA = 256
PRM_ROWS = 2
PRM_COLS = ADA + 48 + 80
assert _row <= PRM_ROWS * P


def flat(ap):
    names = "abcdefgh"[:len(ap.shape)]
    return ap.rearrange(f"{' '.join(names)} -> ({' '.join(names)})") if len(ap.shape) > 1 else ap


def load_parameters(nc, mem, env, ins):
    xT, prm, ident = env["xT"], env["prm"], env["ident"]
    xin = [mem.at(f"xin{b}", 104 + 4 * b, [P, D]) for b in range(2)]
    rows = [mem.at(f"prm_rows{r}", 112 + r, [P, P]) for r in range(PRM_ROWS)]
    x = ins["x"].rearrange("a (i p) d -> (a i) p d", p=P)
    used = [0] * PRM_ROWS
    for name, n in VECTORS:
        used[PRM[name] // P] = PRM[name] % P + n
    with phase(nc, "x_loaded0 x_loaded1 rows_loaded const_loaded turned0 turned1 copied0 copied1 rows_turned rows_zero",
               [("turn0", [P, KD, P], F32), ("turn1", [P, KD, P], F32), ("rowsT", [P, PRM_ROWS, P], F32)]) as (block, s, ps):
        turn = [ps["turn0"], ps["turn1"]]

        @block.sync
        def _(sp):
            sp.dma_start(ident[:], ins["k_ident"]).then_inc(s["const_loaded"], 16)
            for i in range(NT):
                b = i % 2
                if i >= 2:
                    sp.wait_ge(s[f"turned{b}"], i // 2)
                sp.dma_start(xin[b][:], x[i]).then_inc(s[f"x_loaded{b}"], 16)

        @block.scalar
        def _(act):
            act.wait_ge(s["rows_zero"], PRM_ROWS)
            for name, n in VECTORS:
                r, at = divmod(PRM[name], P)
                act.dma_start(rows[r][at:at + n, :], flat(ins[name]).rearrange("(r p) -> r p", p=P)).then_inc(s["rows_loaded"], 16)

        @block.tensor
        def _(pe):
            pe.wait_ge(s["const_loaded"], 16)
            for i in range(NT):
                b = i % 2
                pe.wait_ge(s[f"x_loaded{b}"], 16 * (i // 2 + 1))
                if i >= 2:
                    pe.wait_ge(s[f"copied{b}"], i // 2)
                for k in range(KD):
                    last = nc.tensor.transpose(turn[b][:, k, :], xin[b][:, k * P:(k + 1) * P], ident[:])
                last.then_inc(s[f"turned{b}"], 1)
            pe.wait_ge(s["rows_loaded"], 16 * len(VECTORS))
            for r in range(PRM_ROWS):
                last = nc.tensor.transpose(ps["rowsT"][:, r, :], rows[r][:], ident[:])
            last.then_inc(s["rows_turned"], 1)

        @block.vector
        def _(dve):
            for r in range(PRM_ROWS):
                nc.vector.memset(rows[r][:], 0.0).then_inc(s["rows_zero"], 1)
            nc.vector.memset(env["ones"][:], 1.0)
            for i in range(NT):
                b = i % 2
                dve.wait_ge(s[f"turned{b}"], i // 2 + 1)
                nc.vector.tensor_copy(xT[:, :, i * P:(i + 1) * P], turn[b][:]).then_inc(s[f"copied{b}"], 1)
            dve.wait_ge(s["rows_turned"], 1)
            nc.vector.tensor_copy(prm[:, 0:PRM_ROWS * P], ps["rowsT"][:].rearrange("p r c -> p (r c)"))


def rms(nc, mem, env, name, at, emit, emit_names=""):
    xT, prm, ones = env["xT"], env["prm"], env["ones"]
    sq = [mem.at(f"{name}_sq{b}", at + 4 * b, [P, S]) for b in range(2)]
    sums = mem.at(f"{name}_sums", at + 8, [P, S])
    rstd = mem.at(f"{name}_rstd", at + 12, [P, S])
    mid = [mem.at(f"{name}_mid{b}", at + 16 + 4 * b, [P, S]) for b in range(2)]
    with phase(nc, "squared0 squared1 summed total rstd_done vector_step hi_done lo_done mid_done " + emit_names,
               [("tot", [P, NH, HALF], F32)]) as (block, s, ps):
        tot = ps["tot"]
        act_tail, dve_tail, pool_tail, sp_tail, pe_tail = emit(s, rstd, mid)

        @block.scalar
        def _(act):
            for k in range(KD):
                b = k % 2
                if k >= 2:
                    act.wait_ge(s["summed"], k - 1)
                nc.scalar.activation(sq[b][:], xT[:, k, :], ACT.Square).then_inc(s[f"squared{b}"], 1)
            act.wait_ge(s["vector_step"], 2)
            nc.scalar.activation(rstd[:], rstd[:], ACT.Sqrt).then_inc(s["rstd_done"], 1)
            act_tail(act)

        @block.vector
        def _(dve):
            for k in range(KD):
                dve.wait_ge(s[f"squared{k % 2}"], k // 2 + 1)
                if k == 0:
                    nc.vector.tensor_copy(sums[:], sq[0][:]).then_inc(s["summed"], 1)
                else:
                    dve.wait_ge(s["summed"], k)
                    nc.vector.tensor_tensor(sums[:], sums[:], sq[k % 2][:], ALU.add).then_inc(s["summed"], 1)
            dve.wait_ge(s["total"], 1)
            steps = Steps(dve, s["vector_step"])
            steps.link(nc.vector.tensor_scalar(rstd[:], tot[:].rearrange("p h t -> p (h t)"), 1.0 / D, EPS, ALU.mult, ALU.add))
            steps.link(nc.vector.reciprocal(rstd[:], rstd[:]))
            dve.wait_ge(s["rstd_done"], 1)
            dve_tail(dve)

        @block.tensor
        def _(pe):
            pe.wait_ge(s["summed"], KD)
            for t in range(NH):
                last = nc.tensor.matmul(tot[:, t, :], ones[:], sums[:, t * HALF:(t + 1) * HALF], start=True, stop=True)
            last.then_inc(s["total"], 1)
            if pe_tail:
                pe_tail(pe)

        if pool_tail:
            @block.gpsimd
            def _(pool):
                pool_tail(pool)

        if sp_tail:
            @block.sync
            def _(sp):
                sp_tail(sp)


def norm_split(nc, mem, env, name, gain=None, scale=None, shift=None):
    xT, prm, hi, lo = env["xT"], env["prm"], env["hi"], env["lo"]

    def emit(s, rstd, mid):
        def act_tail(act):
            for k in range(KD):
                act.wait_ge(s["mid_done"], k + 1)
                if scale is None:
                    nc.scalar.activation(hi[:, k, :], mid[k % 2][:], ACT.Copy).then_inc(s["hi_done"], 1)
                else:
                    nc.scalar.activation(mid[k % 2][:], mid[k % 2][:], ACT.Identity, bias=prm[:, shift + k:shift + k + 1],
                                         scale=prm[:, scale + k:scale + k + 1]).then_inc(s["modulated"], 1)
                    act.wait_ge(s["modulated"], k + 1)
                    nc.scalar.activation(hi[:, k, :], mid[k % 2][:], ACT.Copy).then_inc(s["hi_done"], 1)

        def dve_tail(dve):
            for k in range(KD):
                if k >= 2:
                    dve.wait_ge(s["lo_done"], k - 1)
                if gain is None:
                    nc.vector.tensor_tensor(mid[k % 2][:], xT[:, k, :], rstd[:], ALU.mult).then_inc(s["mid_done"], 1)
                else:
                    nc.vector.scalar_tensor_tensor(out=mid[k % 2][:], in0=xT[:, k, :], scalar=prm[:, gain + k:gain + k + 1],
                                                   in1=rstd[:], op0=ALU.mult, op1=ALU.mult).then_inc(s["mid_done"], 1)

        def pool_tail(pool):
            for k in range(KD):
                pool.wait_ge(s["hi_done"], k + 1)
                nc.gpsimd.tensor_tensor(lo[:, k, :], mid[k % 2][:], hi[:, k, :], ALU.subtract).then_inc(s["lo_done"], 1)

        return act_tail, dve_tail, pool_tail, None, None

    rms(nc, mem, env, name, 104, emit, "modulated")


def norm_in_place(nc, mem, env, name, gain):
    xT, prm = env["xT"], env["prm"]

    def emit(s, rstd, mid):
        def dve_tail(dve):
            for k in range(KD):
                nc.vector.scalar_tensor_tensor(out=xT[:, k, :], in0=xT[:, k, :], scalar=prm[:, gain + k:gain + k + 1],
                                               in1=rstd[:], op0=ALU.mult, op1=ALU.mult)

        return (lambda act: None), dve_tail, None, None, None

    rms(nc, mem, env, name, 104, emit)


def norm_out(nc, mem, env, name, gain, out):
    xT, prm, ident = env["xT"], env["prm"], env["ident"]
    rows = [mem.at(f"{name}_rows{b}", 128 + 4 * b, [P, D]) for b in range(2)]
    o = out.rearrange("a (i p) d -> (a i) p d", p=P)

    def emit(s, rstd, mid):
        turn = env["turn_out"]

        def dve_tail(dve):
            for k in range(KD):
                nc.vector.scalar_tensor_tensor(out=xT[:, k, :], in0=xT[:, k, :], scalar=prm[:, gain + k:gain + k + 1],
                                               in1=rstd[:], op0=ALU.mult, op1=ALU.mult).then_inc(s["scaled"], 1)

        def pe_tail(pe):
            pe.wait_ge(s["scaled"], KD)
            for i in range(NT):
                b = i % 2
                if i >= 2:
                    pe.wait_ge(s[f"rows_copied{b}"], i // 2)
                for k in range(KD):
                    last = nc.tensor.transpose(turn[b][:, k, :], xT[:, k, i * P:(i + 1) * P], ident[:])
                last.then_inc(s[f"turned{b}"], 1)

        def act_tail(act):
            for i in range(NT):
                b = i % 2
                act.wait_ge(s[f"turned{b}"], i // 2 + 1)
                if i >= 2:
                    act.wait_ge(s[f"row_stored{b}"], 16 * (i // 2))
                nc.scalar.activation(rows[b][:].rearrange("p (k f) -> p k f", k=KD), turn[b][:], ACT.Copy).then_inc(s[f"rows_copied{b}"], 1)

        def sp_tail(sp):
            for i in range(NT):
                b = i % 2
                sp.wait_ge(s[f"rows_copied{b}"], i // 2 + 1)
                sp.dma_start(o[i], rows[b][:]).then_inc(s[f"row_stored{b}"], 16)
            for b in range(2):
                sp.wait_ge(s[f"row_stored{b}"], 16 * (NT // 2))

        return act_tail, dve_tail, None, sp_tail, pe_tail

    with nc.psum_tensor(f"{name}_t0", [P, KD, P], F32) as t0, nc.psum_tensor(f"{name}_t1", [P, KD, P], F32) as t1:
        env["turn_out"] = [t0, t1]
        rms(nc, mem, env, name, 104, emit, "scaled rows_copied0 rows_copied1 turned0 turned1 row_stored0 row_stored1")


def store_epilogue(nc, mem, name, at, n_units, dst, step=1):
    stage = [mem.at(f"{name}_stage{b}", at + 4 * b, [P, S]) for b in range(2)]
    half = lambda b, h: stage[b][:].rearrange("p (j h m) -> p h m j", h=NH, j=step)[:, h]
    chunks = lambda b, h, acc: acc[b][:, h, :].rearrange("p (m j) -> p m j", j=step)

    def epilogue(block, s, acc, ps):
        @block.scalar
        def _(act):
            def copy(p, b):
                act.wait_ge(s[f"products_done{b}"], p + 1)
                act.wait_ge(s[f"stored{b}"], 16 * p)
                nc.scalar.activation(half(b, 0), chunks(b, 0, acc), ACT.Copy).then_inc(s[f"epilogue_a{b}"], 1)
                act.wait_ge(s[f"epilogue_a{b}"], p + 1)
                act.wait_ge(s[f"acc_read{b}"], p + 1)
                act.dma_start(dst[bass.ds((2 * p + b) * P, P), :], stage[b][:]).then_inc(s[f"stored{b}"], 16)

            pairs(act, n_units, copy)
            act.wait_ge(s["stored0"], 16 * ((n_units + 1) // 2))
            act.wait_ge(s["stored1"], 16 * (n_units // 2))

        @block.vector
        def _(dve):
            def copy(p, b):
                dve.wait_ge(s[f"products_done{b}"], p + 1)
                dve.wait_ge(s[f"stored{b}"], 16 * p)
                dve.wait_ge(s[f"epilogue_a{b}"], p + 1)
                nc.vector.tensor_copy(half(b, 1), chunks(b, 1, acc)).then_inc(s[f"acc_read{b}"], 1)

            pairs(dve, n_units, copy)

    return epilogue


def residual_gemm(nc, mem, env, name, weight, rhs, k_tiles, gate=None):
    xT, prm = env["xT"], env["prm"]

    def epilogue(block, s, acc, ps):
        @block.vector
        def _(dve):
            def add(p, b):
                dve.wait_ge(s[f"products_done{b}"], p + 1)
                u = 2 * p + b
                x = xT[:, bass.ds(u, 1), :].rearrange("p k (h t) -> p (k h) t", h=NH)
                if gate is None:
                    nc.vector.tensor_tensor(x, x, acc[b][:], ALU.add).then_inc(s[f"acc_read{b}"], 1)
                else:
                    nc.vector.scalar_tensor_tensor(out=x, in0=acc[b][:], scalar=prm[:, bass.ds(gate + u, 1)], in1=x,
                                                   op0=ALU.mult, op1=ALU.add).then_inc(s[f"acc_read{b}"], 1)

            pairs(dve, KD, add)

    gemm(nc, mem, name, KD, k_tiles, weight, rhs, epilogue, 104)


def columns(w, k_tiles):
    v = w.rearrange("a (k p) n -> (a p) k n", p=P)
    return lambda u: v[:, :, bass.ds(u * P, P)]


def feed_forward(nc, mem, env, name, up, down, kind, gate=None):
    xT, prm, hi, lo = env["xT"], env["prm"], env["hi"], env["lo"]
    C = FT // 2
    at = 104
    raw = [mem.at(f"{name}_raw{b}", at + 4 * b, [P, KD, P]) for b in range(2)]
    w_hi = [mem.at(f"{name}_whi{b}", at + 8 + 4 * b, [P, KD, P], F32R) for b in range(2)]
    w_lo = [mem.at(f"{name}_wlo{b}", at + 16 + 4 * b, [P, KD, P], F32R) for b in range(2)]
    d_raw = mem.at(f"{name}_draw", at + 24, [P, 2, D])
    d_hi = mem.at(f"{name}_dhi", at + 32, [P, 2, D], F32R)
    d_lo = mem.at(f"{name}_dlo", at + 40, [P, 2, D], F32R)
    g_hi = mem.at(f"{name}_ghi", at + 48, [P, 2, S], F32R)
    g_lo = mem.at(f"{name}_glo", at + 56, [P, 2, S], F32R)
    conv = mem.at(f"{name}_conv", at + 64, [P, S])
    act_out = mem.at(f"{name}_act", at + 68, [P, S])
    prod = [mem.at(f"{name}_prod{j}", at + 72 + 4 * j, [P, S]) for j in range(2)]
    names = ("up_loaded0 up_loaded1 up_hi0 up_hi1 up_split0 up_split1 up_done0 up_done1 a_read b_read "
             "down_loaded down_hi down_split down_done0 down_done1 chunk_done down_read0 down_read1 "
             "conv_done activated product_done g_hi_done g_split vector_step")
    banks = [(n, [P, NH, HALF], F32) for n in ("up0", "up1", "dn0", "dn1")]
    with phase(nc, names, banks) as (block, s, ps):
        acc = [ps["up0"], ps["up1"]]
        dn = [ps["dn0"], ps["dn1"]]

        def turns(eng, hidden, down):
            hidden(0, 0)
            hidden(0, 1)
            with eng.Fori(1, C) as c:
                hidden(c, 0)
                down(c - 1)
                hidden(c, 1)
            down(C - 1)

        @block.sync
        def _(sp):
            def load_up(c, j):
                for i in range(2):
                    sp.wait_ge(s[f"up_split{i}"], 2 * c + j)
                    sp.dma_start(raw[i][:], up(i, 2 * c + j)).then_inc(s[f"up_loaded{i}"], 16)

            def load_down(d):
                sp.wait_ge(s["down_split"], d)
                sp.dma_start(d_raw[:], down(d)).then_inc(s["down_loaded"], 16)

            turns(sp, load_up, load_down)

        @block.gpsimd
        def _(pool):
            def split_up(c, j):
                for i in range(2):
                    pool.wait_ge(s[f"up_loaded{i}"], 32 * c + 16 * (j + 1))
                    pool.wait_ge(s[f"up_done{i}"], 2 * c + j)
                    pool_high(nc, w_hi[i][:], raw[i][:], mem.one).then_inc(s[f"up_hi{i}"], 1)
                    pool.wait_ge(s[f"up_hi{i}"], 2 * c + j + 1)
                    nc.gpsimd.tensor_tensor(w_lo[i][:], raw[i][:], w_hi[i][:], ALU.subtract).then_inc(s[f"up_split{i}"], 1)

            def split_down(d):
                pool.wait_ge(s["down_loaded"], 16 * d + 16)
                pool.wait_ge(s["chunk_done"], d)
                pool_high(nc, d_hi[:], d_raw[:], mem.one).then_inc(s["down_hi"], 1)
                pool.wait_ge(s["down_hi"], d + 1)
                nc.gpsimd.tensor_tensor(d_lo[:], d_raw[:], d_hi[:], ALU.subtract).then_inc(s["down_split"], 1)

            turns(pool, split_up, split_down)

        @block.tensor
        def _(pe):
            def up_products(c, j):
                for i in range(2):
                    pe.wait_ge(s[f"up_split{i}"], 2 * c + j + 1)
                    pe.wait_ge(s["b_read" if i else "a_read" if kind == "conv" else "activated"], 2 * c + j)
                    three_pass(nc, acc[i], w_hi[i], w_lo[i], hi, lo, KD).then_inc(s[f"up_done{i}"], 1)

            def down_products(d):
                pe.wait_ge(s["down_split"], d + 1)
                pe.wait_ge(s["g_split"], 2 * d + 2)
                for n in range(KD):
                    b = n % 2
                    pe.wait_ge(s[f"down_read{b}"], 4 * d + n // 2)
                    last = three_pass(nc, dn[b], d_hi, d_lo, g_hi, g_lo, 2, slice(n * P, (n + 1) * P))
                    last.then_inc(s[f"down_done{b}"] if n < KD - 1 else s["chunk_done"], 1)

            turns(pe, up_products, down_products)

        @block.vector
        def _(dve):
            def hidden(c, j):
                f = 2 * c + j
                dve.wait_ge(s["up_done0"], f + 1)
                a = acc[0][:].rearrange("p h t -> p (h t)")
                if kind == "conv":
                    steps = Steps(dve, s["vector_step"], f * 2)
                    dve.wait_ge(s["activated"], f)
                    w = [prm[:, bass.ds(f + (PRM["conv_w"] + FT * i), 1)] for i in range(3)]
                    steps.link(nc.vector.tensor_scalar(conv[:], a, w[2], prm[:, bass.ds(f + PRM["conv_b"], 1)], ALU.mult, ALU.add))
                    steps.link(nc.vector.scalar_tensor_tensor(out=conv[:, 1:S], in0=a[:, 0:S - 1], scalar=w[1], in1=conv[:, 1:S],
                                                              op0=ALU.mult, op1=ALU.add))
                    nc.vector.scalar_tensor_tensor(out=conv[:, 2:S], in0=a[:, 0:S - 2], scalar=w[0], in1=conv[:, 2:S],
                                                   op0=ALU.mult, op1=ALU.add).then_inc(s["a_read"], 1)
                dve.wait_ge(s["activated"], f + 1)
                dve.wait_ge(s["up_done1"], f + 1)
                nc.vector.tensor_tensor(prod[j][:].rearrange("p (h t) -> p h t", h=NH), act_out[:].rearrange("p (h t) -> p h t", h=NH),
                                        acc[1][:], ALU.mult).then_inc(s["b_read"], 1)
                if j == 1:
                    split_low(c, 1)

            def split_low(c, j):
                dve.wait_ge(s["g_hi_done"], 2 * c + j + 1)
                nc.vector.tensor_tensor(g_lo[:, j, :], prod[j][:], g_hi[:, j, :], ALU.subtract).then_inc(s["g_split"], 1)

            def add_down(d):
                for n in range(KD):
                    b = n % 2
                    if n < KD - 1:
                        dve.wait_ge(s[f"down_done{b}"], (4 if b == 0 else 3) * d + n // 2 + 1)
                    else:
                        dve.wait_ge(s["chunk_done"], d + 1)
                    x = xT[:, n, :].rearrange("p (h t) -> p h t", h=NH)
                    if gate is None:
                        nc.vector.tensor_tensor(x, x, dn[b][:], ALU.add).then_inc(s[f"down_read{b}"], 1)
                    else:
                        nc.vector.scalar_tensor_tensor(out=x, in0=dn[b][:], scalar=prm[:, gate + n:gate + n + 1], in1=x,
                                                       op0=ALU.mult, op1=ALU.add).then_inc(s[f"down_read{b}"], 1)

            hidden(0, 0)
            split_low(0, 0)
            hidden(0, 1)
            with dve.Fori(1, C) as c:
                hidden(c, 0)
                add_down(c - 1)
                split_low(c, 0)
                hidden(c, 1)
            add_down(C - 1)

        @block.scalar
        def _(act):
            def hidden(c, j):
                f = 2 * c + j
                act.wait_ge(s["b_read"], f)
                if kind == "conv":
                    act.wait_ge(s["a_read"], f + 1)
                    nc.scalar.activation(act_out[:], conv[:], ACT.Gelu_apprx_tanh).then_inc(s["activated"], 1)
                else:
                    act.wait_ge(s["up_done0"], f + 1)
                    nc.scalar.activation(act_out[:].rearrange("p (h t) -> p h t", h=NH), acc[0][:], ACT.Silu).then_inc(s["activated"], 1)
                act.wait_ge(s["chunk_done"], c)
                act.wait_ge(s["b_read"], f + 1)
                nc.scalar.activation(g_hi[:, j, :], prod[j][:], ACT.Copy).then_inc(s["g_hi_done"], 1)

            for j in range(2):
                hidden(0, j)
            with act.Fori(1, C) as c:
                for j in range(2):
                    hidden(c, j)




def retention(nc, mem, env, projT, ins):
    prm, ident, hi, lo = env["prm"], env["ident"], env["hi"], env["lo"]
    NCH = S // P
    qT = [mem.at(f"ret_q{b}", 104 + 4 * b, [P, S]) for b in range(2)]
    kT = [mem.at(f"ret_k{b}", 112 + 4 * b, [P, S]) for b in range(2)]
    vT = [mem.at(f"ret_v{b}", 120 + 8 * b, [P, 2, S]) for b in range(2)]
    gT = [mem.at(f"ret_g{b}", 136 + 8 * b, [P, 2, S]) for b in range(2)]
    y32 = [mem.at(f"ret_y{b}", 152 + 8 * b, [P, 2, S]) for b in range(2)]
    dmask = mem.at("ret_dmask", 168, [P, RET_H, P])
    xi = mem.at("ret_xi", 170, [P, RET_H, P])
    col = mem.at("ret_col", 172, [P, 2 * RET_H])
    kn = [mem.at(f"ret_kn{q}", 173 + q, [P, P]) for q in range(2)]
    vn = [mem.at(f"ret_vn{q}", 175 + q, [P, RET_DV]) for q in range(2)]
    pT = [mem.at(f"ret_p{q}", 177 + q, [P, P]) for q in range(2)]
    qx = [mem.at(f"ret_qx{q}", 179 + q, [P, P]) for q in range(2)]
    R = [mem.at(f"ret_R{q}", 181 + q, [P, RET_DV]) for q in range(2)]
    on = [mem.at(f"ret_on{q}", 183 + q, [P, RET_DV]) for q in range(2)]
    stats = [mem.at(f"ret_stats{q}", 185 + q, [P, 16]) for q in range(2)]

    zeta = [mem.at(f"ret_zeta{b}", 187 + b * 0.125, [P, 1]) for b in range(2)]
    dec = [mem.at(f"ret_dec{b}", 187.25 + b * 0.125, [P, 1]) for b in range(2)]
    gain = [mem.at(f"ret_gain{b}", 187.5 + b * 0.125, [P, 2]) for b in range(2)]
    dmask_h = [mem.at(f"ret_dmask_h{b}", 188 + b * 0.5, [P, P]) for b in range(2)]
    xi_h = [mem.at(f"ret_xi_h{b}", 189 + b * 0.5, [P, P]) for b in range(2)]

    names = both("head_loaded gates_loaded turned kv_copied scores_masked q_scaled out_done state_done stats_done root_done "
                 "normed y_turned y_gated silu_done head_done high_done") + "consts zeta_done vector_step scalar_step "
    banks = [(f"{n}{q}", [P, HALF], F32) for n in ("turn", "score", "out", "y") for q in range(2)]
    with phase(nc, names, banks) as (block, s, ps):
        turn, score, outp, y = ([ps[f"{n}0"], ps[f"{n}1"]] for n in ("turn", "score", "out", "y"))

        def heads(eng, body):
            with eng.Fori(0, RET_H // 2) as p:
                for b in range(2):
                    body(p, b)

        def use(p, b, n):
            return NCH * p + (NCH // 2) * b + n // 2

        @block.sync
        def _(sp):
            sp.dma_start(dmask[:], ins["k_dmask"].rearrange("h m c -> m h c")).then_inc(s["consts"], 16)
            sp.dma_start(xi[:], ins["k_xi"]).then_inc(s["consts"], 16)
            sp.dma_start(col[:], ins["k_retcol"]).then_inc(s["consts"], 16)

            def load(p, b):
                h = 2 * p + b
                sp.wait_ge(s[f"head_done{b}"], p)
                sp.dma_start(qT[b][:], projT[bass.ds((RQ + h) * P, P), :]).then_inc(s[f"head_loaded{b}"], 16)
                sp.dma_start(kT[b][:], projT[bass.ds((RK + h) * P, P), :]).then_inc(s[f"head_loaded{b}"], 16)
                sp.dma_start(vT[b][:], projT[bass.ds((RV + 2 * h) * P, 2 * P), :].rearrange("(e p) t -> p e t", p=P)).then_inc(s[f"head_loaded{b}"], 16)
                sp.dma_start(gT[b][:], projT[bass.ds((RG + 2 * h) * P, 2 * P), :].rearrange("(e p) t -> p e t", p=P)).then_inc(s[f"gates_loaded{b}"], 16)

            heads(sp, load)

        @block.tensor
        def _(pe):
            def stage_a(p, b, n):
                q, m = n % 2, use(p, b, n)
                if n == 0:
                    pe.wait_ge(s[f"head_loaded{b}"], 48 * p + 48)
                c = slice(n * P, (n + 1) * P)
                pe.wait_ge(s[f"kv_copied{q}"], m)
                pe.wait_ge(s[f"scores_masked{q}"], m)
                nc.tensor.transpose(turn[q][:, 0:P], kT[b][:, c], ident[:])
                for e in range(2):
                    nc.tensor.transpose(turn[q][:, (1 + e) * P:(2 + e) * P], vT[b][:, e, c], ident[:])
                nc.tensor.matmul(score[q][:, 0:P], kT[b][:, c], qT[b][:, c], start=True, stop=True).then_inc(s[f"turned{q}"], 1)

            def stage_b(p, b, n):
                q, m = n % 2, use(p, b, n)
                pe.wait_ge(s[f"kv_copied{q}"], m + 1)
                pe.wait_ge(s[f"scores_masked{q}"], m + 1)
                pe.wait_ge(s[f"q_scaled{q}"], m + 1)
                pe.wait_ge(s[f"normed{q}"], m)
                pe.wait_ge(s[f"state_done{q}"], m)
                nc.tensor.matmul(outp[q][:, 0:RET_DV], pT[q][:], vn[q][:], start=True, stop=(n == 0))
                if n > 0:
                    pe.wait_ge(s[f"state_done{1 - q}"], use(p, b, n - 1) + 1)
                    nc.tensor.matmul(outp[q][:, 0:RET_DV], qx[q][:], R[q][:], start=False, stop=True)
                nc.tensor.matmul(outp[q][:, RET_DV:2 * RET_DV], kn[q][:], vn[q][:], start=True, stop=True).then_inc(s[f"out_done{q}"], 1)

            def stage_d(p, b, n):
                q, m = n % 2, use(p, b, n)
                pe.wait_ge(s[f"normed{q}"], m + 1)
                pe.wait_ge(s[f"y_gated{q}"], m)
                for e in range(2):
                    last = nc.tensor.transpose(y[q][:, e * P:(e + 1) * P], on[q][:, e * P:(e + 1) * P], ident[:])
                last.then_inc(s[f"y_turned{q}"], 1)

            def head(p, b):
                stage_a(p, b, 0)
                for n in range(NCH):
                    if n + 1 < NCH:
                        stage_a(p, b, n + 1)
                    stage_b(p, b, n)
                    if n > 0:
                        stage_d(p, b, n - 1)
                stage_d(p, b, NCH - 1)

            heads(pe, head)

        @block.scalar
        def _(act):
            act.wait_ge(s["consts"], 48)

            def copies(p, b, n):
                q, m = n % 2, use(p, b, n)
                act.wait_ge(s[f"out_done{q}"], m)
                act.wait_ge(s[f"turned{q}"], m + 1)
                nc.scalar.activation(vn[q][:], turn[q][:, P:3 * P], ACT.Copy).then_inc(s["scalar_step"], 1)
                nc.scalar.activation(kn[q][:], turn[q][:, 0:P], ACT.Identity, scale=zeta[b][:]).then_inc(s[f"kv_copied{q}"], 1)

            def root(p, b, n):
                q, m = n % 2, use(p, b, n)
                act.wait_ge(s[f"stats_done{q}"], m + 1)
                nc.scalar.activation(stats[q][:, 10:11], stats[q][:, 9:10], ACT.Sqrt).then_inc(s[f"root_done{q}"], 1)

            def head(p, b):
                act.wait_ge(s[f"gates_loaded{b}"], 16 * p + 16)
                nc.scalar.activation(gT[b][:], gT[b][:], ACT.Silu).then_inc(s[f"silu_done{b}"], 1)
                act.wait_ge(s[f"zeta_done"], 2 * p + b + 1)
                for n in range(NCH):
                    copies(p, b, n)
                    if n > 0:
                        root(p, b, n - 1)
                root(p, b, NCH - 1)

            heads(act, head)

        @block.gpsimd
        def _(pool):
            pool.wait_ge(s["consts"], 48)

            def head(p, b):
                pool.wait_ge(s[f"head_loaded{b}"], 48 * p + 48)
                for n in range(NCH):
                    q, m = n % 2, use(p, b, n)
                    if n == 0:
                        pool.wait_ge(s["zeta_done"], 2 * p + b + 1)
                    pool.wait_ge(s[f"out_done{q}"], m)
                    nc.gpsimd.tensor_tensor(qx[q][:], qT[b][:, n * P:(n + 1) * P], xi_h[b][:], ALU.mult).then_inc(s[f"q_scaled{q}"], 1)

            heads(pool, head)

        @block.vector
        def _(dve):
            dve.wait_ge(s["consts"], 48)

            def masked(p, b, n):
                q, m = n % 2, use(p, b, n)
                dve.wait_ge(s[f"out_done{q}"], m)
                dve.wait_ge(s[f"turned{q}"], m + 1)
                nc.vector.tensor_tensor(pT[q][:], score[q][:, 0:P], dmask_h[b][:], ALU.mult).then_inc(s[f"scores_masked{q}"], 1)

            def state(p, b, n):
                q, m = n % 2, use(p, b, n)
                dve.wait_ge(s[f"out_done{q}"], m + 1)
                addend = outp[q][:, RET_DV:2 * RET_DV]
                st = stats[q]
                steps = Steps(dve, s["vector_step"], (16 * p + 8 * b + n) * 3)
                steps.link(nc.vector.bn_stats(st[:, 0:6], outp[q][:, 0:RET_DV]))
                if n == 0:
                    nc.vector.tensor_copy(R[1][:], addend).then_inc(s[f"state_done{q}"], 1)
                else:
                    dve.wait_ge(s[f"state_done{1 - q}"], use(p, b, n - 1) + 1)
                    nc.vector.scalar_tensor_tensor(out=R[1 - q][:], in0=R[q][:], scalar=dec[b][:], in1=addend,
                                                   op0=ALU.mult, op1=ALU.add).then_inc(s[f"state_done{q}"], 1)
                steps.link(nc.vector.bn_aggr(st[:, 6:8], st[:, 0:6]))
                steps.link(nc.vector.tensor_scalar(st[:, 8:9], st[:, 7:8], EPS, None, ALU.add))
                nc.vector.reciprocal(st[:, 9:10], st[:, 8:9]).then_inc(s[f"stats_done{q}"], 1)

            def normed(p, b, n):
                q, m = n % 2, use(p, b, n)
                dve.wait_ge(s[f"y_turned{q}"], m)
                dve.wait_ge(s[f"root_done{q}"], m + 1)
                st = stats[q]
                nc.vector.tensor_scalar(on[q][:], outp[q][:, 0:RET_DV], st[:, 6:7], st[:, 10:11], ALU.subtract, ALU.mult).then_inc(s[f"normed{q}"], 1)

            def gated(p, b, n):
                q, m = n % 2, use(p, b, n)
                dve.wait_ge(s[f"y_turned{q}"], m + 1)
                c = slice(n * P, (n + 1) * P)
                for e in range(2):
                    last = nc.vector.scalar_tensor_tensor(out=y32[b][:, e, c], in0=y[q][:, e * P:(e + 1) * P],
                                                          scalar=gain[b][:, e:e + 1], in1=gT[b][:, e, c], op0=ALU.mult, op1=ALU.mult)
                last.then_inc(s[f"y_gated{q}"], 1)

            def head(p, b):
                h = 2 * p + b
                nc.vector.tensor_scalar(zeta[b][:], col[:, bass.ds(h, 1)], 1.0, None, ALU.mult)
                nc.vector.tensor_scalar(dec[b][:], col[:, bass.ds(h + RET_H, 1)], 1.0, None, ALU.mult)
                nc.vector.tensor_scalar(gain[b][:], prm[:, bass.ds(2 * h + PRM["ret_gn_g"], 2)], 1.0, None, ALU.mult)
                nc.vector.tensor_scalar(dmask_h[b][:], dmask[:, bass.ds(h, 1), :].rearrange("m h c -> m (h c)"), 1.0, None, ALU.mult)
                nc.vector.tensor_scalar(xi_h[b][:], xi[:, bass.ds(h, 1), :].rearrange("m h c -> m (h c)"), 1.0, None, ALU.mult).then_inc(s["zeta_done"], 1)
                dve.wait_ge(s["zeta_done"], h + 1)
                dve.wait_ge(s[f"silu_done{b}"], p + 1)
                masked(p, b, 0)
                for n in range(NCH):
                    if n + 1 < NCH:
                        masked(p, b, n + 1)
                    state(p, b, n)
                    if n > 0:
                        normed(p, b, n - 1)
                    if n > 1:
                        gated(p, b, n - 2)
                normed(p, b, NCH - 1)
                gated(p, b, NCH - 2)
                gated(p, b, NCH - 1)
                dve.wait_ge(s["y_gated0"], use(p, b, NCH))
                dve.wait_ge(s["y_gated1"], use(p, b, NCH))
                nc.vector.tensor_scalar(hi[:, bass.ds(2 * h, 2), :], y32[b][:], 1.0, None, ALU.mult).then_inc(s[f"high_done{b}"], 1)
                dve.wait_ge(s[f"high_done{b}"], p + 1)
                nc.vector.tensor_tensor(lo[:, bass.ds(2 * h, 2), :], y32[b][:], hi[:, bass.ds(2 * h, 2), :], ALU.subtract).then_inc(s[f"head_done{b}"], 1)

            heads(dve, head)


def nsa_buffers(mem):
    return dict(
        ksT=mem.at("nsa_ksT", 104, [P, NSA_G, S]),
        kwT=mem.at("nsa_kwT", 112, [P, NSA_G, S]),
        vs=mem.at("nsa_vs", 120, [P, NT, P]),
        vw=mem.at("nsa_vw", 124, [P, NT, P]),
        kcT=mem.at("nsa_kcT", 128, [P, NSA_G, NC_PAD]),
        vc=mem.at("nsa_vc", 128.5, [P, NSA_G, NSA_D]),
        gates=mem.at("nsa_gates", 129, [P, NT, N_GATE]),
        slopes=mem.at("nsa_slopes", 130, [P, NSA_H]),
        o=mem.at("nsa_o", 56, [P, NT, NSA_H * NSA_D]),
        dist=mem.at("nsa_dist", 88, [P, 2 * S - P], F32R),
        dwin=mem.at("nsa_dwin", 95.5, [P, WINDOW + P], F32R),
        dcmp=mem.at("nsa_dcmp", 98, [P, NT, NC_PAD], F32R),
        cmask=mem.at("nsa_cmask", 100, [P, NT, NC_PAD]),
    )


def nsa_prepare(nc, mem, env, N, projT, ins):
    prm, ident = env["prm"], env["ident"]
    scale = NSA_D ** -0.5
    w1 = [mem.at(f"cmp_w1{j}", 131 + 32 * j, [P, CMP_LEN, CMP_HID]) for j in range(2)]
    base = 72
    src = [mem.at(f"cmp_src{j}", base + 4 * j, [P, S]) for j in range(2)]
    shifted = [mem.at(f"cmp_shift{i}", 195 + 4 * i, [P, NC_PAD, CMP_STRIDE]) for i in range(2)]
    w2 = mem.at("cmp_w2", 203, [P, 2, 2, NSA_D])
    pos = mem.at("cmp_pos", 204, [CMP_LEN, 2, P])
    posT = mem.at("cmp_posT", 205, [P, 2, CMP_LEN])
    hid = mem.at("cmp_hid", 205.5, [P, 2, NSA_G, NC_PAD])
    kraw = mem.at("nsa_kraw", 40, [P, 2, NSA_G, S])
    tmp = mem.at("nsa_tmp", 80, [P, S])
    names = ("w1a w1b w2_in pos_in src_in kv_in tab_in pos_turned pos_copied shift0 shift1 hidden_done hid_act_done out_done out_copied "
             "vrow_turned vrow_copied gate_done table_done k_done pad_done gate_turned gate_copied vrow_in gate_in vector_step scalar_step")
    banks = [("hid_ps0", [P, 2, NC_PAD], F32), ("hid_ps1", [P, 2, NC_PAD], F32), ("out_ps", [P, 2, NSA_D], F32), ("pos_ps", [P, 2, CMP_LEN], F32),
             ("vrow_ps", [P, 4, P], F32), ("gate_ps", [P, NT, N_GATE], F32)]
    vrow = mem.at("nsa_vrow", 84, [P, S])
    with phase(nc, names, banks) as (block, s, ps):
        @block.sync
        def _(sp):
            for j, name in enumerate(("cmp_w1_k", "cmp_w1_v")):
                v = ins[name].rearrange("a (l d) n -> (a d) l n", d=NSA_D)
                for half in range(2):
                    sp.dma_start(w1[j][half * NSA_D:(half + 1) * NSA_D], v).then_inc(s["w1a" if j == 0 else "w1b"], 16)

        @block.scalar
        def _(act):
            for j, name in enumerate(("cmp_pos_k", "cmp_pos_v")):
                for half in range(2):
                    act.dma_start(pos[:, j, half * NSA_D:(half + 1) * NSA_D], ins[name].rearrange("a l d -> (a l) d")).then_inc(s["pos_in"], 16)
            act.dma_start(src[0][:], projT[KCR * P:(KCR + 1) * P, :]).then_inc(s["src_in"], 16)
            act.dma_start(src[1][:], projT[VCR * P:(VCR + 1) * P, :]).then_inc(s["src_in"], 16)
            for j, name in enumerate(("cmp_w2_k", "cmp_w2_v")):
                act.dma_start(w2[:, j], ins[name].rearrange("a (i p) d -> (a p) i d", p=P)).then_inc(s["w2_in"], 16)
            act.dma_start(tmp[0:N_GATE, :], projT[GATE * P:GATE * P + N_GATE, :]).then_inc(s["gate_in"], 16)
            for j, t in enumerate((KS, KW)):
                for g in range(NSA_G):
                    act.dma_start(kraw[0:NSA_D, j, g, :], projT[t * P + g * NSA_D:t * P + (g + 1) * NSA_D, :]).then_inc(s["kv_in"], 16)
            act.dma_start(N["ksT"][NSA_D:NSA_D + N_BLK], ins["k_onehot"]).then_inc(s["tab_in"], 16)
            act.dma_start(N["slopes"][:], ins["k_slopes"]).then_inc(s["tab_in"], 16)
            act.dma_start(N["cmask"][:], ins["k_cmask"]).then_inc(s["tab_in"], 16)
            act.wait_ge(s["gate_in"], 16)
            nc.scalar.activation(tmp[0:N_GATE, :], tmp[0:N_GATE, :], ACT.Sigmoid).then_inc(s["gate_done"], 1)
            for j in range(2):
                act.wait_ge(s["hidden_done"], j + 1)
                if j == 1:
                    act.wait_ge(s["out_done"], 1)
                bias = PRM["cmp_b1_k" if j == 0 else "cmp_b1_v"]
                act.wait_ge(s["pad_done"], 1)
                for i in range(2):
                    for g in range(NSA_G):
                        last = nc.scalar.activation(hid[:, i, g, 0:N_CMP], ps[f"hid_ps{g}"][:, i, 0:N_CMP], ACT.Gelu_apprx_tanh,
                                                    bias=prm[:, bias + i:bias + i + 1])
                last.then_inc(s["hid_act_done"], 1)
                act.wait_ge(s["out_done"], j + 1)
                if j == 0:
                    nc.scalar.activation(N["kcT"][0:NSA_D], ps["out_ps"][0:NSA_D], ACT.Copy, scale=scale).then_inc(s["out_copied"], 1)
                else:
                    nc.scalar.activation(N["vc"][:], ps["out_ps"][:], ACT.Copy).then_inc(s["out_copied"], 1)

        @block.gpsimd
        def _(pool):
            for j, t in enumerate((VS, VW)):
                if j == 1:
                    pool.wait_ge(s["vrow_turned"], 2)
                pool.dma_start(vrow[:], projT[t * P:(t + 1) * P, :]).then_inc(s["vrow_in"], 16)
            for name, dst in (("k_dist", N["dist"]), ("k_dwin", N["dwin"]), ("k_dcmp", N["dcmp"])):
                pool.dma_start(dst[:], ins[name]).then_inc(s["table_done"], 16)
            pool.wait_ge(s["table_done"], 48)

        @block.tensor
        def _(pe):
            pe.wait_ge(s["pos_in"], 64)
            for j in range(2):
                last = nc.tensor.transpose(ps["pos_ps"][:, j, :], pos[:, j, :], ident[0:CMP_LEN, 0:CMP_LEN])
            last.then_inc(s["pos_turned"], 1)
            pe.wait_ge(s["gate_done"], 1)
            for i in range(NT):
                last = nc.tensor.transpose(ps["gate_ps"][:, i, :], tmp[0:N_GATE, i * P:(i + 1) * P], ident[0:N_GATE, 0:N_GATE])
            last.then_inc(s["gate_turned"], 1)
            for j in range(2):
                pe.wait_ge(s["vrow_in"], 16 * (j + 1))
                for half in range(2):
                    if 2 * j + half > 0:
                        pe.wait_ge(s["vrow_copied"], 2 * j + half)
                    for i in range(4):
                        c = (half * 4 + i) * P
                        last = nc.tensor.transpose(ps["vrow_ps"][:, i, :], vrow[:, c:c + P], ident[:])
                    last.then_inc(s["vrow_turned"], 1)
            for j in range(2):
                pe.wait_ge(s["w1a" if j == 0 else "w1b"], 32)
                pe.wait_ge(s["shift0"], j + 1)
                pe.wait_ge(s["shift1"], j + 1)
                if j == 1:
                    pe.wait_ge(s["hid_act_done"], 1)
                for i in range(2):
                    for l in range(CMP_LEN):
                        half, r = divmod(l, CMP_STRIDE)
                        for g in range(NSA_G):
                            rows = slice(g * NSA_D, (g + 1) * NSA_D)
                            last = nc.tensor.matmul(ps[f"hid_ps{g}"][:, i, 0:N_CMP], w1[j][rows, l, i * P:(i + 1) * P],
                                                    shifted[half][rows, half:half + N_CMP, r], start=(l == 0), stop=(l == CMP_LEN - 1))
                last.then_inc(s["hidden_done"], 1)
                pe.wait_ge(s["hid_act_done"], j + 1)
                pe.wait_ge(s["w2_in"], 32)
                if j == 1:
                    pe.wait_ge(s["out_copied"], 1)
                for g in range(NSA_G):
                    for half in range(1 if j == 0 else 2):
                        for i in range(2):
                            out = ps["out_ps"][half * NSA_D:(half + 1) * NSA_D, g, :]
                            if j == 0:
                                last = nc.tensor.matmul(out, w2[:, 0, i, :], hid[:, i, g, :], start=(i == 0), stop=(i == 1))
                            else:
                                last = nc.tensor.matmul(out, hid[:, i, g, :], w2[:, 1, i, :], start=(i == 0), stop=(i == 1))
                last.then_inc(s["out_done"], 1)

        @block.vector
        def _(dve):
            nc.vector.memset(hid[:, :, :, N_CMP:NC_PAD], 0.0).then_inc(s["pad_done"], 1)
            dve.wait_ge(s["pos_turned"], 1)
            nc.vector.tensor_copy(posT[:], ps["pos_ps"][:]).then_inc(s["pos_copied"], 1)
            dve.wait_ge(s["pos_copied"], 1)
            dve.wait_ge(s["src_in"], 32)

            def shift(j):
                for half in range(2):
                    p = posT[:, j, half * CMP_STRIDE:(half + 1) * CMP_STRIDE].unsqueeze(1).broadcast_to([P, NC_PAD, CMP_STRIDE])
                    nc.vector.tensor_tensor(shifted[half][:], src[j][:].rearrange("p (c r) -> p c r", r=CMP_STRIDE), p, ALU.add)\
                        .then_inc(s[f"shift{half}"], 1)

            shift(0)
            dve.wait_ge(s["gate_turned"], 1)
            nc.vector.tensor_copy(N["gates"][:], ps["gate_ps"][:]).then_inc(s["gate_copied"], 1)
            for n in range(4):
                dve.wait_ge(s["vrow_turned"], n + 1)
                dst = (N["vs"], N["vw"])[n // 2]
                nc.vector.tensor_copy(dst[:, (n % 2) * 4:(n % 2) * 4 + 4, :], ps["vrow_ps"][:]).then_inc(s["vrow_copied"], 1)
            dve.wait_ge(s["kv_in"], 64)
            nc.vector.tensor_scalar(N["ksT"][0:NSA_D], kraw[0:NSA_D, 0], scale, None, ALU.mult)
            nc.vector.tensor_scalar(N["kwT"][0:NSA_D], kraw[0:NSA_D, 1], scale, None, ALU.mult)
            dve.wait_ge(s["tab_in"], 48)
            dve.wait_ge(s["hidden_done"], 1)
            shift(1)


def nsa_compressed(nc, mem, env, N, projT, selT, ins):
    ident = env["ident"]
    qc = [mem.at(f"cmpq{b}", 131 + 4 * b, [NSA_D, NSA_H, P]) for b in range(2)]
    slopeI = mem.at("cmp_slopeI", 139, [P, NSA_H, P], F32R)
    e = [mem.at(f"cmp_e{b}", 143 + 2 * b, [P, NSA_H, NC_PAD]) for b in range(2)]
    pT = [mem.at(f"cmp_pT{b}", 147 + 2 * b, [P, 4, P]) for b in range(2)]
    small = mem.at("cmp_small", 151, [P, 4, NSA_H])
    pg = mem.at("cmp_pg", 152, [P, NSA_G, NC_PAD + 4])
    imp = mem.at("cmp_imp", 153, [P, 4, NSA_G, N_BLK])
    above = mem.at("cmp_above", 154, [P, NSA_G, N_BLK, N_BLK])
    equal = mem.at("cmp_equal", 156, [P, NSA_G, N_BLK, N_BLK])
    before = mem.at("cmp_before", 158, [P, N_BLK, N_BLK])
    keep = mem.at("cmp_keep", 159, [P, NT, N_BLK])
    force = mem.at("cmp_force", 159.5, [P, NT, N_BLK])
    selrow = [mem.at(f"cmp_selrow{b}", 160 + b * 0.5, [NSA_G * N_BLK, P]) for b in range(2)]
    names = both("q_in scores_done exp_in exp_done p_done turned p_copied o_done bias_done bias_turned bias_copied bias_stored") \
        + "o_taken tab_in slope_done vector_step setup"
    banks = [(f"{n}{b}", [P, HALF], F32) for n in ("sc", "pt", "odd") for b in range(2)] + [("bt", [P, 2, P], F32)]
    K = 17
    with phase(nc, names, banks) as (block, s, ps):
        @block.sync
        def _(sp):
            sp.dma_start(before[:], ins["k_before"]).then_inc(s["tab_in"], 16)
            sp.dma_start(keep[:], ins["k_keep"]).then_inc(s["tab_in"], 16)
            sp.dma_start(force[:], ins["k_force"]).then_inc(s["tab_in"], 16)

            def load(p, b):
                sp.wait_ge(s[f"scores_done{b}"], p)
                q = projT[NQ * P:(NQ + 4) * P, bass.ds((2 * p + b) * P, P)].rearrange("(h d) t -> d h t", d=NSA_D)
                sp.dma_start(qc[b][:], q).then_inc(s[f"q_in{b}"], 16)

            pairs(sp, NT, load)

        @block.tensor
        def _(pe):
            pe.wait_ge(s["slope_done"], 1)

            def scores(p, b):
                i = 2 * p + b
                pe.wait_ge(s[f"q_in{b}"], 16 * p + 16)
                pe.wait_ge(s[f"exp_in{b}"], p)
                for h in range(NSA_H):
                    out = ps[f"sc{b}"][:, h * NC_PAD:(h + 1) * NC_PAD]
                    nc.tensor.matmul(out, qc[b][:, h, :], N["kcT"][0:NSA_D, h // 4, :], start=True, stop=False)
                    last = nc.tensor.matmul(out, slopeI[:, h, :], N["dcmp"][:, bass.ds(i, 1), :].rearrange("p i c -> p (i c)"),
                                            start=False, stop=True)
                last.then_inc(s[f"scores_done{b}"], 1)

            def values(p, b):
                pe.wait_ge(s[f"p_done{b}"], p + 1)
                pe.wait_ge(s[f"p_copied{b}"], p)
                for k in range(4):
                    last = nc.tensor.transpose(ps[f"pt{b}"][:, k * P:(k + 1) * P], e[b][:, 2 * k:2 * k + 2, :].rearrange("p h c -> p (h c)"), ident[:])
                last.then_inc(s[f"turned{b}"], 1)
                pe.wait_ge(s[f"p_copied{b}"], p + 1)
                pe.wait_ge(s["o_taken"], 2 * p + b)
                for h in range(NSA_H):
                    rows = slice((h % 2) * NC_PAD, (h % 2 + 1) * NC_PAD)
                    last = nc.tensor.matmul(ps[f"odd{h % 2}"][:, h // 2 * NSA_D:(h // 2 + 1) * NSA_D], pT[b][rows, h // 2, :], N["vc"][rows, h // 4, :],
                                            start=True, stop=True)
                last.then_inc(s[f"o_done{b}"], 1)
                pe.wait_ge(s[f"bias_done{b}"], p + 1)
                for o in range(2):
                    pe.wait_ge(s[f"bias_copied{o}"], p + (b if o == 0 else 0))
                nc.tensor.transpose(ps["bt"][0:NSA_G * N_BLK, b, :], imp[:, 3].rearrange("p g j -> p (g j)"), ident[:]).then_inc(s[f"bias_turned{b}"], 1)

            with pe.Fori(0, NT // 2) as p:
                scores(p, 0)
                scores(p, 1)
                values(p, 0)
                values(p, 1)

        @block.scalar
        def _(act):
            def body(p, b):
                act.wait_ge(s[f"exp_in{b}"], p + 1)
                nc.scalar.activation(e[b][:], e[b][:], ACT.Exp).then_inc(s[f"exp_done{b}"], 1)
                act.wait_ge(s[f"turned{b}"], p + 1)
                act.wait_ge(s[f"o_done{b}"], p)
                nc.scalar.activation(pT[b][:].rearrange("p k t -> p (k t)"), ps[f"pt{b}"][:], ACT.Copy).then_inc(s[f"p_copied{b}"], 1)
                act.wait_ge(s[f"bias_turned{b}"], p + 1)
                act.wait_ge(s[f"bias_stored{b}"], 16 * p)
                nc.scalar.activation(selrow[b][:], ps["bt"][0:NSA_G * N_BLK, b, :], ACT.Copy).then_inc(s[f"bias_copied{b}"], 1)
                act.wait_ge(s[f"bias_copied{b}"], p + 1)
                act.dma_start(selT[:, bass.ds((2 * p + b) * P, P)], selrow[b][:]).then_inc(s[f"bias_stored{b}"], 16)

            pairs(act, NT, body)
            for b in range(2):
                act.wait_ge(s[f"bias_stored{b}"], 16 * (NT // 2))

        @block.vector
        def _(dve):
            dve.wait_ge(s["tab_in"], 48)
            for h in range(NSA_H):
                last = nc.vector.tensor_scalar(slopeI[:, h, :], ident[:], N["slopes"][:, h:h + 1], None, ALU.mult)
            last.then_inc(s["slope_done"], 1)
            nc.vector.memset(pg[:], 0.0).then_inc(s["setup"], 1)
            dve.wait_ge(s["setup"], 1)
            wide = [P, NSA_H, NC_PAD]

            def body(p, b):
                i = 2 * p + b
                steps = Steps(dve, s["vector_step"], i * K)
                sc = ps[f"sc{b}"][:].rearrange("p (h c) -> p h c", c=NC_PAD)
                dve.wait_ge(s[f"scores_done{b}"], p + 1)
                steps.link(nc.vector.tensor_reduce(small[:, 0, :], sc, AX, ALU.max))
                dve.wait_ge(s[f"turned{b}"], p)
                nc.vector.tensor_tensor(e[b][:], sc, small[:, 0, :].unsqueeze(2).broadcast_to(wide), ALU.subtract).then_inc(s[f"exp_in{b}"], 1)
                dve.wait_ge(s[f"exp_done{b}"], p + 1)
                steps.link(nc.vector.tensor_reduce(small[:, 1, :], e[b][:, :, 0:N_CMP], AX, ALU.add))
                steps.link(nc.vector.reciprocal(small[:, 2, :], small[:, 1, :]))
                steps.link(nc.vector.tensor_tensor(e[b][:], e[b][:], small[:, 2, :].unsqueeze(2).broadcast_to(wide), ALU.mult))
                mask = N["cmask"][:, bass.ds(i, 1), :].broadcast_to(wide)
                nc.vector.tensor_tensor(e[b][:], e[b][:], mask, ALU.mult).then_inc(s[f"p_done{b}"], 1)
                dve.wait_ge(s[f"p_done{b}"], p + 1)
                for g in range(NSA_G):
                    steps.do(nc.vector.tensor_reduce(pg[:, g, 4:], e[b][:, 4 * g:4 * g + 4, :].rearrange("p r c -> p c r"), AX, ALU.add))
                steps.wait()
                steps.link(nc.vector.tensor_reduce(imp[:, 0], pg[:, :, 4:].rearrange("p g (j c) -> p g j c", c=4), AX, ALU.add))
                over = pg[:, :, 0:NC_PAD].rearrange("p g (j c) -> p g j c", c=4)[:, :, :, 3]
                steps.link(nc.vector.tensor_tensor(imp[:, 0], imp[:, 0], over, ALU.add))
                per = [P, NSA_G, N_BLK]
                steps.link(nc.vector.tensor_tensor(imp[:, 1], imp[:, 0], keep[:, bass.ds(i, 1), :].broadcast_to(per), ALU.mult))
                steps.link(nc.vector.tensor_tensor(imp[:, 1], imp[:, 1], force[:, bass.ds(i, 1), :].broadcast_to(per), ALU.add))
                for g in range(NSA_G):
                    other = imp[:, 1, g].unsqueeze(1).broadcast_to([P, N_BLK, N_BLK])
                    own = imp[:, 1, g].unsqueeze(2).broadcast_to([P, N_BLK, N_BLK])
                    steps.do(nc.vector.tensor_tensor(above[:, g], other, own, ALU.is_gt))
                    steps.do(nc.vector.tensor_tensor(equal[:, g], other, own, ALU.is_equal))
                steps.wait()
                for g in range(NSA_G):
                    last = nc.vector.tensor_tensor(equal[:, g], equal[:, g], before[:], ALU.mult)
                steps.link(last)
                steps.link(nc.vector.tensor_tensor(above[:], above[:], equal[:], ALU.add))
                steps.link(nc.vector.tensor_reduce(imp[:, 2], above[:], AX, ALU.add))
                for o in range(2):
                    dve.wait_ge(s[f"bias_turned{o}"], p + (b if o == 0 else 0))
                nc.vector.tensor_scalar(imp[:, 3], imp[:, 2], float(SEL_K), NEG, ALU.is_ge, ALU.mult).then_inc(s[f"bias_done{b}"], 1)
                assert steps.n == K, steps.n
                dve.wait_ge(s[f"o_done{b}"], p + 1)
                gates = N["gates"][:, bass.ds(i, 1), 0:NSA_H].rearrange("p i (h o) -> p (i h) o", o=2)
                o = N["o"][:, bass.ds(i, 1), :].rearrange("p i (h o d) -> p (i h) o d", o=2, d=NSA_D)
                for odd in range(2):
                    last = nc.vector.tensor_tensor(o[:, :, odd, :], ps[f"odd{odd}"][:, 0:4 * NSA_D].rearrange("p (h d) -> p h d", d=NSA_D),
                                                   gates[:, :, odd:odd + 1].broadcast_to([P, 4, NSA_D]), ALU.mult)
                last.then_inc(s["o_taken"], 1)

            pairs(dve, NT, body)


def nsa_attend(nc, mem, env, N, projT, selT, ins):
    ident = env["ident"]
    qh = [mem.at(f"att_q{b}", 131 + 4 * b, [P, S]) for b in range(2)]
    slopeI = [mem.at(f"att_slopeI{b}", 139 + 0.5 * b, [P, P], F32R) for b in range(2)]
    prob = [mem.at("att_prob0", 140, [P, S]), mem.at("att_prob1", 144, [P, S])]
    probT = [mem.at("att_probT0", 148, [P, NT, P]), mem.at("att_probT1", 152, [P, NT, P])]
    small = [mem.at(f"att_small{r}", 156 + r, [P, 4]) for r in range(2)]
    names = both("q_in head_scored slope_done scores_done max_done exp_done grouped group_copied o_done o_read") + "vector_step"
    banks = [(f"sc{r}", [P, S], F32) for r in range(2)] + [(f"{n}{r}", [P, HALF], F32) for n in ("pt", "ob") for r in range(2)]
    JOBS = [(i, r) for i in range(NT) for r in range(2)]
    first = lambda i, r: 0 if r == 0 else max(0, i - WINDOW // P)
    tiles = lambda i, r: i + 1 - first(i, r)
    GROUPS, before = [], []
    for j, (i, r) in enumerate(JOBS):
        before.append(len(GROUPS))
        for g in range(-(-tiles(i, r) // 4)):
            GROUPS.append((j, 4 * g, min(4, tiles(i, r) - 4 * g)))
    NG = len(GROUPS)
    assert NG % 2 == 0
    with phase(nc, names, banks) as (block, s, ps):
        def heads(eng, body):
            with eng.Fori(0, NSA_H // 2) as p:
                for b in range(2):
                    body(p, b)

        def use(p, b, j):
            return 2 * NT * p + NT * b + j // 2

        def scored(p, b, j):
            if j == len(JOBS) - 1:
                return s[f"head_scored{b}"], p + 1
            if j % 2:
                return s["scores_done1"], 2 * (NT - 1) * p + (NT - 1) * b + j // 2 + 1
            return s["scores_done0"], use(p, b, j) + 1

        def group_use(p, b, n):
            return NG * p + (NG // 2) * b + n // 2

        @block.sync
        def _(sp):
            def load(p, b):
                h = 2 * p + b
                sp.wait_ge(s[f"head_scored{b}"], p)
                sp.dma_start(qh[b][0:NSA_D], projT[bass.ds(h * NSA_D + NQ * P, NSA_D), :]).then_inc(s[f"q_in{b}"], 16)
                sp.dma_start(qh[b][NSA_D:NSA_D + N_BLK], selT[bass.ds(p // 2 * N_BLK, N_BLK), :]).then_inc(s[f"q_in{b}"], 16)

            heads(sp, load)

        @block.tensor
        def _(pe):
            def scores(p, b, j):
                i, r = JOBS[j]
                m = use(p, b, j)
                if j == 0:
                    pe.wait_ge(s[f"q_in{b}"], 32 * p + 32)
                    pe.wait_ge(s[f"slope_done{b}"], p + 1)
                pe.wait_ge(s[f"exp_done{r}"], m)
                n = tiles(i, r) * P
                rows = NSA_D + N_BLK if r == 0 else NSA_D
                keys = N["ksT"] if r == 0 else N["kwT"]
                table = N["dist"] if r == 0 else N["dwin"]
                off = (NT - 1 - i) * P if r == 0 else WINDOW + P - n
                for c in range(0, n, HALF):
                    w = min(HALF, n - c)
                    out = ps[f"sc{r}"][:, c:c + w]
                    k = keys[0:rows, bass.ds(p // 2, 1), first(i, r) * P + c:first(i, r) * P + c + w].rearrange("p g s -> p (g s)")
                    nc.tensor.matmul(out, slopeI[b][:], table[:, off + c:off + c + w], start=True, stop=False)
                    last = nc.tensor.matmul(out, qh[b][0:rows, i * P:(i + 1) * P], k, start=False, stop=True)
                last.then_inc(scored(p, b, j)[0], 1)

            def turns(p, b, j):
                i, r = JOBS[j]
                pe.wait_ge(s[f"exp_done{r}"], use(p, b, j) + 1)
                for n in range(before[j], NG if j + 1 == len(JOBS) else before[j + 1]):
                    _, t0, nt = GROUPS[n]
                    pe.wait_ge(s[f"group_copied{n % 2}"], group_use(p, b, n))
                    for t in range(nt):
                        last = nc.tensor.transpose(ps[f"pt{n % 2}"][:, t * P:(t + 1) * P], prob[r][:, (t0 + t) * P:(t0 + t + 1) * P], ident[:])
                    last.then_inc(s[f"grouped{n % 2}"], 1)

            def values(p, b, j):
                i, r = JOBS[j]
                for n in range(before[j], NG if j + 1 == len(JOBS) else before[j + 1]):
                    pe.wait_ge(s[f"group_copied{n % 2}"], group_use(p, b, n) + 1)
                pe.wait_ge(s[f"o_read{r}"], use(p, b, j))
                v = N["vs"] if r == 0 else N["vw"]
                for t in range(tiles(i, r)):
                    last = nc.tensor.matmul(ps[f"ob{r}"][:, 0:NSA_D], probT[r][:, t, :], v[:, first(i, r) + t, bass.ds(p // 2 * NSA_D, NSA_D)],
                                            start=(t == 0), stop=(t == tiles(i, r) - 1))
                last.then_inc(s[f"o_done{r}"], 1)

            def head(p, b):
                scores(p, b, 0)
                for j in range(len(JOBS)):
                    if j + 1 < len(JOBS):
                        scores(p, b, j + 1)
                    turns(p, b, j)
                    if j > 0:
                        values(p, b, j - 1)
                values(p, b, len(JOBS) - 1)

            heads(pe, head)

        def copy_group(eng, p, b, n, op):
            j, t0, nt = GROUPS[n]
            i, r = JOBS[j]
            eng.wait_ge(s[f"grouped{n % 2}"], group_use(p, b, n) + 1)
            if j >= 2:
                eng.wait_ge(s[f"o_done{r}"], use(p, b, j))
            dst = probT[r][:, t0:t0 + nt, :].rearrange("p t c -> p (t c)")
            op(dst, ps[f"pt{n % 2}"][:, 0:nt * P]).then_inc(s[f"group_copied{n % 2}"], 1)

        def groups_of(j, parity):
            return [n for n in range(NG) if GROUPS[n][0] == j and n % 2 == parity]

        @block.scalar
        def _(act):
            def exps(p, b, j):
                i, r = JOBS[j]
                act.wait_ge(s[f"max_done{r}"], use(p, b, j) + 1)
                if j >= 2:
                    n = before[j - 1] - 1
                    act.wait_ge(s[f"grouped{n % 2}"], group_use(p, b, n) + 1)
                else:
                    for parity in range(2):
                        act.wait_ge(s[f"grouped{parity}"], group_use(p, b, 0))
                n = tiles(i, r) * P
                nc.scalar.activation(prob[r][:, 0:n], ps[f"sc{r}"][:, 0:n], ACT.Exp, bias=small[r][:, 0:1],
                                     accum_out=small[r][:, 1:2]).then_inc(s[f"exp_done{r}"], 1)

            def head(p, b):
                exps(p, b, 0)
                for j in range(len(JOBS)):
                    if j + 1 < len(JOBS):
                        exps(p, b, j + 1)
                    for n in groups_of(j, 0):
                        copy_group(act, p, b, n, lambda o, x: nc.scalar.activation(o, x, ACT.Copy))

            heads(act, head)

        @block.vector
        def _(dve):
            def maxima(p, b, j):
                i, r = JOBS[j]
                m = use(p, b, j)
                dve.wait_ge(*scored(p, b, j))
                dve.wait_ge(s[f"exp_done{r}"], m)
                nc.vector.tensor_reduce(small[r][:, 0:1], ps[f"sc{r}"][:, 0:tiles(i, r) * P], AX, ALU.max, negate=True).then_inc(s[f"max_done{r}"], 1)

            def weight(p, b, j):
                i, r = JOBS[j]
                m = use(p, b, j)
                steps = Steps(dve, s["vector_step"], (4 * NT * p + 2 * NT * b + j) * 2)
                dve.wait_ge(s[f"exp_done{r}"], m + 1)
                steps.link(nc.vector.reciprocal(small[r][:, 2:3], small[r][:, 1:2]))
                gate = N["gates"][:, i, bass.ds(2 * p + ((1 + r) * NSA_H + b), 1)]
                steps.link(nc.vector.tensor_tensor(small[r][:, 3:4], small[r][:, 2:3], gate, ALU.mult))

            def output(p, b, j):
                i, r = JOBS[j]
                m = use(p, b, j)
                dve.wait_ge(s[f"o_done{r}"], m + 1)
                if r == 1:
                    dve.wait_ge(s["o_read0"], m + 1)
                o = N["o"][:, i, bass.ds((2 * p + b) * NSA_D, NSA_D)]
                nc.vector.scalar_tensor_tensor(out=o, in0=ps[f"ob{r}"][:, 0:NSA_D], scalar=small[r][:, 3:4], in1=o,
                                               op0=ALU.mult, op1=ALU.add).then_inc(s[f"o_read{r}"], 1)

            def head(p, b):
                nc.vector.tensor_scalar(slopeI[b][:], ident[:], N["slopes"][:, bass.ds(2 * p + b, 1)], None, ALU.mult).then_inc(s[f"slope_done{b}"], 1)
                maxima(p, b, 0)
                for j in range(len(JOBS)):
                    if j + 1 < len(JOBS):
                        maxima(p, b, j + 1)
                    for n in groups_of(j, 1):
                        copy_group(dve, p, b, n, lambda o, x: nc.vector.tensor_copy(o, x))
                    if j > 0:
                        output(p, b, j - 1)
                    weight(p, b, j)
                output(p, b, len(JOBS) - 1)

            heads(dve, head)


def turn_split(nc, mem, env, name, src, k_tiles, width):
    ident, hi, lo = env["ident"], env["hi"], env["lo"]
    with phase(nc, both("turned high_done low_done"), [(f"t{b}", [P, k_tiles, P], F32) for b in range(2)]) as (block, s, ps):
        @block.tensor
        def _(pe):
            for i in range(NT):
                b = i % 2
                pe.wait_ge(s[f"low_done{b}"], i // 2)
                for k in range(k_tiles):
                    last = nc.tensor.transpose(ps[f"t{b}"][:, k, :], src[:, i, k * P:(k + 1) * P], ident[:])
                last.then_inc(s[f"turned{b}"], 1)

        @block.scalar
        def _(act):
            for i in range(NT):
                b = i % 2
                act.wait_ge(s[f"turned{b}"], i // 2 + 1)
                nc.scalar.activation(hi[:, 0:k_tiles, i * P:(i + 1) * P], ps[f"t{b}"][:], ACT.Copy).then_inc(s[f"high_done{b}"], 1)

        @block.vector
        def _(dve):
            for i in range(NT):
                b = i % 2
                dve.wait_ge(s[f"high_done{b}"], i // 2 + 1)
                c = slice(i * P, (i + 1) * P)
                nc.vector.tensor_tensor(lo[:, 0:k_tiles, c], ps[f"t{b}"][:], hi[:, 0:k_tiles, c], ALU.subtract).then_inc(s[f"low_done{b}"], 1)


def gated_epilogue(nc, mem, name, gate, store=None, other=None, split=None):
    gbuf = [mem.at(f"{name}_gate{b}", 192 + 4 * b, [P, S]) for b in range(2)]
    if store is None:
        mbuf = [mem.at(f"{name}_other{b}", 200 + 3.5 * b, [P, S]) for b in range(1)] * 2
    st = [mem.at(f"{name}_stage{b}", (128 if store is not None else 92) + 4 * b, [P, S]) for b in range(2)]
    halves = lambda x: x.rearrange("p (h t) -> p h t", h=NH)

    def epilogue(block, s, acc, ps):
        @block.scalar
        def _(act):
            def body(p, b):
                u = 2 * p + b
                act.wait_ge(s[f"acc_read{b}"], p)
                act.dma_start(gbuf[b][:], gate[bass.ds(u * P, P), :]).then_inc(s[f"loaded{b}"], 16)
                act.wait_ge(s[f"loaded{b}"], 16 * p + 16)
                nc.scalar.activation(gbuf[b][:], gbuf[b][:], ACT.Sigmoid).then_inc(s[f"epilogue_a{b}"], 1)
                if store is not None:
                    act.wait_ge(s[f"acc_read{b}"], p + 1)
                    act.dma_start(store[bass.ds(u * P, P), :], st[b][:]).then_inc(s[f"stored{b}"], 16)
                else:
                    act.wait_ge(s["merged"], u)
                    act.dma_start(mbuf[b][:], other[bass.ds(u * P, P), :]).then_inc(s[f"stored{b}"], 16)

            pairs(act, KD, body)
            for b in range(2):
                act.wait_ge(s[f"stored{b}"], 16 * (KD // 2))

        @block.vector
        def _(dve):
            def body(p, b):
                u = 2 * p + b
                dve.wait_ge(s[f"products_done{b}"], p + 1)
                if store is not None:
                    dve.wait_ge(s[f"stored{b}"], 16 * p)
                dve.wait_ge(s[f"epilogue_a{b}"], p + 1)
                nc.vector.tensor_tensor(halves(st[b][:]), acc[b][:], halves(gbuf[b][:]), ALU.mult).then_inc(s[f"acc_read{b}"], 1)
                if store is None:
                    m_hi, m_lo = split
                    tile = lambda x: x[:, bass.ds(u, 1), :].rearrange("p k t -> p (k t)")
                    dve.wait_ge(s[f"acc_read{b}"], p + 1)
                    dve.wait_ge(s[f"stored{b}"], 16 * p + 16)
                    nc.vector.tensor_tensor(st[b][:], st[b][:], mbuf[b][:], ALU.add).then_inc(s["merged"], 1)
                    dve.wait_ge(s["merged"], u + 1)
                    nc.vector.tensor_scalar(tile(m_hi), st[b][:], 1.0, None, ALU.mult).then_inc(s[f"epilogue_b{b}"], 1)
                    dve.wait_ge(s[f"epilogue_b{b}"], p + 1)
                    nc.vector.tensor_tensor(tile(m_lo), st[b][:], tile(m_hi), ALU.subtract).then_inc(s["vector_step"], 1)
                    dve.wait_ge(s["vector_step"], u + 1)

            pairs(dve, KD, body)

    return epilogue


def shift_epilogue(nc, mem, env, name, at, n_units, dst, mu):
    prm = env["prm"]
    st = [mem.at(f"{name}_stage{b}", at + 4 * b, [P, S]) for b in range(2)]
    df = [mem.at(f"{name}_diff{b}", at + 8 + 4 * b, [P, S]) for b in range(2)]

    def epilogue(block, s, acc, ps):
        @block.scalar
        def _(act):
            def body(p, b):
                act.wait_ge(s[f"products_done{b}"], p + 1)
                act.wait_ge(s[f"epilogue_b{b}"], p)
                nc.scalar.activation(st[b][:].rearrange("p (h t) -> p h t", h=NH), acc[b][:], ACT.Copy).then_inc(s[f"acc_read{b}"], 1)
                act.wait_ge(s[f"epilogue_b{b}"], p + 1)
                act.dma_start(dst[bass.ds((2 * p + b) * P, P), :], df[b][:]).then_inc(s[f"stored{b}"], 16)

            pairs(act, n_units, body)
            act.wait_ge(s["stored0"], 16 * ((n_units + 1) // 2))
            act.wait_ge(s["stored1"], 16 * (n_units // 2))

        @block.vector
        def _(dve):
            def body(p, b):
                u = 2 * p + b
                steps = Steps(dve, s["vector_step"], u * 2)
                dve.wait_ge(s[f"stored{b}"], 16 * p)
                dve.wait_ge(s[f"acc_read{b}"], p + 1)
                steps.do(nc.vector.tensor_scalar(df[b][:, 0:1], st[b][:, 0:1], -1.0, None, ALU.mult))
                steps.do(nc.vector.tensor_tensor(df[b][:, 1:S], st[b][:, 0:S - 1], st[b][:, 1:S], ALU.subtract))
                steps.wait()
                nc.vector.scalar_tensor_tensor(out=df[b][:], in0=df[b][:], scalar=prm[:, bass.ds(u + mu, 1)], in1=st[b][:],
                                               op0=ALU.mult, op1=ALU.add).then_inc(s[f"epilogue_b{b}"], 1)

            pairs(dve, n_units, body)

    return epilogue


def modulation(nc, mem, env, ins):
    prm = env["prm"]
    W = 2 * P
    raw = [mem.at(f"ada_raw{b}", 104 + 8 * b, [P, KD, W]) for b in range(2)]
    c_act = mem.at("ada_c", 120, [P, KD])
    w = ins["w_ada_2"].rearrange("a (k p) n -> (a p) k n", p=P)
    n = 6 * D // W
    with phase(nc, both("w_in done read") + "c_done all_done", [(f"ada{b}", [P, 2], F32) for b in range(2)]) as (block, s, ps):
        @block.sync
        def _(sp):
            def load(p, b):
                sp.wait_ge(s[f"done{b}"], p)
                sp.dma_start(raw[b][:], w[:, :, bass.ds((2 * p + b) * W, W)]).then_inc(s[f"w_in{b}"], 16)

            pairs(sp, n, load)

        @block.scalar
        def _(act):
            nc.scalar.activation(c_act[:], prm[:, PRM["c_2"]:PRM["c_2"] + KD], ACT.Silu).then_inc(s["c_done"], 1)

        @block.tensor
        def _(pe):
            pe.wait_ge(s["c_done"], 1)

            def body(p, b):
                pe.wait_ge(s[f"w_in{b}"], 16 * p + 16)
                pe.wait_ge(s[f"read{b}"], p)
                for j in range(2):
                    for k in range(KD):
                        last = nc.tensor.matmul(ps[f"ada{b}"][:, j:j + 1], raw[b][:, k, j * P:(j + 1) * P], c_act[:, k:k + 1],
                                                start=(k == 0), stop=(k == KD - 1))
                last.then_inc(s[f"done{b}"], 1)

            pairs(pe, n, body)

        @block.vector
        def _(dve):
            def body(p, b):
                dve.wait_ge(s[f"done{b}"], p + 1)
                u = 4 * p + 2 * b
                nc.vector.tensor_tensor(prm[:, bass.ds(u + ADA, 2)], ps[f"ada{b}"][:], prm[:, bass.ds(u + PRM["b_ada_2"], 2)], ALU.add)\
                    .then_inc(s[f"read{b}"], 1)

            pairs(dve, n, body)
            for b in range(2):
                dve.wait_ge(s[f"read{b}"], n // 2)
            for group in (1, 4):
                c = prm[:, ADA + group * KD:ADA + (group + 1) * KD]
                nc.vector.tensor_scalar(c, c, 1.0, None, ALU.add)


L = 64
RWKV_TILES = 4
VSTEPS = 135
DECAY = float(np.exp(-0.5))


def rwkv(nc, mem, env, zT, ins):
    prm, ident, hi, lo = env["prm"], env["ident"], env["hi"], env["lo"]
    at = iter(range(104, 208, 4))
    big = lambda name: mem.at(f"rw_{name}", next(at), [P, S])
    r, k, v, lw, cs, a, kk, e1, e2, e3, bb, kb, g, y, rh = map(big, "r k v lw cs a kk e1 e2 e3 bb kb g y rh".split())
    chunk_mask, lora = map(big, "mask lora".split())
    glo = mem.at("rw_glo", 36, [P, S])
    base = next(at)
    nat = [mem.at(f"rw_nat{j}", base + 2 * j, [P, 4, P]) for j in range(2)]
    GT = mem.at("rw_GT", base + 4, [P, 16, P])
    H = mem.at("rw_H", base + 12, [P, 16, L])
    ST = mem.at("rw_ST", base + 16, [P, 16, L])
    X0 = mem.at("rw_X0", base + 20, [P, 4, P])
    XA = mem.at("rw_XA", base + 22, [P, 4, P])
    Q = mem.at("rw_Q", base + 24, [P, 4, P])
    QT = mem.at("rw_QT", base + 26, [P, 4, P])
    Pm = mem.at("rw_P", base + 28, [P, 4, P])
    Mab, Mak, Mrb, Mrk = (mem.at(f"rw_M{n}", 56 + 2 * i, [P, 4, P]) for i, n in enumerate(("ab", "ak", "rb", "rk")))
    masks = mem.at("rw_masks", 64, [P, 8, P])
    w2t = mem.at("rw_w2t", 68, [P, P])
    g2t = mem.at("rw_g2t", 68.5, [P, P])
    blockones = mem.at("rw_blockones", 69, [P, P])
    eye2 = mem.at("rw_eye2", 69.5, [P, L])
    cols = mem.at("rw_cols", 70, [P, 16])
    wend = mem.at("rw_wend", 70.5, [P, 16])
    t1 = mem.at("rw_t1", 88, [P, S])
    t2 = mem.at("rw_t2", 92, [P, S])
    t3 = mem.at("rw_t3", 96, [P, S])
    t4 = mem.at("rw_t4", 100, [P, S])
    LEVELS = (2, 4, 8, 16, 32)

    names = ("setup z_in const_in lora_done glo_done turn_done cols_done cols2 "
             "lora_w_mm lora_w_read lora_a_mm lora_a_read lora_g_mm lora_g_read lw_sig a_sig scanned "
             "kk_sq kk_mm kk_root kk_done exp1 exp2 exp3 exp4 prep vector_step bonus_mm bonus_read rtk "
             "nat_turned nat_copied m_done m1_read m2_read q1_turned q1_copied p_mm p_read qq_mm qq_read "
             "x_mm x_read xa_mm xa_read rn_mm rn_read gh_mm gh_read g_fin h_fin s_mm s_done y_mm y_read "
             "mean_mm mean_read var_sq var_mm var_read var_root out_pre high low act_step")
    banks = [("A", [P, NH, HALF], F32), ("B", [P, NH, HALF], F32), ("C", [P, NH, HALF], F32), ("D", [P, NH, HALF], F32)]
    with phase(nc, names, banks) as (block, s, ps):
        A, B, C, Dd = ps["A"], ps["B"], ps["C"], ps["D"]
        flat2 = lambda x: x[:].rearrange("p h t -> p (h t)")
        two = lambda x: x[:].rearrange("p (h t) -> p h t", h=NH)

        per = dict(z_in=96, lora_w_mm=1, lora_a_mm=1, lora_g_mm=1, lora_w_read=1, lora_a_read=1, lora_g_read=1,
                   scanned=1, kk_sq=1, kk_mm=1, kk_root=1, kk_done=1, exp1=1, exp2=1, exp3=1, exp4=1, prep=1, rtk=1,
                   bonus_mm=1, bonus_read=1, nat_turned=8, nat_copied=8, m_done=8, m1_read=4, m2_read=4, q1_turned=4,
                   q1_copied=4, p_mm=20, p_read=20, qq_mm=20, qq_read=20, x_mm=4, x_read=4, xa_mm=4, xa_read=4, rn_mm=4,
                   rn_read=4, gh_mm=4, gh_read=4, s_mm=16, s_done=16, y_mm=1, y_read=1, mean_mm=1, mean_read=1,
                   var_sq=1, var_mm=1, var_read=1, var_root=1, out_pre=1, high=1, low=1, cols_done=1, cols2=1, turn_done=1)

        def turns(eng, body):
            with eng.Fori(0, RWKV_TILES) as f:
                def wait(name, n):
                    eng.wait_ge(s[name], f * per[name] + n)
                body(f, wait)

        @block.sync
        def _(sp):
            sp.dma_start(lora[:], zT[ZLO * P:(ZLO + 1) * P, :]).then_inc(s["const_in"], 16)
            sp.dma_start(glo[:], zT[ZG * P:(ZG + 1) * P, :]).then_inc(s["const_in"], 16)
            sp.dma_start(chunk_mask[:], ins["k_chunk"]).then_inc(s["const_in"], 16)
            sp.dma_start(masks[:], ins["k_masks"]).then_inc(s["const_in"], 16)
            sp.dma_start(blockones[:], ins["k_blockones"]).then_inc(s["const_in"], 16)
            sp.dma_start(eye2[:], ins["k_eye2"]).then_inc(s["const_in"], 16)

            def body(f, wait):
                sp.wait_ge(s["turn_done"], f)
                for dst, t in ((r, ZR), (k, ZK), (v, ZV)):
                    sp.dma_start(dst[:], zT[bass.ds((f + t) * P, P), :]).then_inc(s["z_in"], 16)
                c = bass.ds(f * P, P)
                sp.dma_start(w2t[0:64, :], ins["rw_w2_2"].rearrange("a k n -> (a k) n")[:, c]).then_inc(s["z_in"], 16)
                sp.dma_start(w2t[64:128, :], ins["rw_a2_2"].rearrange("a k n -> (a k) n")[:, c]).then_inc(s["z_in"], 16)
                sp.dma_start(g2t[:], ins["rw_g2_2"].rearrange("a k n -> (a k) n")[:, c]).then_inc(s["z_in"], 16)

            turns(sp, body)

        @block.scalar
        def _(act):
            act.wait_ge(s["const_in"], 96)
            nc.scalar.activation(lora[0:64, :], lora[0:64, :], ACT.Tanh).then_inc(s["lora_done"], 1)
            nc.scalar.activation(glo[:], glo[:], ACT.Sigmoid).then_inc(s["lora_done"], 1)

            def body(f, wait):
                wait("cols_done", 1)
                wait("lora_w_mm", 1)
                nc.scalar.activation(two(lw), A[:], ACT.Sigmoid, bias=cols[:, 0:1]).then_inc(s["lora_w_read"], 1)
                wait("lora_a_mm", 1)
                nc.scalar.activation(two(a), B[:], ACT.Sigmoid, bias=cols[:, 1:2]).then_inc(s["lora_a_read"], 1)
                wait("lora_g_mm", 1)
                nc.scalar.activation(two(g), C[:], ACT.Copy).then_inc(s["lora_g_read"], 1)
                wait("kk_mm", 1)
                nc.scalar.activation(two(t1), Dd[:], ACT.Sqrt).then_inc(s["kk_root"], 1)
                wait("scanned", 1)
                nc.scalar.activation(e1[:], cs[:], ACT.Exp).then_inc(s["exp1"], 1)
                nc.scalar.activation(e2[:], cs[:], ACT.Exp, scale=-1.0).then_inc(s["exp2"], 1)
                nc.scalar.activation(t2[:], t2[:], ACT.Exp).then_inc(s["exp3"], 1)
                nc.scalar.activation(e3[:], e3[:], ACT.Exp).then_inc(s["exp4"], 1)
                for n in range(4):
                    for j in range(2):
                        q = 2 * n + j
                        wait("nat_turned", q + 1)
                        if n > 0:
                            wait("gh_mm", n)
                        nc.scalar.activation(nat[j][:].rearrange("p i c -> p (i c)"), C[:, j, :], ACT.Copy).then_inc(s["nat_copied"], 1)
                    wait("q1_turned", n + 1)
                    nc.scalar.activation(Q[:].rearrange("p x c -> p (x c)"), C[:, 0, :], ACT.Copy).then_inc(s["q1_copied"], 1)
                    wait("x_mm", n + 1)
                    for x in range(4):
                        j, h = divmod(x, 2)
                        ao, no = (0, L) if h == 0 else (L, 0)
                        nc.scalar.activation(X0[:, x, ao:ao + L], nat[j][:, 0, h * L:(h + 1) * L], ACT.Copy)
                        last = nc.scalar.activation(X0[:, x, no:no + L], Dd[:, 0, x * L:(x + 1) * L], ACT.Copy)
                    last.then_inc(s["x_read"], 1)
                    wait("xa_mm", n + 1)
                    nc.scalar.activation(XA[:].rearrange("p x c -> p (x c)"), Dd[:, 1, :], ACT.Copy).then_inc(s["xa_read"], 1)
                wait("var_mm", 1)
                nc.scalar.activation(two(t1), B[:], ACT.Sqrt, bias=cols[:, 9:10], scale=1.0 / L).then_inc(s["var_root"], 1)

            turns(act, body)

        @block.tensor
        def _(pe):
            pe.wait_ge(s["lora_done"], 2)

            def body(f, wait):
                wait("z_in", 96)
                for t in range(NH):
                    c = slice(t * HALF, (t + 1) * HALF)
                    last = nc.tensor.matmul(A[:, t, :], w2t[0:64, :], lora[0:64, c], start=True, stop=True)
                last.then_inc(s["lora_w_mm"], 1)
                for t in range(NH):
                    c = slice(t * HALF, (t + 1) * HALF)
                    last = nc.tensor.matmul(B[:, t, :], w2t[64:128, :], lora[64:128, c], start=True, stop=True)
                last.then_inc(s["lora_a_mm"], 1)
                for t in range(NH):
                    c = slice(t * HALF, (t + 1) * HALF)
                    last = nc.tensor.matmul(C[:, t, :], g2t[:], glo[:, c], start=True, stop=True)
                last.then_inc(s["lora_g_mm"], 1)
                wait("kk_sq", 1)
                for t in range(NH):
                    c = slice(t * HALF, (t + 1) * HALF)
                    last = nc.tensor.matmul(Dd[:, t, :], blockones[:], t1[:, c], start=True, stop=True)
                last.then_inc(s["kk_mm"], 1)
                wait("rtk", 1)
                wait("lora_w_read", 1)
                for t in range(NH):
                    c = slice(t * HALF, (t + 1) * HALF)
                    last = nc.tensor.matmul(A[:, t, :], blockones[:], t3[:, c], start=True, stop=True)
                last.then_inc(s["bonus_mm"], 1)
                wait("prep", 1)
                wait("lora_g_read", 1)
                wait("lora_a_read", 1)
                wait("kk_root", 1)
                wait("bonus_read", 1)
                for n in range(4):
                    for j in range(2):
                        c = slice((2 * n + j) * P, (2 * n + j + 1) * P)
                        if n > 0 and j == 0:
                            wait("q1_copied", n)
                        for i, x in enumerate((kk, bb, kb, v)):
                            last = nc.tensor.transpose(C[:, j, i * P:(i + 1) * P], x[:, c], ident[:])
                        last.then_inc(s["nat_turned"], 1)
                    if n > 0:
                        wait("gh_read", n)
                        wait("rn_read", n)
                    for m, (left, right) in enumerate(((a, kk), (lw, kk), (a, r), (lw, r))):
                        bank = A if m < 2 else B
                        for j in range(2):
                            c = slice((2 * n + j) * P, (2 * n + j + 1) * P)
                            for h in range(2):
                                rows = slice(h * L, (h + 1) * L)
                                col = ((m % 2) * 2 + j) * P
                                last = nc.tensor.matmul(bank[:, h, col:col + P], left[rows, c], right[rows, c], start=True, stop=True)
                        if m % 2:
                            last.then_inc(s["m_done"], 1)
                    wait("m1_read", n + 1)
                    wait("nat_copied", 2 * n + 2)
                    for x in range(4):
                        last = nc.tensor.transpose(C[:, 0, x * P:(x + 1) * P], QT[:, x, :], ident[:])
                    last.then_inc(s["q1_turned"], 1)
                    wait("q1_copied", n + 1)
                    for i in range(len(LEVELS)):
                        lv = 5 * n + i
                        if lv > 0:
                            wait("qq_read", lv)
                        for x in range(4):
                            last = nc.tensor.matmul(A[:, 0, x * P:(x + 1) * P], Mab[:, x, :], Q[:, x, :], start=True, stop=True)
                        last.then_inc(s["p_mm"], 1)
                        wait("p_read", lv + 1)
                        for x in range(4):
                            if i < len(LEVELS) - 1:
                                nc.tensor.matmul(A[:, 1, x * P:(x + 1) * P], QT[:, x, :], Pm[:, x, :], start=True, stop=True)
                            last = nc.tensor.matmul(C[:, 1, x * P:(x + 1) * P], Pm[:, x, :], QT[:, x, :], start=True, stop=True)
                        last.then_inc(s["qq_mm"], 1)
                    wait("m2_read", n + 1)
                    for x in range(4):
                        j, h = divmod(x, 2)
                        last = nc.tensor.matmul(Dd[:, 0, x * L:(x + 1) * L], Mak[:, x, :], nat[j][:, 3, h * L:(h + 1) * L], start=True, stop=True)
                    last.then_inc(s["x_mm"], 1)
                    wait("x_read", n + 1)
                    wait("qq_read", 5 * n + 5)
                    for x in range(4):
                        last = nc.tensor.matmul(Dd[:, 1, x * P:(x + 1) * P], QT[:, x, :], X0[:, x, :], start=True, stop=True)
                    last.then_inc(s["xa_mm"], 1)
                    wait("xa_read", n + 1)
                    for x in range(4):
                        j, h = divmod(x, 2)
                        no = L if h == 0 else 0
                        c = slice(x * P, (x + 1) * P)
                        nc.tensor.matmul(B[:, 0, c], XA[:, x, :], Mrb[:, x, :], start=True, stop=False, skip_group_check=True)
                        last = nc.tensor.matmul(B[no:no + L, 0, c], nat[j][:, 3, h * L:(h + 1) * L], Mrk[:, x, :], start=False, stop=True,
                                                skip_group_check=True)
                    last.then_inc(s["rn_mm"], 1)
                    for x in range(4):
                        j, h = divmod(x, 2)
                        ao, no = (0, L) if h == 0 else (L, 0)
                        orow = slice(h * L, (h + 1) * L)
                        for q in range(2):
                            rows = slice(q * L, (q + 1) * L)
                            hc = slice(h * L, (h + 1) * L)
                            g_out = A[orow, q, j * L:(j + 1) * L]
                            h_out = A[orow, q, (2 + j) * L:(3 + j) * L]
                            nc.tensor.matmul(g_out, XA[rows, x, ao:ao + L], nat[j][rows, 1, hc], start=True, stop=True)
                            nc.tensor.matmul(h_out, nat[j][rows, 1, hc], XA[rows, x, no:no + L], start=True, stop=False)
                            last = nc.tensor.matmul(h_out, nat[j][rows, 2, hc], nat[j][rows, 3, hc], start=False, stop=True)
                    last.then_inc(s["gh_mm"], 1)
                wait("gh_read", 4)
                wait("rn_read", 4)
                for c in range(16):
                    wait("s_done", c + 1)
                    nc.tensor.matmul(Dd[:, 0, (c % 2) * L:(c % 2 + 1) * L], GT[:, c, :], ST[:, c, :], start=True, stop=True)\
                        .then_inc(s["s_mm"], 1)
                    for h in range(2):
                        rows = slice(h * L, (h + 1) * L)
                        last = nc.tensor.matmul(B[rows, c // 8, (c % 8) * L:(c % 8 + 1) * L], ST[rows, c, :], rh[rows, c * L:(c + 1) * L],
                                                start=True, stop=True)
                last.then_inc(s["y_mm"], 1)
                wait("y_read", 1)
                for t in range(NH):
                    c = slice(t * HALF, (t + 1) * HALF)
                    last = nc.tensor.matmul(A[:, t, :], blockones[:], y[:, c], start=True, stop=True)
                last.then_inc(s["mean_mm"], 1)
                wait("var_sq", 1)
                for t in range(NH):
                    c = slice(t * HALF, (t + 1) * HALF)
                    last = nc.tensor.matmul(B[:, t, :], blockones[:], t2[:, c], start=True, stop=True)
                last.then_inc(s["var_mm"], 1)
                wait("turn_done", 1)

            turns(pe, body)

        @block.vector
        def _(dve):
            dve.wait_ge(s["const_in"], 96)
            nc.vector.memset(GT[:], 0.0).then_inc(s["setup"], 1)
            dve.wait_ge(s["setup"], 1)
            K = VSTEPS

            def body(f, wait):
                st = Steps(dve, s["vector_step"], f * K)
                tt = lambda o, x, yv, op: nc.vector.tensor_tensor(o, x, yv, op)
                ts = lambda o, x, s1, s2, o0, o1=ALU.bypass: nc.vector.tensor_scalar(o, x, s1, s2, o0, o1)
                for i, n in enumerate(("rw_w0_2", "rw_a0_2", "rw_k_k_2", "rw_k_a_2", None, "rw_r_k_2", "rw_lnx_w_2", "rw_lnx_b_2")):
                    if n:
                        st.do(ts(cols[:, i:i + 1], prm[:, bass.ds(f + PRM[n], 1)], 1.0, None, ALU.mult))
                st.do(nc.vector.memset(cols[:, 9:10], 64e-5))
                st.wait()
                ts(cols[:, 4:5], cols[:, 3:4], -1.0, 1.0, ALU.mult, ALU.add).then_inc(s["cols_done"], 1)
                wait("cols_done", 1)
                wait("z_in", 96)
                st.link(ts(kk[:], k[:], cols[:, 2:3], None, ALU.mult))
                tt(t1[:], kk[:], kk[:], ALU.mult).then_inc(s["kk_sq"], 1)
                wait("lora_w_read", 1)
                st.link(ts(lw[:], lw[:], -DECAY, None, ALU.mult))
                st.link(nc.vector.tensor_tensor_scan(cs[:], chunk_mask[:], lw[:], 0.0, ALU.mult, ALU.add))
                st.do(tt(t2[:], cs[:], lw[:], ALU.subtract))
                ch = lambda x: x[:].rearrange("p (c t) -> p c t", t=L)
                tt(ch(e3), ch(cs)[:, :, L - 1:L].broadcast_to([P, S // L, L]), ch(cs), ALU.subtract).then_inc(s["scanned"], 1)
                wait("lora_a_read", 1)
                st.link(ts(t3[:], a[:], cols[:, 3:4], cols[:, 4:5], ALU.mult, ALU.add))
                st.link(tt(k[:], k[:], t3[:], ALU.mult))
                nc.vector.scalar_tensor_tensor(out=t3[:], in0=r[:], scalar=cols[:, 5:6], in1=k[:], op0=ALU.mult, op1=ALU.mult)\
                    .then_inc(s["rtk"], 1)
                wait("kk_root", 1)
                st.link(ts(t1[:], t1[:], 1e-12, None, ALU.max))
                st.link(nc.vector.reciprocal(t1[:], t1[:]))
                st.link(tt(kk[:], kk[:], t1[:], ALU.mult))
                st.link(tt(a[:], kk[:], a[:], ALU.mult))
                wait("exp4", 1)
                st.do(tt(bb[:], a[:], e3[:], ALU.mult))
                st.do(tt(kb[:], k[:], e3[:], ALU.mult))
                st.wait()
                st.do(tt(a[:], a[:], e2[:], ALU.mult))
                st.do(tt(lw[:], k[:], e2[:], ALU.mult))
                st.do(nc.vector.scalar_tensor_tensor(out=kk[:], in0=kk[:], scalar=-1.0, in1=t2[:], op0=ALU.mult, op1=ALU.mult))
                st.do(tt(r[:], r[:], e1[:], ALU.mult))
                nc.vector.tensor_copy(wend[:], ch(e1)[:, :, L - 1]).then_inc(s["prep"], 1)
                wait("bonus_mm", 1)
                tt(two(t4), A[:], two(v), ALU.mult).then_inc(s["bonus_read"], 1)
                for n in range(4):
                    wait("m_done", 2 * n + 1)
                    src = lambda bank, m: bank[:, :, 2 * m * P:(2 * m + 2) * P].rearrange("p h (j t) -> p j h t", t=P)
                    dst = lambda x: x[:].rearrange("p (j h) t -> p j h t", h=2)
                    mk = lambda i: masks[:, i, :].unsqueeze(1).broadcast_to([P, 4, P])
                    for j in range(2):
                        for (o, m, i) in ((Mab, 0, 0), (Mak, 1, 0)):
                            last = tt(dst(o)[:, j], src(A, m)[:, j], masks[:, i, :].unsqueeze(1).broadcast_to([P, 2, P]), ALU.mult)
                            st.do(last)
                    st.wait()
                    st.link(tt(QT[:], Mab[:], mk(2), ALU.mult))
                    tt(QT[:], QT[:], ident[:].unsqueeze(1).broadcast_to([P, 4, P]), ALU.add).then_inc(s["m1_read"], 1)
                    wait("m_done", 2 * n + 2)
                    for j in range(2):
                        for (o, m, i) in ((Mrb, 0, 1), (Mrk, 1, 1)):
                            last = tt(dst(o)[:, j], src(B, m)[:, j], masks[:, i, :].unsqueeze(1).broadcast_to([P, 2, P]), ALU.mult)
                            if (j, m) != (1, 1):
                                st.do(last)
                    last.then_inc(s["m2_read"], 1)
                    for i in range(len(LEVELS)):
                        lv = 5 * n + i
                        wait("p_mm", lv + 1)
                        if i == 0:
                            wait("q1_copied", n + 1)
                        tt(Pm[:], A[:, 0, :].rearrange("p (x t) -> p x t", t=P), mk(3 + i), ALU.mult).then_inc(s["p_read"], 1)
                        wait("qq_mm", lv + 1)
                        if i < len(LEVELS) - 1:
                            st.do(tt(Q[:], Q[:], A[:, 1, :].rearrange("p (x t) -> p x t", t=P), ALU.add))
                        tt(QT[:], QT[:], C[:, 1, :].rearrange("p (x t) -> p x t", t=P), ALU.add).then_inc(s["qq_read"], 1)
                    wait("rn_mm", n + 1)
                    for h in range(2):
                        rows, other = slice(h * L, (h + 1) * L), slice((1 - h) * L, (2 - h) * L)
                        c = slice(2 * n * P, (2 * n + 2) * P)
                        pair = lambda x: x.rearrange("p (j t) -> p j t", t=P)
                        b3 = B[:, 0, :].rearrange("p (j h t) -> p h j t", h=2, t=P)
                        st.do(tt(pair(rh[rows, c]), b3[rows, h], pair(r[rows, c]), ALU.add))
                        last = nc.vector.tensor_copy(pair(y[rows, c]), b3[other, h])
                        if h == 0:
                            st.do(last)
                    last.then_inc(s["rn_read"], 1)
                    wait("gh_mm", n + 1)
                    for j in range(2):
                        for q in range(2):
                            c = 4 * n + 2 * j + q
                            for h in range(2):
                                rows = slice(h * L, (h + 1) * L)
                                st.do(nc.vector.scalar_tensor_tensor(out=GT[rows, c, rows], in0=eye2[rows, :], scalar=wend[rows, c:c + 1],
                                                                     in1=A[rows, q, j * L:(j + 1) * L], op0=ALU.mult, op1=ALU.add))
                            last = nc.vector.tensor_copy(H[:, c, :], A[:, q, (2 + j) * L:(3 + j) * L])
                            if (j, q) != (1, 1):
                                st.do(last)
                    last.then_inc(s["gh_read"], 1)
                wait("gh_read", 4)
                nc.vector.memset(ST[:, 0, :], 0.0).then_inc(s["s_done"], 1)
                for c in range(15):
                    wait("s_mm", c + 1)
                    tt(ST[:, c + 1, :], Dd[:, 0, (c % 2) * L:(c % 2 + 1) * L], H[:, c, :], ALU.add).then_inc(s["s_done"], 1)
                wait("y_mm", 1)
                tt(two(y), two(y), B[:], ALU.add).then_inc(s["y_read"], 1)
                wait("mean_mm", 1)
                st.link(ts(two(t1), A[:], 1.0 / L, None, ALU.mult))
                st.link(tt(y[:], y[:], t1[:], ALU.subtract))
                tt(t2[:], y[:], y[:], ALU.mult).then_inc(s["var_sq"], 1)
                wait("var_root", 1)
                st.link(nc.vector.reciprocal(t1[:], t1[:]))
                st.link(tt(y[:], y[:], t1[:], ALU.mult))
                st.link(ts(y[:], y[:], cols[:, 6:7], cols[:, 7:8], ALU.mult, ALU.add))
                st.link(tt(y[:], y[:], t4[:], ALU.add))
                tt(y[:], y[:], g[:], ALU.mult).then_inc(s["out_pre"], 1)
                wait("out_pre", 1)
                tile = lambda x: x[:, bass.ds(f, 1), :].rearrange("p k t -> p (k t)")
                st.link(ts(tile(hi), y[:], 1.0, None, ALU.mult))
                tt(tile(lo), y[:], tile(hi), ALU.subtract).then_inc(s["turn_done"], 1)
                wait("turn_done", 1)
                assert st.n == VSTEPS, st.n

            turns(dve, body)


S5_G, S5_P, S5_C = 32, 64, 16
GP = S5_G // 2
STEP = 8
NCK = S // STEP


def s5_buffers(mem):
    return dict(
        vin=mem.at("s5_vin", 104, [P, GP, 2, P]),
        wc=mem.at("s5_wc", 120, [P, 2, GP, STEP + 1, S5_C]),
        toep=mem.at("s5_toep", 138, [P, S5_G, P]),
        pw=mem.at("s5_pw", 154, [P, 2, GP, STEP + 1]),
        u8=mem.at("s5_u8", 155.5, [P, S5_G, NCK]),
    )


def s5_setup(nc, mem, env, B5, uperm, ins):
    ident = env["ident"]
    vin, wc, toep, pw, u8 = (B5[n] for n in ("vin", "wc", "toep", "pw", "u8"))
    rows = mem.at("s5_rows", 200, [GP, 3, P])
    dt_row = mem.at("s5_dt_row", 201.5, [GP, 2])
    d_row = mem.at("s5_d_row", 201.75, [S5_G, S5_C])
    crow = mem.at("s5_crow", 202, [P, 2, 4, P])
    ab = mem.at("s5_ab", 175, [P, 32, GP])
    braw = mem.at("s5_b", 177, [P, 2, GP, S5_C])
    bbar = mem.at("s5_bbar", 179, [P, 2, GP, S5_C])
    cT = mem.at("s5_cT", 181, [P, 2, GP, S5_C])
    powr = mem.at("s5_powr", 183, [P, 2, GP, STEP])
    wb = mem.at("s5_wb", 184, [P, 2, GP, STEP, S5_C])
    tmp = mem.at("s5_tmp", 56, [P, GP, STEP + 1, S5_C])
    kall = mem.at("s5_kall", 88, [S5_C, S5_G, STEP, S5_C])
    dsk = mem.at("s5_dsk", 65, [S5_C, S5_G])
    eyed = mem.at("s5_eyed", 66, [S5_C, S5_G, S5_C])
    names = "dt_in dt_row_done turned_in params_in b_in u_in rows_turned rows_copied step trig0 trig1 exp_dt exp_mag wb_done wc_done turned0 turned1 vin_copied0 vin_copied1 c_turned k_mm k_copied k_skip toep_zero banded ramp"
    banks = [("r", [P, 3, GP], F32), ("d", [S5_C, S5_G], F32), ("c", [P, 2, 4, P], F32), ("t0", [P, 4, P], F32), ("t1", [P, 4, P], F32),
             ("k0", [S5_C, 4, P], F32), ("k1", [S5_C, 4, P], F32)]
    dre, dim, dt, x, th, n_, rr, cosv, sinv, mag, pr, pi, den, cre, cim, tA, tB, tC = range(18)
    col = lambda i: ab[:, i, :]
    with phase(nc, names, banks) as (block, s, ps):
        @block.sync
        def _(sp):
            for i, name in enumerate(("s5_a_re_2", "s5_a_im_2")):
                sp.dma_start(rows[:, i, :], ins[name].rearrange("a (g o) p -> (a g) (o p)", o=2)).then_inc(s["params_in"], 16)
            sp.dma_start(dt_row[:], ins["s5_log_dt_2"].rearrange("a (g o) -> (a g) o", o=2)).then_inc(s["dt_in"], 16)
            sp.dma_start(d_row[:], ins["s5_d_2"].rearrange("a g c -> (a g) c")).then_inc(s["params_in"], 16)
            for i, name in enumerate(("s5_c_re_2", "s5_c_im_2")):
                cv = ins[name].rearrange("a (b g) c p -> (a g c) b p", b=4)
                for half in range(2):
                    sp.dma_start(crow[:, i, :, half * S5_P:(half + 1) * S5_P], cv).then_inc(s["params_in"], 16)
            for i, name in enumerate(("s5_b_re_2", "s5_b_im_2")):
                sp.dma_start(braw[:, i], ins[name].rearrange("a (g o) p c -> (a o p) g c", o=2)).then_inc(s["b_in"], 16)
            for j in range(STEP):
                sp.dma_start(u8[j * S5_C:(j + 1) * S5_C], uperm[:, j, :].rearrange("(g c) m -> c g m", c=S5_C)).then_inc(s["u_in"], 16)
            sp.wait_ge(s["k_skip"], 1)
            sp.wait_ge(s["toep_zero"], 1)
            for j in range(STEP):
                sp.dma_start(toep[j * S5_C:(j + 1) * S5_C, :, j * S5_C:].rearrange("p g (i c) -> p g i c", c=S5_C),
                             kall[:, :, 0:STEP - j, :]).then_inc(s["banded"], 16)
            sp.wait_ge(s["banded"], 16 * STEP)
            sp.wait_ge(s["u_in"], 16 * STEP)

        @block.gpsimd
        def _(pool):
            nc.gpsimd.memset(toep[:], 0.0).then_inc(s["toep_zero"], 1)

        @block.scalar
        def _(act):
            act.wait_ge(s["turned_in"], 1)
            nc.scalar.activation(col(dt), col(dt), ACT.Exp).then_inc(s["exp_dt"], 1)
            act.wait_ge(s["ramp"], 1)
            nc.scalar.activation(col(mag), col(x), ACT.Exp).then_inc(s["exp_mag"], 1)
            act.wait_ge(s["ramp"], 2)
            nc.scalar.activation(col(sinv), col(rr), ACT.Sin).then_inc(s["trig0"], 1)
            act.wait_ge(s["ramp"], 3)
            nc.scalar.activation(col(cosv), col(tC), ACT.Sin).then_inc(s["trig1"], 1)
            for gq in range(8):
                b = gq % 2
                act.wait_ge(s[f"turned{b}"], gq // 2 + 1)
                nc.scalar.activation(vin[:, 2 * gq:2 * gq + 2].rearrange("p g r c -> p (g r) c"), ps[f"t{b}"][:], ACT.Copy).then_inc(s[f"vin_copied{b}"], 1)

        @block.tensor
        def _(pe):
            pe.wait_ge(s["params_in"], 16 * 7)
            pe.wait_ge(s["dt_row_done"], 1)
            nc.tensor.transpose(ps["d"][:], d_row[:], ident[0:S5_G, 0:S5_G])
            for i in range(3):
                nc.tensor.transpose(ps["r"][:, i, :], rows[:, i, :], ident[0:GP, 0:GP])
            for i in range(2):
                for e in range(4):
                    last = nc.tensor.transpose(ps["c"][:, i, e, :], crow[:, i, e, :], ident[:])
            last.then_inc(s["rows_turned"], 1)
            pe.wait_ge(s["wb_done"], 1)
            for gq in range(8):
                b = gq % 2
                pe.wait_ge(s[f"vin_copied{b}"], gq // 2)
                for q in range(4):
                    gp, ri = 2 * gq + q // 2, q % 2
                    last = nc.tensor.transpose(ps[f"t{b}"][:, q, :], wb[:, ri, gp].rearrange("p j c -> p (j c)"), ident[:])
                last.then_inc(s[f"turned{b}"], 1)
            pe.wait_ge(s["wc_done"], 1)
            for gq in range(4):
                pe.wait_ge(s["k_copied"], gq)
                for q in range(4):
                    gp = 4 * gq + q
                    for ri in range(2):
                        for o in range(2):
                            rws = slice(o * S5_P, (o + 1) * S5_P)
                            last = nc.tensor.matmul(ps[f"k{o}"][:, q, :], wb[rws, ri, gp, STEP - 1, :],
                                                    wc[rws, ri, gp, 0:STEP, :].rearrange("p m c -> p (m c)"), start=(ri == 0), stop=(ri == 1))
                last.then_inc(s["k_mm"], 1)

        @block.vector
        def _(dve):
            st = Steps(dve, s["step"])
            tt = lambda o, xx, yv, op: st.link(nc.vector.tensor_tensor(o, xx, yv, op))
            ts = lambda o, xx, s1, s2, o0, o1=ALU.bypass: st.link(nc.vector.tensor_scalar(o, xx, s1, s2, o0, o1))
            dve.wait_ge(s["dt_in"], 16)
            nc.vector.tensor_copy(rows[:, 2, :].rearrange("g (o p) -> g o p", o=2), dt_row[:].unsqueeze(2).broadcast_to([GP, 2, S5_P]))\
                .then_inc(s["dt_row_done"], 1)
            dve.wait_ge(s["rows_turned"], 1)
            st.do(nc.vector.tensor_copy(dsk[:], ps["d"][:]))
            nc.vector.tensor_copy(ab[:, dre:dt + 1, :], ps["r"][:]).then_inc(s["turned_in"], 1)
            dve.wait_ge(s["turned_in"], 1)
            for ri in range(2):
                for o in range(2):
                    half = slice(o * S5_P, (o + 1) * S5_P)
                    src = ps["c"][half, ri].rearrange("p e (g o c) -> p (e g) o c", o=2, c=S5_C)[:, :, o]
                    st.do(nc.vector.tensor_copy(cT[half, ri], src))
            st.wait()
            dve.wait_ge(s["exp_dt"], 1)
            tt(col(th), col(dt), col(dim), ALU.mult)
            nc.vector.tensor_tensor(col(x), col(dt), col(dre), ALU.mult).then_inc(s["ramp"], 1)
            ROUND = 12582912.0
            ts(col(n_), col(th), float(0.5 / np.pi), ROUND, ALU.mult, ALU.add)
            ts(col(n_), col(n_), ROUND, None, ALU.subtract)
            c1 = 6.28125
            c2 = float(np.float32(2 * np.pi - c1))
            c3 = float(2 * np.pi - c1 - c2)
            stt = lambda o, i0, sc, i1: st.link(nc.vector.scalar_tensor_tensor(out=o, in0=i0, scalar=sc, in1=i1, op0=ALU.mult, op1=ALU.add))
            stt(col(rr), col(n_), -c1, col(th))
            stt(col(rr), col(n_), -c2, col(rr))
            stt(col(rr), col(n_), -c3, col(rr))
            nc.vector.tensor_scalar(col(rr), col(rr), 3.1415925, -3.1415925, ALU.min, ALU.max).then_inc(s["ramp"], 1)
            dve.wait_ge(s["ramp"], 2)
            ts(col(tB), col(rr), -1.0, None, ALU.mult)
            tt(col(tC), col(rr), col(tB), ALU.max)
            nc.vector.tensor_scalar(col(tC), col(tC), -1.0, float(np.pi / 2), ALU.mult, ALU.add).then_inc(s["ramp"], 1)
            dve.wait_ge(s["trig1"], 1)
            dve.wait_ge(s["trig0"], 1)
            dve.wait_ge(s["exp_mag"], 1)
            P0 = lambda ri, m: pw[:, ri, :, m]
            st.do(nc.vector.memset(pw[:, 0, :, 0], 1.0))
            st.do(nc.vector.memset(pw[:, 1, :, 0], 0.0))
            tt(P0(0, 1), col(mag), col(cosv), ALU.mult)
            tt(P0(1, 1), col(mag), col(sinv), ALU.mult)
            ts(col(pr), P0(0, 1), -1.0, None, ALU.add)
            tt(col(tA), col(dre), col(dre), ALU.mult)
            tt(col(tB), col(dim), col(dim), ALU.mult)
            tt(col(den), col(tA), col(tB), ALU.add)
            st.link(nc.vector.reciprocal(col(den), col(den)))
            tt(col(tA), col(pr), col(dre), ALU.mult)
            tt(col(tB), P0(1, 1), col(dim), ALU.mult)
            tt(col(cre), col(tA), col(tB), ALU.add)
            tt(col(cre), col(cre), col(den), ALU.mult)
            tt(col(tA), P0(1, 1), col(dre), ALU.mult)
            tt(col(tB), col(pr), col(dim), ALU.mult)
            tt(col(cim), col(tA), col(tB), ALU.subtract)
            tt(col(cim), col(cim), col(den), ALU.mult)
            dve.wait_ge(s["b_in"], 32)

            def complex_product(o_re, o_im, xr, xi, yr, yi, t, minus_im=False, done=None):
                tt(o_re, xr, yr, ALU.mult)
                tt(t, xi, yi, ALU.mult)
                tt(o_re, o_re, t, ALU.subtract)
                tt(o_im, xr, yi, ALU.mult)
                tt(t, xi, yr, ALU.mult)
                if minus_im:
                    last = nc.vector.scalar_tensor_tensor(out=o_im, in0=o_im, scalar=-1.0, in1=t, op0=ALU.mult, op1=ALU.subtract)
                else:
                    last = nc.vector.tensor_tensor(o_im, o_im, t, ALU.add)
                if done:
                    last.then_inc(s[done], 1)
                else:
                    st.link(last)

            wide = lambda v: v.unsqueeze(2).broadcast_to([P, GP, S5_C])
            complex_product(bbar[:, 0], bbar[:, 1], wide(col(cre)), wide(col(cim)), braw[:, 0], braw[:, 1], tmp[:, :, 0, :])
            for m in range(2, STEP + 1):
                complex_product(P0(0, m), P0(1, m), P0(0, 1), P0(1, 1), P0(0, m - 1), P0(1, m - 1), col(tC))
            for j in range(STEP):
                st.do(nc.vector.tensor_copy(powr[:, :, :, j], pw[:, :, :, STEP - 1 - j]))
            st.wait()
            full = [P, GP, STEP, S5_C]
            pf = lambda ri: powr[:, ri].unsqueeze(3).broadcast_to(full)
            bf = lambda ri: bbar[:, ri].unsqueeze(2).broadcast_to(full)
            complex_product(wb[:, 0], wb[:, 1], pf(0), pf(1), bf(0), bf(1), tmp[:, :, 0:STEP, :], done="wb_done")
            full9 = [P, GP, STEP + 1, S5_C]
            pf9 = lambda ri: pw[:, ri].unsqueeze(3).broadcast_to(full9)
            cf9 = lambda ri: cT[:, ri].unsqueeze(2).broadcast_to(full9)
            complex_product(wc[:, 0], wc[:, 1], pf9(0), pf9(1), cf9(0), cf9(1), tmp[:], minus_im=True, done="wc_done")
            st.link(nc.vector.tensor_tensor(eyed[:], ident[0:S5_C, 0:S5_C].unsqueeze(1).broadcast_to([S5_C, S5_G, S5_C]),
                                            dsk[:].unsqueeze(2).broadcast_to([S5_C, S5_G, S5_C]), ALU.mult))
            for gq in range(4):
                dve.wait_ge(s["k_mm"], gq + 1)
                for o in range(2):
                    dst = kall[:, 8 * gq:8 * gq + 8].rearrange("p (g o) m c -> p o g (m c)", o=2)[:, o]
                    last = nc.vector.tensor_copy(dst, ps[f"k{o}"][:])
                last.then_inc(s["k_copied"], 1)
            dve.wait_ge(s["k_copied"], 4)
            nc.vector.tensor_tensor(kall[:, :, 0, :], kall[:, :, 0, :], eyed[:], ALU.add).then_inc(s["k_skip"], 1)


def s5_run(nc, mem, env, B5, yperm):
    vin, wc, toep, pw, u8 = (B5[n] for n in ("vin", "wc", "toep", "pw", "u8"))
    z = mem.at("s5_z", 172, [P, 2, GP, NCK])
    sp_ = mem.at("s5_s", 56, [P, NCK, 2, GP])
    sT = mem.at("s5_sT", 188, [P, 2, GP, NCK])
    trans = mem.at("s5_trans", 88, [P, 2, 2, GP])
    t = [mem.at(f"s5_tmp{i}", 89 + i * 0.5, [P, 2, GP]) for i in range(3)]
    y8 = mem.at("s5_y8", 92, [P, 2, 4, NCK])
    names = "z_mm0 z_mm1 z_read0 z_read1 step scanned turned " + both("y_mm y_read y_stored")
    banks = [("z0", [P, 4, P], F32), ("z1", [P, 4, P], F32), ("y0", [P, 4, P], F32), ("y1", [P, 4, P], F32)]
    with phase(nc, names, banks) as (block, s, ps):
        @block.tensor
        def _(pe):
            for gp in range(GP):
                b = gp // 2 % 2
                if gp % 2 == 0:
                    pe.wait_ge(s[f"z_read{b}"], gp // 4)
                for ri in range(2):
                    for o in range(2):
                        last = nc.tensor.matmul(ps[f"z{b}"][o * S5_P:(o + 1) * S5_P, (gp % 2) * 2 + ri, :],
                                                vin[:, gp, ri, o * S5_P:(o + 1) * S5_P], u8[:, 2 * gp + o, :], start=True, stop=True)
                if gp % 2:
                    last.then_inc(s[f"z_mm{b}"], 1)
            pe.wait_ge(s["turned"], 1)
            for h in range(GP // 4):
                for o in range(2):
                    rws = slice(o * S5_P, (o + 1) * S5_P)
                    pe.wait_ge(s[f"y_read{o}"], h)
                    for q in range(4):
                        gp = 4 * h + q
                        out = ps[f"y{o}"][:, q, :]
                        nc.tensor.matmul(out, toep[:, 2 * gp + o, :], u8[:, 2 * gp + o, :], start=True, stop=False)
                        for ri in range(2):
                            last = nc.tensor.matmul(out, wc[rws, ri, gp, 1:STEP + 1, :].rearrange("p m c -> p (m c)"),
                                                    sT[rws, ri, gp, :], start=False, stop=(ri == 1))
                    last.then_inc(s[f"y_mm{o}"], 1)

        @block.scalar
        def _(act):
            rows = yperm.rearrange("(g o c) j m -> o j c g m", o=2, c=S5_C)
            for h in range(GP // 4):
                for o in range(2):
                    act.wait_ge(s[f"y_mm{o}"], h + 1)
                    if h > 0:
                        act.wait_ge(s[f"y_stored{o}"], 16 * STEP * h)
                    nc.scalar.activation(y8[:, o], ps[f"y{o}"][:], ACT.Copy).then_inc(s[f"y_read{o}"], 1)
                    act.wait_ge(s[f"y_read{o}"], h + 1)
                    for i in range(STEP):
                        act.dma_start(rows[o, i, :, 4 * h:4 * h + 4], y8[i * S5_C:(i + 1) * S5_C, o]).then_inc(s[f"y_stored{o}"], 16)
            for b in range(2):
                act.wait_ge(s[f"y_stored{b}"], 16 * STEP * 4)

        @block.vector
        def _(dve):
            st = Steps(dve, s["step"])
            for ri in range(2):
                st.do(nc.vector.tensor_copy(trans[:, 0, ri, :], pw[:, 0, :, STEP]))
            st.do(nc.vector.tensor_scalar(trans[:, 1, 0, :], pw[:, 1, :, STEP], -1.0, None, ALU.mult))
            st.do(nc.vector.tensor_copy(trans[:, 1, 1, :], pw[:, 1, :, STEP]))
            st.do(nc.vector.memset(sp_[:, 0], 0.0))
            for gh in range(8):
                b = gh % 2
                dve.wait_ge(s[f"z_mm{b}"], gh // 2 + 1)
                dst = z[:, :, 2 * gh:2 * gh + 2, :].rearrange("p r g m -> p g r m")
                src = ps[f"z{b}"][:].rearrange("p (g r) m -> p g r m", r=2)
                nc.vector.tensor_copy(dst[:, 0], src[:, 0])
                nc.vector.tensor_copy(dst[:, 1], src[:, 1]).then_inc(s[f"z_read{b}"], 1)
            dve.wait_ge(s["z_read0"], 4)
            dve.wait_ge(s["z_read1"], 4)
            st.wait()
            n0 = st.n

            with dve.Fori(0, NCK - 1) as m:
                steps = Steps(dve, s["step"], m * 5 + n0)
                now = sp_[:, bass.ds(m, 1)].rearrange("p m r g -> p (m r) g")
                new = sp_[:, bass.ds(m + 1, 1)].rearrange("p m r g -> p (m r) g")
                steps.do(nc.vector.tensor_tensor(t[0][:], now, trans[:, 0], ALU.mult))
                for ri in range(2):
                    steps.do(nc.vector.tensor_tensor(t[1][:, ri], now[:, 1 - ri], trans[:, 1, ri], ALU.mult))
                zz = z[:, :, :, bass.ds(m, 1)].rearrange("p r g m -> p r (g m)")
                steps.wait()
                steps.link(nc.vector.tensor_tensor(t[2][:], t[0][:], t[1][:], ALU.add))
                steps.link(nc.vector.tensor_tensor(new, t[2][:], zz, ALU.add))
            dve.wait_ge(s["step"], 5 * (NCK - 1) + n0)
            nc.vector.tensor_copy(sT[:].rearrange("p r g m -> p m r g")[:, :, 0], sp_[:, :, 0]) 
            nc.vector.tensor_copy(sT[:].rearrange("p r g m -> p m r g")[:, :, 1], sp_[:, :, 1]).then_inc(s["turned"], 1)


def s5_gate(nc, mem, env, yperm, ins, cat):
    prm, ones = env["prm"], env["ones"]
    zz = mem.at("glu_zz", 136, [P, 4, S])
    z_hi = mem.at("glu_zhi", 152, [P, 4, S], F32R)
    z_lo = mem.at("glu_zlo", 168, [P, 4, S], F32R)
    yin = [mem.at(f"glu_in{b}", 184 + 4 * b, [P, STEP, NCK]) for b in range(2)]
    hi, lo = cat
    with phase(nc, both("y_in done") + "gelu_done high_done low_done", []) as (block, s, ps):
        @block.sync
        def _(sp):
            for k in range(4):
                b = k % 2
                if k >= 2:
                    sp.wait_ge(s["gelu_done"], k - 1)
                sp.dma_start(yin[b][:], yperm[k * P:(k + 1) * P]).then_inc(s[f"y_in{b}"], 16)

        @block.scalar
        def _(act):
            for k in range(4):
                b = k % 2
                act.wait_ge(s[f"y_in{b}"], 16 * (k // 2 + 1))
                nc.scalar.activation(zz[:, k, :].rearrange("p (m j) -> p m j", j=STEP), yin[b][:].rearrange("p j m -> p m j"),
                                     ACT.Gelu_apprx_tanh).then_inc(s["gelu_done"], 1)
                act.wait_ge(s["gelu_done"], k + 1)
                nc.scalar.activation(z_hi[:, k, :], zz[:, k, :], ACT.Copy).then_inc(s["high_done"], 1)

        @block.vector
        def _(dve):
            for k in range(4):
                dve.wait_ge(s["high_done"], k + 1)
                nc.vector.tensor_tensor(z_lo[:, k, :], zz[:, k, :], z_hi[:, k, :], ALU.subtract)

    gout = [mem.at(f"glu_sig{b}", 184 + 4 * b, [P, S]) for b in range(2)]

    def epilogue(block, s, acc, ps):
        @block.scalar
        def _(act):
            for u in range(4):
                p, b = divmod(u, 2)
                act.wait_ge(s[f"products_done{b}"], p + 1)
                act.wait_ge(s[f"epilogue_b{b}"], p)
                c = PRM["s5_b_glu_2"] + u
                nc.scalar.activation(gout[b][:].rearrange("p (h t) -> p h t", h=NH), acc[b][:], ACT.Sigmoid, bias=prm[:, c:c + 1])\
                    .then_inc(s[f"acc_read{b}"], 1)

        @block.vector
        def _(dve):
            for u in range(4):
                p, b = divmod(u, 2)
                dve.wait_ge(s[f"acc_read{b}"], p + 1)
                nc.vector.tensor_tensor(zz[:, u, :], zz[:, u, :], gout[b][:], ALU.mult).then_inc(s[f"epilogue_b{b}"], 1)

    gemm(nc, mem, "glu", 4, 4, columns(ins["s5_w_glu_2"], 4), (z_hi, z_lo), epilogue, 104)

    sq = mem.at("glu_sq", 152, [P, S])
    sums = mem.at("glu_sums", 156, [P, S])
    rs = mem.at("glu_rs", 160, [P, S])
    with phase(nc, "step summed total inverse root scaled high", [("tot", [P, NH, HALF], F32)]) as (block, s, ps):
        @block.vector
        def _(dve):
            st = Steps(dve, s["step"])
            st.link(nc.vector.tensor_tensor(sums[:], zz[:, 0, :], zz[:, 0, :], ALU.mult))
            for k in range(1, 4):
                st.link(nc.vector.tensor_tensor(sq[:], zz[:, k, :], zz[:, k, :], ALU.mult))
                last = nc.vector.tensor_tensor(sums[:], sums[:], sq[:], ALU.add)
                if k < 3:
                    st.link(last)
            last.then_inc(s["summed"], 1)
            dve.wait_ge(s["total"], 1)
            st.link(nc.vector.tensor_scalar(rs[:], ps["tot"][:].rearrange("p h t -> p (h t)"), 1.0 / 512, EPS, ALU.mult, ALU.add))
            nc.vector.reciprocal(rs[:], rs[:]).then_inc(s["inverse"], 1)
            dve.wait_ge(s["root"], 1)
            for k in range(4):
                c = PRM["s5_gain_2"] + k
                nc.vector.scalar_tensor_tensor(out=zz[:, k, :], in0=zz[:, k, :], scalar=prm[:, c:c + 1], in1=rs[:],
                                               op0=ALU.mult, op1=ALU.mult).then_inc(s["scaled"], 1)
                dve.wait_ge(s["high"], k + 1)
                nc.vector.tensor_tensor(lo[:, 4 + k, :], zz[:, k, :], hi[:, 4 + k, :], ALU.subtract)

        @block.tensor
        def _(pe):
            pe.wait_ge(s["summed"], 1)
            for h in range(NH):
                last = nc.tensor.matmul(ps["tot"][:, h, :], ones[:], sums[:, h * HALF:(h + 1) * HALF], start=True, stop=True)
            last.then_inc(s["total"], 1)

        @block.scalar
        def _(act):
            act.wait_ge(s["inverse"], 1)
            nc.scalar.activation(rs[:], rs[:], ACT.Sqrt).then_inc(s["root"], 1)
            for k in range(4):
                act.wait_ge(s["scaled"], k + 1)
                nc.scalar.activation(hi[:, 4 + k, :], zz[:, k, :], ACT.Copy).then_inc(s["high"], 1)


def s5(nc, mem, env, uperm, yperm, ins, cat):
    B5 = s5_buffers(mem)
    s5_setup(nc, mem, env, B5, uperm, ins)
    s5_run(nc, mem, env, B5, yperm)
    s5_gate(nc, mem, env, yperm, ins, cat)


def constants():
    f = np.float32
    c = {"k_ident": np.eye(P, dtype=f)}
    h = np.arange(RET_H, dtype=f)
    lg = np.log1p(-np.exp2(-5.0 - h)).astype(f)
    pos = np.arange(P, dtype=f)
    diff = pos[None, :] - pos[:, None]
    scale = f(RET_DK) ** f(-0.5)
    dm = np.where(diff >= 0, np.exp(lg[:, None, None] * np.maximum(diff, 0.0)), 0.0)
    c["k_dmask"] = (dm * scale).astype(f)
    xi = np.exp(lg[:, None] * (pos + 1.0)).astype(f)
    c["k_xi"] = np.broadcast_to(xi[None], (P, RET_H, P)).copy()
    zeta = np.exp(lg[:, None] * (P - 1 - pos)) * scale
    dec = np.broadcast_to(np.exp(lg * P)[:, None], (RET_H, P))
    c["k_retcol"] = np.concatenate([zeta, dec]).T.astype(f).copy()
    t = np.arange(S)
    onehot = (t[None, :] // 64 == np.arange(N_BLK)[:, None]).astype(f)
    c["k_onehot"] = np.stack([onehot] * NSA_G, 1)
    c["k_slopes"] = np.broadcast_to(np.exp2(-(np.arange(NSA_H, dtype=f) + 1)), (P, NSA_H)).astype(f).copy()
    q = np.arange(P)[:, None]
    d = q + (S - P) - np.arange(2 * S - P)[None, :]
    c["k_dist"] = np.where(d >= 0, -d, NEG).astype(f)
    d = q + WINDOW - np.arange(WINDOW + P)[None, :]
    c["k_dwin"] = np.where((d >= 0) & (d < WINDOW), -d, NEG).astype(f)
    tok = (np.arange(NT)[None, :] * P + q)[:, :, None]
    blk = np.arange(NC_PAD)[None, None, :]
    d = tok - (blk * CMP_STRIDE + CMP_LEN - 1)
    ok = (d >= 0) & (blk < N_CMP)
    c["k_dcmp"] = np.where(ok, -d, NEG).astype(f)
    c["k_cmask"] = ok.astype(f)
    j = np.arange(N_BLK)
    c["k_before"] = np.broadcast_to((j[None, :] < j[:, None]).astype(f), (P, N_BLK, N_BLK)).copy()
    cur, jj = tok // 64, j[None, None, :]
    always = (jj == 0) | (jj == cur) | (jj == cur - 1)
    c["k_keep"] = (~always & (jj <= cur)).astype(f)
    c["k_force"] = np.where(jj > cur, -FORCE, np.where(always, FORCE, 0.0)).astype(f)
    return c


def rwkv_constants():
    f = np.float32
    c = {}
    c["k_chunk"] = np.broadcast_to((np.arange(S) % 64 != 0).astype(f), (P, S)).copy()
    i, t = np.arange(P)[:, None], np.arange(P)[None, :]
    same = i // 64 == t // 64
    m = [same & (i < t), same & (i <= t), same & (i // 2 == t // 2) & (i < t)]
    for sz in (2, 4, 8, 16, 32):
        m.append((i // (2 * sz) == t // (2 * sz)) & (i % (2 * sz) >= sz) & (t % (2 * sz) < sz))
    c["k_masks"] = np.stack(m, 1).astype(f)
    c["k_blockones"] = same.astype(f)
    c["k_eye2"] = np.tile(np.eye(64, dtype=f), (2, 1))
    return c


def build(nc, ins, out):
    mem = Memory(nc)
    env = dict(
        xT=mem.at("xT", 0, [P, KD, S]),
        prm=mem.at("prm", 32, [P, PRM_COLS]),
        ident=mem.at("ident", 34, [P, P]),
        ones=mem.at("ones", 35, [P, P]),
        hi=mem.at("h_hi", 40, [P, KD, S], F32R),
        lo=mem.at("h_lo", 72, [P, KD, S], F32R),
    )
    mem.one = env["ones"][:, 0:1]
    h = (env["hi"], env["lo"])
    scratch = lambda name, shape: nc.dram_tensor(name, shape, F32, kind="Internal").ap()
    projT = scratch("projT", [N_PROJ * P, S])
    proj2T = scratch("proj2T", [N_PROJ2 * P, S])
    yaT = scratch("yaT", [D, S])
    selT = scratch("selT", [NSA_G * N_BLK, S])
    uperm = scratch("uperm", [HALF, STEP, NCK])
    yperm = scratch("yperm", [HALF, STEP, NCK])

    load_parameters(nc, mem, env, ins)
    norm_split(nc, mem, env, "norm_mix", gain=PRM["norm_mix"])
    w_in = ins["w_in"].rearrange("a (k p) n -> (a p) k n", p=P)
    gemm(nc, mem, "proj_a", GATE + 1, KD, lambda u: w_in[:, :, bass.ds(u * P, P)], h,
         store_epilogue(nc, mem, "proj_a", 128, GATE + 1, projT), 104)
    gemm(nc, mem, "proj_b", N_PROJ - GA, KD, lambda u: w_in[:, :, bass.ds(u * P + GATE_COL + N_GATE, P)], h,
         store_epilogue(nc, mem, "proj_b", 128, N_PROJ - GA, projT[GA * P:N_PROJ * P, :]), 104)
    retention(nc, mem, env, projT, ins)
    gemm(nc, mem, "ret_out", KD, KD, columns(ins["w_ret_o"], KD), h,
         gated_epilogue(nc, mem, "ret_out", projT[GA * P:(GA + KD) * P, :], store=yaT), 104)
    N = nsa_buffers(mem)
    nsa_prepare(nc, mem, env, N, projT, ins)
    nsa_compressed(nc, mem, env, N, projT, selT, ins)
    nsa_attend(nc, mem, env, N, projT, selT, ins)
    turn_split(nc, mem, env, "nsa_turn", N["o"], 4, P)
    merged = (mem.at("merged_hi", 128, [P, KD, S], F32R), mem.at("merged_lo", 160, [P, KD, S], F32R))
    gemm(nc, mem, "nsa_out", KD, 4, columns(ins["w_nsa_o"], 4), h,
         gated_epilogue(nc, mem, "nsa_out", projT[GB * P:(GB + KD) * P, :], other=yaT, split=merged), 104, extra="merged ")
    residual_gemm(nc, mem, env, "mix_out", columns(ins["w_out"], KD), merged, KD)
    norm_split(nc, mem, env, "norm_ffn", gain=PRM["norm_ffn"])
    up = ins["w_up"].rearrange("a (k p) n -> (a p) k n", p=P)
    rows = lambda w: (lambda c: w.rearrange("a (c j p) n -> c (a p) j n", p=P, j=2)[bass.ds(c, 1)].rearrange("c p j n -> (c p) j n"))
    feed_forward(nc, mem, env, "ffn", lambda i, f: up[:, :, bass.ds(f * P + i * FT * P, P)], rows(ins["w_down"]), "conv")
    norm_in_place(nc, mem, env, "norm_final", PRM["norm_final"])

    modulation(nc, mem, env, ins)
    norm_split(nc, mem, env, "norm_mix2", scale=ADA + 8, shift=ADA)
    w_in2 = ins["w_in_2"].rearrange("a (k p) n -> (a p) k n", p=P)
    gemm(nc, mem, "proj2_z", UU, KD, lambda u: w_in2[:, :, bass.ds(u * P, P)], h,
         shift_epilogue(nc, mem, env, "proj2_z", 128, UU, proj2T, PRM["mu_shift_2"]), 104)
    gemm(nc, mem, "proj2_u", N_PROJ2 - UU, KD, lambda u: w_in2[:, :, bass.ds((UU + u) * P, P)], h,
         store_epilogue(nc, mem, "proj2_u", 128, N_PROJ2 - UU, uperm.rearrange("r j m -> r (j m)"), STEP), 104)
    rwkv(nc, mem, env, proj2T, ins)
    s5(nc, mem, env, uperm, yperm, ins, h)
    residual_gemm(nc, mem, env, "mix2_out", columns(ins["w_out_2"], KD), h, KD, gate=ADA + 16)
    norm_split(nc, mem, env, "norm_ffn2", scale=ADA + 32, shift=ADA + 24)
    up2 = [ins[n].rearrange("a (k p) n -> (a p) k n", p=P) for n in ("ffn_w_gate_2", "ffn_w_up_2")]
    feed_forward(nc, mem, env, "ffn2", lambda i, f: up2[i][:, :, bass.ds(f * P, P)], rows(ins["ffn_w_down_2"]), "silu", gate=ADA + 40)
    norm_out(nc, mem, env, "final", PRM["final_gain_2"], out)


def kernel(**inputs):
    import concourse.bacc as _bacc
    from concourse.bass_utils import run_bass_kernel_spmd as _run

    nc = _bacc.Bacc("TRN2", target_bir_lowering=False, num_devices=1)
    arrays = {name: np.ascontiguousarray(a) for name, a in inputs.items()}
    arrays.update(constants())
    arrays.update(rwkv_constants())
    args = {name: nc.dram_tensor(name, a.shape, mybir.dt.from_np(a.dtype), kind="ExternalInput").ap() for name, a in arrays.items()}
    out = nc.dram_tensor("out", (1, S, D), F32, kind="ExternalOutput").ap()
    build(nc, args, out)
    r = _run(nc, [arrays], core_ids=[0])
    return r.results[0]["out"]
```

```python
from contextlib import ExitStack, contextmanager

import numpy as np
import concourse.bass as bass
from concourse import mybir

P = 128
F32 = mybir.dt.float32
F32R = mybir.dt.float32r
ACT = mybir.ActivationFunctionType
ALU = mybir.AluOpType
AX = mybir.AxisListType.X

S = 1024
D = 1024
KD = D // P
NT = S // P
HALF = 512
NH = S // HALF
FT = 2816 // P
EPS = 1e-6

RQ, RK, RV, RG, NQ = 0, 4, 8, 16, 24
KCR, VCR, KS, VS, KW, VW, GA, GB, GATE = 28, 29, 30, 31, 32, 33, 34, 42, 50
N_PROJ = 51
GATE_COL = 4352
N_GATE = 24
RET_H, RET_DK, RET_DV = 4, 128, 256
NSA_H, NSA_G, NSA_D = 8, 2, 64
NC_PAD, N_CMP = 64, 63
CMP_LEN, CMP_STRIDE, CMP_HID = 32, 16, 256
N_BLK, SEL_K = 16, 8
WINDOW = 512
NEG = -1e30
FORCE = 1e9

N_PROJ2 = 18
ZR, ZK, ZV, ZLO, ZG, UU = 0, 4, 8, 12, 13, 14

KB = 1024
ARENA = 17 * KB


NORM_AT = 176


class Memory:

    def __init__(self, nc):
        self.nc = nc

    def at(self, name, kib, shape, dtype=F32):
        return self.nc.alloc_sbuf_tensor_at(name, shape, dtype, offset=ARENA + int(kib * KB))


@contextmanager
def phase(nc, names, banks=()):
    with ExitStack() as ctx:
        sems = {n: nc.alloc_semaphore(name=f"{n}_{nc.next_id()}") for n in names.split()}
        psum = {n: ctx.enter_context(nc.psum_tensor(f"{n}_{nc.next_id()}", shape, dt)) for n, shape, dt in banks}
        with nc.Block() as block:
            yield block, sems, psum
        nc.clear_and_free_semaphores(list(sems.values()))
        nc.all_engine_barrier()


class Steps:

    def __init__(self, eng, sem, base=0):
        self.eng, self.sem, self.base, self.n = eng, sem, base, 0

    def do(self, ins):
        self.n += 1
        ins.then_inc(self.sem, 1)
        return ins

    def wait(self):
        self.eng.wait_ge(self.sem, self.base + self.n)

    def link(self, ins):
        self.do(ins)
        self.wait()


def both(names):
    return " ".join(f"{n}{b}" for n in names.split() for b in range(2)) + " "


def repeat(eng, n, body, between=None):
    body(0)
    if between:
        between(eng)
    if n == 2:
        body(1)
    elif n > 2:
        with eng.Fori(1, n) as p:
            body(p)


def pairs(eng, n, body, between=None):
    def both_parities(p):
        for b in range(2):
            body(p, b)

    repeat(eng, n // 2, both_parities, between)
    if n % 2:
        body(n // 2, 0)


def gemm(nc, mem, name, n_units, k_tiles, weight, rhs, epilogue, at, extra="", norm=None, later=None):
    raw = [mem.at(f"{name}_raw{b}", at + 4 * b, [P, KD, P]) for b in range(2)]
    w_hi = [mem.at(f"{name}_whi{b}", at + 8 + 4 * b, [P, KD, P], F32R) for b in range(2)]
    w_lo = [mem.at(f"{name}_wlo{b}", at + 16 + 4 * b, [P, KD, P], F32R) for b in range(2)]
    names = "weight_loaded0 weight_loaded1 hi_done0 hi_done1 split_done0 split_done1 products_done0 products_done1 "
    names += "acc_read0 acc_read1 vector_step scalar_step stored0 stored1 loaded0 loaded1 epilogue_a0 epilogue_a1 epilogue_b0 epilogue_b1 " + extra
    names += RMS_SEMS if norm else ""
    banks = [(n, [P, NH, HALF], F32) for n in ("acc0", "acc1", "tot")[0:3 if norm else 2]]
    hi, lo = rhs
    with phase(nc, names, banks) as (block, s, ps):
        acc = [ps["acc0"], ps["acc1"]]
        if norm:
            norm.programs(block, s, ps["tot"], NORM_AT)

        @block.sync
        def _(sp):
            def load(p, b, shift=0):
                sp.wait_ge(s[f"split_done{b}"], p)
                view = weight(2 * p + b, shift) if later else weight(2 * p + b)
                sp.dma_start(raw[b][:, 0:k_tiles, :], view).then_inc(s[f"weight_loaded{b}"], 16)

            if later is None:
                pairs(sp, n_units, load)
            else:
                start, shift, last_shift = later
                pairs(sp, 2 * start, load)
                with sp.Fori(start, n_units // 2) as p:
                    for b in range(2):
                        load(p, b, shift)
                load(n_units // 2, 0, last_shift)

        @block.gpsimd
        def _(pool):
            def split(p, b):
                pool.wait_ge(s[f"weight_loaded{b}"], 16 * p + 16)
                pool.wait_ge(s[f"products_done{b}"], p)
                pool_high(nc, w_hi[b][:, 0:k_tiles, :], raw[b][:, 0:k_tiles, :], mem.one).then_inc(s[f"hi_done{b}"], 1)
                pool.wait_ge(s[f"hi_done{b}"], p + 1)
                nc.gpsimd.tensor_tensor(w_lo[b][:, 0:k_tiles, :], raw[b][:, 0:k_tiles, :], w_hi[b][:, 0:k_tiles, :],
                                        ALU.subtract).then_inc(s[f"split_done{b}"], 1)

            pairs(pool, n_units, split, norm.pool_part if norm else None)

        @block.tensor
        def _(pe):
            first = [True]

            def products(p, b):
                pe.wait_ge(s[f"split_done{b}"], p + 1)
                pe.wait_ge(s[f"acc_read{b}"], p)
                ready = (lambda k: norm.ready(pe, k)) if norm and first else None
                first.clear()
                three_pass(nc, acc[b], w_hi[b], w_lo[b], hi, lo, k_tiles, ready=ready).then_inc(s[f"products_done{b}"], 1)

            pairs(pe, n_units, products)

        epilogue(block, s, acc, ps)


def pool_high(nc, out, x, one):
    return nc.gpsimd.tensor_tensor(out, x, one.unsqueeze(2).broadcast_to(x.shape), ALU.mult)


def three_pass(nc, acc, w_hi, w_lo, hi, lo, k_tiles, w_cols=slice(0, P), ready=None):
    last = None
    for k in range(k_tiles):
        if ready:
            ready(k)
        for i, (w, x) in enumerate(((w_hi, hi), (w_hi, lo), (w_lo, hi))):
            for t in range(NH):
                last = nc.tensor.matmul(acc[:, t, :], w[:, k, w_cols], x[:, k, t * HALF:(t + 1) * HALF],
                                        start=(k == 0 and i == 0), stop=(k == k_tiles - 1 and i == 2))
    return last


VECTORS = [("norm_mix", 8), ("ret_gn_g", 8), ("cmp_b1_k", 2), ("cmp_b1_v", 2), ("norm_ffn", 8), ("conv_w", 66),
           ("conv_b", 22), ("norm_final", 8), ("mu_shift_2", 14), ("rw_w0_2", 4), ("rw_a0_2", 4), ("rw_k_k_2", 4),
           ("rw_k_a_2", 4), ("rw_r_k_2", 4), ("rw_lnx_w_2", 4), ("rw_lnx_b_2", 4), ("s5_b_glu_2", 4), ("s5_gain_2", 4),
           ("s5_d_2", 4), ("final_gain_2", 8), ("c_2", 8), ("b_ada_2", 48)]
PRM = {}
_row = 0
for _name, _n in VECTORS:
    if _row // P != (_row + _n - 1) // P:
        _row = (_row // P + 1) * P
    PRM[_name] = _row
    _row += _n
ADA = 256
PRM_ROWS = 2
PRM_COLS = ADA + 48 + 80
assert _row <= PRM_ROWS * P


def flat(ap):
    names = "abcdefgh"[:len(ap.shape)]
    return ap.rearrange(f"{' '.join(names)} -> ({' '.join(names)})") if len(ap.shape) > 1 else ap


def load_parameters(nc, mem, env, ins):
    xT, prm, ident = env["xT"], env["prm"], env["ident"]
    xin = [mem.at(f"xin{b}", 104 + 4 * b, [P, D]) for b in range(2)]
    rows = [mem.at(f"prm_rows{r}", 112 + r, [P, P]) for r in range(PRM_ROWS)]
    x = ins["x"].rearrange("a (i p) d -> (a i) p d", p=P)
    used = [0] * PRM_ROWS
    for name, n in VECTORS:
        used[PRM[name] // P] = PRM[name] % P + n
    with phase(nc, "x_loaded0 x_loaded1 rows_loaded const_loaded turned0 turned1 copied0 copied1 rows_turned rows_zero",
               [("turn0", [P, KD, P], F32), ("turn1", [P, KD, P], F32), ("rowsT", [P, PRM_ROWS, P], F32)]) as (block, s, ps):
        turn = [ps["turn0"], ps["turn1"]]

        @block.sync
        def _(sp):
            sp.dma_start(ident[:], ins["k_ident"]).then_inc(s["const_loaded"], 16)
            for i in range(NT):
                b = i % 2
                if i >= 2:
                    sp.wait_ge(s[f"turned{b}"], i // 2)
                sp.dma_start(xin[b][:], x[i]).then_inc(s[f"x_loaded{b}"], 16)

        @block.scalar
        def _(act):
            act.wait_ge(s["rows_zero"], PRM_ROWS)
            for name, n in VECTORS:
                r, at = divmod(PRM[name], P)
                act.dma_start(rows[r][at:at + n, :], flat(ins[name]).rearrange("(r p) -> r p", p=P)).then_inc(s["rows_loaded"], 16)

        @block.tensor
        def _(pe):
            pe.wait_ge(s["const_loaded"], 16)
            for i in range(NT):
                b = i % 2
                pe.wait_ge(s[f"x_loaded{b}"], 16 * (i // 2 + 1))
                if i >= 2:
                    pe.wait_ge(s[f"copied{b}"], i // 2)
                for k in range(KD):
                    last = nc.tensor.transpose(turn[b][:, k, :], xin[b][:, k * P:(k + 1) * P], ident[:])
                last.then_inc(s[f"turned{b}"], 1)
            pe.wait_ge(s["rows_loaded"], 16 * len(VECTORS))
            for r in range(PRM_ROWS):
                last = nc.tensor.transpose(ps["rowsT"][:, r, :], rows[r][:], ident[:])
            last.then_inc(s["rows_turned"], 1)

        @block.vector
        def _(dve):
            for r in range(PRM_ROWS):
                nc.vector.memset(rows[r][:], 0.0).then_inc(s["rows_zero"], 1)
            nc.vector.memset(env["ones"][:], 1.0)
            for i in range(NT):
                b = i % 2
                dve.wait_ge(s[f"turned{b}"], i // 2 + 1)
                nc.vector.tensor_copy(xT[:, :, i * P:(i + 1) * P], turn[b][:]).then_inc(s[f"copied{b}"], 1)
            dve.wait_ge(s["rows_turned"], 1)
            nc.vector.tensor_copy(prm[:, 0:PRM_ROWS * P], ps["rowsT"][:].rearrange("p r c -> p (r c)"))


RMS_SEMS = "squared0 squared1 summed total rstd_done norm_step hi_done lo_done mid_done modulated "


def rms_programs(nc, mem, env, block, s, tot, name, at, tails, act_middle=None):
    xT, ones = env["xT"], env["ones"]
    sq = [mem.at(f"{name}_sq{b}", at + 4 * b, [P, S]) for b in range(2)]
    sums = mem.at(f"{name}_sums", at + 8, [P, S])
    rstd = mem.at(f"{name}_rstd", at + 12, [P, S])
    mid = [mem.at(f"{name}_mid{b}", at + 16 + 4 * b, [P, S]) for b in range(2)]
    act_tail, dve_tail, pe_tail = tails(rstd, mid)

    @block.scalar
    def _(act):
        for k in range(KD):
            b = k % 2
            if k >= 2:
                act.wait_ge(s["summed"], k - 1)
            nc.scalar.activation(sq[b][:], xT[:, k, :], ACT.Square).then_inc(s[f"squared{b}"], 1)
        if act_middle:
            act_middle(act)
        act.wait_ge(s["norm_step"], 2)
        nc.scalar.activation(rstd[:], rstd[:], ACT.Sqrt).then_inc(s["rstd_done"], 1)
        if act_tail:
            act_tail(act)

    @block.vector
    def _(dve):
        for k in range(KD):
            dve.wait_ge(s[f"squared{k % 2}"], k // 2 + 1)
            if k == 0:
                nc.vector.tensor_copy(sums[:], sq[0][:]).then_inc(s["summed"], 1)
            else:
                dve.wait_ge(s["summed"], k)
                nc.vector.tensor_tensor(sums[:], sums[:], sq[k % 2][:], ALU.add).then_inc(s["summed"], 1)
        dve.wait_ge(s["total"], 1)
        steps = Steps(dve, s["norm_step"])
        steps.link(nc.vector.tensor_scalar(rstd[:], tot[:].rearrange("p h t -> p (h t)"), 1.0 / D, EPS, ALU.mult, ALU.add))
        steps.link(nc.vector.reciprocal(rstd[:], rstd[:]))
        dve.wait_ge(s["rstd_done"], 1)
        dve_tail(dve)

    @block.tensor
    def _(pe):
        pe.wait_ge(s["summed"], KD)
        for t in range(NH):
            last = nc.tensor.matmul(tot[:, t, :], ones[:], sums[:, t * HALF:(t + 1) * HALF], start=True, stop=True)
        last.then_inc(s["total"], 1)
        if pe_tail:
            pe_tail(pe)


class SplitNorm:

    def __init__(self, nc, mem, env, name, gain=None, scale=None, shift=None):
        self.nc, self.mem, self.env, self.name, self.gain, self.scale, self.shift = nc, mem, env, name, gain, scale, shift

    def programs(self, block, s, tot, at):
        nc, prm, xT, gain, scale, shift = self.nc, self.env["prm"], self.env["xT"], self.gain, self.scale, self.shift
        hi = self.env["hi"]
        self.s = s

        def tails(rstd, mid):
            self.mid = mid

            def act_tail(act):
                for k in range(KD):
                    act.wait_ge(s["mid_done"], k + 1)
                    if scale is not None:
                        nc.scalar.activation(mid[k % 2][:], mid[k % 2][:], ACT.Identity, bias=prm[:, shift + k:shift + k + 1],
                                             scale=prm[:, scale + k:scale + k + 1]).then_inc(s["modulated"], 1)
                        act.wait_ge(s["modulated"], k + 1)
                    nc.scalar.activation(hi[:, k, :], mid[k % 2][:], ACT.Copy).then_inc(s["hi_done"], 1)

            def dve_tail(dve):
                for k in range(KD):
                    if k >= 2:
                        dve.wait_ge(s["lo_done"], k - 1)
                    if gain is None:
                        nc.vector.tensor_tensor(mid[k % 2][:], xT[:, k, :], rstd[:], ALU.mult).then_inc(s["mid_done"], 1)
                    else:
                        nc.vector.scalar_tensor_tensor(out=mid[k % 2][:], in0=xT[:, k, :], scalar=prm[:, gain + k:gain + k + 1],
                                                       in1=rstd[:], op0=ALU.mult, op1=ALU.mult).then_inc(s["mid_done"], 1)

            return act_tail, dve_tail, None

        rms_programs(nc, self.mem, self.env, block, s, tot, self.name, at, tails)

    def pool_part(self, pool):
        nc, hi, lo = self.nc, self.env["hi"], self.env["lo"]
        for k in range(KD):
            pool.wait_ge(self.s["hi_done"], k + 1)
            nc.gpsimd.tensor_tensor(lo[:, k, :], self.mid[k % 2][:], hi[:, k, :], ALU.subtract).then_inc(self.s["lo_done"], 1)

    def ready(self, pe, k):
        pe.wait_ge(self.s["lo_done"], k + 1)


def norm_out(nc, mem, env, name, gain, out):
    xT, prm, ident = env["xT"], env["prm"], env["ident"]
    rows = [mem.at(f"{name}_rows{b}", 128 + 4 * b, [P, D]) for b in range(2)]
    o = out.rearrange("a (i p) d -> (a i) p d", p=P)

    banks = [("tot", [P, NH, HALF], F32), ("turn0", [P, KD, P], F32), ("turn1", [P, KD, P], F32)]
    with phase(nc, RMS_SEMS + "gained gained_too scaled " + both("rows_copied turned row_stored"), banks) as (block, s, ps):
        turn = [ps["turn0"], ps["turn1"]]

        @block.gpsimd
        def _(pool):
            pool.wait_ge(s["squared0"], KD // 2)
            pool.wait_ge(s["squared1"], KD // 2)
            for k in range(KD // 2):
                nc.gpsimd.tensor_tensor(xT[:, k, :], xT[:, k, :], prm[:, gain + k:gain + k + 1].broadcast_to([P, S]), ALU.mult)\
                    .then_inc(s["gained"], 1)

        def tails(rstd, mid):
            def dve_tail(dve):
                dve.wait_ge(s["gained"], KD // 2)
                dve.wait_ge(s["gained_too"], KD // 2)
                for i in range(NT):
                    c = slice(i * P, (i + 1) * P)
                    nc.vector.tensor_tensor(xT[:, :, c], xT[:, :, c], rstd[:, c].unsqueeze(1).broadcast_to([P, KD, P]), ALU.mult)\
                        .then_inc(s["scaled"], 1)

            def pe_tail(pe):
                for i in range(NT):
                    pe.wait_ge(s["scaled"], i + 1)
                    b = i % 2
                    if i >= 2:
                        pe.wait_ge(s[f"rows_copied{b}"], i // 2)
                    for k in range(KD):
                        last = nc.tensor.transpose(turn[b][:, k, :], xT[:, k, i * P:(i + 1) * P], ident[:])
                    last.then_inc(s[f"turned{b}"], 1)

            def act_tail(act):
                for i in range(NT):
                    b = i % 2
                    act.wait_ge(s[f"turned{b}"], i // 2 + 1)
                    if i >= 2:
                        act.wait_ge(s[f"row_stored{b}"], 16 * (i // 2))
                    nc.scalar.activation(rows[b][:].rearrange("p (k f) -> p k f", k=KD), turn[b][:], ACT.Copy).then_inc(s[f"rows_copied{b}"], 1)

            return act_tail, dve_tail, pe_tail

        def gain_too(act):
            for k in range(KD // 2, KD):
                nc.scalar.activation(xT[:, k, :], xT[:, k, :], ACT.Copy, scale=prm[:, gain + k:gain + k + 1]).then_inc(s["gained_too"], 1)

        rms_programs(nc, mem, env, block, s, ps["tot"], name, 104, tails, gain_too)

        @block.sync
        def _(sp):
            for i in range(NT):
                b = i % 2
                sp.wait_ge(s[f"rows_copied{b}"], i // 2 + 1)
                sp.dma_start(o[i], rows[b][:]).then_inc(s[f"row_stored{b}"], 16)
            for b in range(2):
                sp.wait_ge(s[f"row_stored{b}"], 16 * (NT // 2))


def store_epilogue(nc, mem, name, at, n_units, dst, step=1):
    stage = [mem.at(f"{name}_stage{b}", at + 4 * b, [P, S]) for b in range(2)]
    half = lambda b, h: stage[b][:].rearrange("p (j h m) -> p h m j", h=NH, j=step)[:, h]
    chunks = lambda b, h, acc: acc[b][:, h, :].rearrange("p (m j) -> p m j", j=step)

    def epilogue(block, s, acc, ps):
        @block.scalar
        def _(act):
            def copy(p, b):
                act.wait_ge(s[f"products_done{b}"], p + 1)
                act.wait_ge(s[f"stored{b}"], 16 * p)
                nc.scalar.activation(half(b, 0), chunks(b, 0, acc), ACT.Copy).then_inc(s[f"epilogue_a{b}"], 1)
                act.wait_ge(s[f"epilogue_a{b}"], p + 1)
                act.wait_ge(s[f"acc_read{b}"], p + 1)
                act.dma_start(dst[bass.ds((2 * p + b) * P, P), :], stage[b][:]).then_inc(s[f"stored{b}"], 16)

            pairs(act, n_units, copy)
            act.wait_ge(s["stored0"], 16 * ((n_units + 1) // 2))
            act.wait_ge(s["stored1"], 16 * (n_units // 2))

        @block.vector
        def _(dve):
            def copy(p, b):
                dve.wait_ge(s[f"products_done{b}"], p + 1)
                dve.wait_ge(s[f"stored{b}"], 16 * p)
                dve.wait_ge(s[f"epilogue_a{b}"], p + 1)
                nc.vector.tensor_copy(half(b, 1), chunks(b, 1, acc)).then_inc(s[f"acc_read{b}"], 1)

            pairs(dve, n_units, copy)

    return epilogue


def residual_gemm(nc, mem, env, name, weight, rhs, k_tiles, gate=None):
    xT, prm = env["xT"], env["prm"]

    def epilogue(block, s, acc, ps):
        @block.vector
        def _(dve):
            def add(p, b):
                dve.wait_ge(s[f"products_done{b}"], p + 1)
                u = 2 * p + b
                x = xT[:, bass.ds(u, 1), :].rearrange("p k (h t) -> p (k h) t", h=NH)
                if gate is None:
                    nc.vector.tensor_tensor(x, x, acc[b][:], ALU.add).then_inc(s[f"acc_read{b}"], 1)
                else:
                    nc.vector.scalar_tensor_tensor(out=x, in0=acc[b][:], scalar=prm[:, bass.ds(gate + u, 1)], in1=x,
                                                   op0=ALU.mult, op1=ALU.add).then_inc(s[f"acc_read{b}"], 1)

            pairs(dve, KD, add)

    gemm(nc, mem, name, KD, k_tiles, weight, rhs, epilogue, 104)


def columns(w, k_tiles):
    v = w.rearrange("a (k p) n -> (a p) k n", p=P)
    return lambda u: v[:, :, bass.ds(u * P, P)]


def feed_forward(nc, mem, env, name, up, down, kind, norm, gate=None):
    xT, prm, hi, lo = env["xT"], env["prm"], env["hi"], env["lo"]
    C = FT // 2
    at = 104
    raw = [mem.at(f"{name}_raw{b}", at + 4 * b, [P, KD, P]) for b in range(2)]
    w_hi = [mem.at(f"{name}_whi{b}", at + 8 + 4 * b, [P, KD, P], F32R) for b in range(2)]
    w_lo = [mem.at(f"{name}_wlo{b}", at + 16 + 4 * b, [P, KD, P], F32R) for b in range(2)]
    d_raw = mem.at(f"{name}_draw", at + 24, [P, 2, D])
    d_hi = mem.at(f"{name}_dhi", at + 32, [P, 2, D], F32R)
    d_lo = mem.at(f"{name}_dlo", at + 40, [P, 2, D], F32R)
    g_hi = mem.at(f"{name}_ghi", at + 48, [P, 2, S], F32R)
    g_lo = mem.at(f"{name}_glo", at + 56, [P, 2, S], F32R)
    conv = mem.at(f"{name}_conv", at + 64, [P, S])
    act_out = mem.at(f"{name}_act", at + 68, [P, S])
    prod = [mem.at(f"{name}_prod{j}", at + 72 + 4 * j, [P, S]) for j in range(2)]
    names = ("up_loaded0 up_loaded1 up_hi0 up_hi1 up_split0 up_split1 up_done0 up_done1 a_read b_read "
             "down_loaded down_hi down_split down_done0 down_done1 chunk_done down_read0 down_read1 "
             "conv_done activated product_done g_hi_done g_split vector_step ") + RMS_SEMS
    banks = [(n, [P, NH, HALF], F32) for n in ("up0", "up1", "dn0", "dn1")]
    with phase(nc, names, banks) as (block, s, ps):
        acc = [ps["up0"], ps["up1"]]
        dn = [ps["dn0"], ps["dn1"]]
        norm.programs(block, s, dn[1], NORM_AT)

        def turns(eng, hidden, down, between=None):
            def turn(c):
                hidden(c, 0)
                down(c - 1)
                hidden(c, 1)

            hidden(0, 0)
            if between:
                between(eng)
            hidden(0, 1)
            turn(1)
            with eng.Fori(2, C) as c:
                turn(c)
            down(C - 1)

        @block.sync
        def _(sp):
            def load_up(c, j):
                for i in range(2):
                    sp.wait_ge(s[f"up_split{i}"], 2 * c + j)
                    sp.dma_start(raw[i][:], up(i, 2 * c + j)).then_inc(s[f"up_loaded{i}"], 16)

            def load_down(d):
                sp.wait_ge(s["down_split"], d)
                sp.dma_start(d_raw[:], down(d)).then_inc(s["down_loaded"], 16)

            turns(sp, load_up, load_down)

        @block.gpsimd
        def _(pool):
            def split_up(c, j):
                for i in range(2):
                    pool.wait_ge(s[f"up_loaded{i}"], 32 * c + 16 * (j + 1))
                    pool.wait_ge(s[f"up_done{i}"], 2 * c + j)
                    pool_high(nc, w_hi[i][:], raw[i][:], mem.one).then_inc(s[f"up_hi{i}"], 1)
                    pool.wait_ge(s[f"up_hi{i}"], 2 * c + j + 1)
                    nc.gpsimd.tensor_tensor(w_lo[i][:], raw[i][:], w_hi[i][:], ALU.subtract).then_inc(s[f"up_split{i}"], 1)

            def split_down(d):
                pool.wait_ge(s["down_loaded"], 16 * d + 16)
                pool.wait_ge(s["chunk_done"], d)
                pool_high(nc, d_hi[:], d_raw[:], mem.one).then_inc(s["down_hi"], 1)
                pool.wait_ge(s["down_hi"], d + 1)
                nc.gpsimd.tensor_tensor(d_lo[:], d_raw[:], d_hi[:], ALU.subtract).then_inc(s["down_split"], 1)

            turns(pool, split_up, split_down, norm.pool_part)

        @block.tensor
        def _(pe):
            first = [True]

            def up_products(c, j):
                for i in range(2):
                    pe.wait_ge(s[f"up_split{i}"], 2 * c + j + 1)
                    pe.wait_ge(s["b_read" if i else "a_read" if kind == "conv" else "activated"], 2 * c + j)
                    ready = (lambda k: norm.ready(pe, k)) if first else None
                    first.clear()
                    three_pass(nc, acc[i], w_hi[i], w_lo[i], hi, lo, KD, ready=ready).then_inc(s[f"up_done{i}"], 1)

            def down_products(d):
                pe.wait_ge(s["down_split"], d + 1)
                pe.wait_ge(s["g_split"], 2 * d + 2)
                for n in range(KD):
                    b = n % 2
                    pe.wait_ge(s[f"down_read{b}"], 4 * d + n // 2)
                    last = three_pass(nc, dn[b], d_hi, d_lo, g_hi, g_lo, 2, slice(n * P, (n + 1) * P))
                    last.then_inc(s[f"down_done{b}"] if n < KD - 1 else s["chunk_done"], 1)

            turns(pe, up_products, down_products)

        @block.vector
        def _(dve):
            def hidden(c, j):
                f = 2 * c + j
                dve.wait_ge(s["up_done0"], f + 1)
                a = acc[0][:].rearrange("p h t -> p (h t)")
                if kind == "conv":
                    steps = Steps(dve, s["vector_step"], f * 2)
                    dve.wait_ge(s["activated"], f)
                    w = [prm[:, bass.ds(f + (PRM["conv_w"] + FT * i), 1)] for i in range(3)]
                    steps.link(nc.vector.tensor_scalar(conv[:], a, w[2], prm[:, bass.ds(f + PRM["conv_b"], 1)], ALU.mult, ALU.add))
                    steps.link(nc.vector.scalar_tensor_tensor(out=conv[:, 1:S], in0=a[:, 0:S - 1], scalar=w[1], in1=conv[:, 1:S],
                                                              op0=ALU.mult, op1=ALU.add))
                    nc.vector.scalar_tensor_tensor(out=conv[:, 2:S], in0=a[:, 0:S - 2], scalar=w[0], in1=conv[:, 2:S],
                                                   op0=ALU.mult, op1=ALU.add).then_inc(s["a_read"], 1)
                dve.wait_ge(s["activated"], f + 1)
                dve.wait_ge(s["up_done1"], f + 1)
                nc.vector.tensor_tensor(prod[j][:].rearrange("p (h t) -> p h t", h=NH), act_out[:].rearrange("p (h t) -> p h t", h=NH),
                                        acc[1][:], ALU.mult).then_inc(s["b_read"], 1)
                if j == 1:
                    split_low(c, 1)

            def split_low(c, j):
                dve.wait_ge(s["g_hi_done"], 2 * c + j + 1)
                nc.vector.tensor_tensor(g_lo[:, j, :], prod[j][:], g_hi[:, j, :], ALU.subtract).then_inc(s["g_split"], 1)

            def add_down(d):
                for n in range(KD):
                    b = n % 2
                    if n < KD - 1:
                        dve.wait_ge(s[f"down_done{b}"], (4 if b == 0 else 3) * d + n // 2 + 1)
                    else:
                        dve.wait_ge(s["chunk_done"], d + 1)
                    x = xT[:, n, :].rearrange("p (h t) -> p h t", h=NH)
                    if gate is None:
                        nc.vector.tensor_tensor(x, x, dn[b][:], ALU.add).then_inc(s[f"down_read{b}"], 1)
                    else:
                        nc.vector.scalar_tensor_tensor(out=x, in0=dn[b][:], scalar=prm[:, gate + n:gate + n + 1], in1=x,
                                                       op0=ALU.mult, op1=ALU.add).then_inc(s[f"down_read{b}"], 1)

            def turn(c):
                hidden(c, 0)
                add_down(c - 1)
                split_low(c, 0)
                hidden(c, 1)

            hidden(0, 0)
            split_low(0, 0)
            hidden(0, 1)
            turn(1)
            with dve.Fori(2, C) as c:
                turn(c)
            add_down(C - 1)

        @block.scalar
        def _(act):
            def hidden(c, j):
                f = 2 * c + j
                act.wait_ge(s["b_read"], f)
                if kind == "conv":
                    act.wait_ge(s["a_read"], f + 1)
                    nc.scalar.activation(act_out[:], conv[:], ACT.Gelu_apprx_tanh).then_inc(s["activated"], 1)
                else:
                    act.wait_ge(s["up_done0"], f + 1)
                    nc.scalar.activation(act_out[:].rearrange("p (h t) -> p h t", h=NH), acc[0][:], ACT.Silu).then_inc(s["activated"], 1)
                act.wait_ge(s["chunk_done"], c)
                act.wait_ge(s["b_read"], f + 1)
                nc.scalar.activation(g_hi[:, j, :], prod[j][:], ACT.Copy).then_inc(s["g_hi_done"], 1)

            def both_tiles(c):
                for j in range(2):
                    hidden(c, j)

            repeat(act, C, both_tiles)




def retention(nc, mem, env, projT, ins):
    prm, ident, hi, lo = env["prm"], env["ident"], env["hi"], env["lo"]
    NCH = S // P
    qT = [mem.at(f"ret_q{b}", 104 + 4 * b, [P, S]) for b in range(2)]
    kT = [mem.at(f"ret_k{b}", 112 + 4 * b, [P, S]) for b in range(2)]
    vT = [mem.at(f"ret_v{b}", 120 + 8 * b, [P, 2, S]) for b in range(2)]
    gT = [mem.at(f"ret_g{b}", 136 + 8 * b, [P, 2, S]) for b in range(2)]
    y32 = [mem.at(f"ret_y{b}", 152 + 8 * b, [P, 2, S]) for b in range(2)]
    dmask = mem.at("ret_dmask", 168, [P, RET_H, P])
    xi = mem.at("ret_xi", 170, [P, RET_H, P])
    col = mem.at("ret_col", 172, [P, 2 * RET_H])
    kn = [mem.at(f"ret_kn{q}", 173 + q, [P, P]) for q in range(2)]
    vn = [mem.at(f"ret_vn{q}", 175 + q, [P, RET_DV]) for q in range(2)]
    pT = [mem.at(f"ret_p{q}", 177 + q, [P, P]) for q in range(2)]
    qx = [mem.at(f"ret_qx{q}", 179 + q, [P, P]) for q in range(2)]
    R = [mem.at(f"ret_R{q}", 181 + q, [P, RET_DV]) for q in range(2)]
    on = [mem.at(f"ret_on{q}", 183 + q, [P, RET_DV]) for q in range(2)]
    stats = [mem.at(f"ret_stats{q}", 185 + q, [P, 16]) for q in range(2)]

    zeta = [mem.at(f"ret_zeta{b}", 187 + b * 0.125, [P, 1]) for b in range(2)]
    dec = [mem.at(f"ret_dec{b}", 187.25 + b * 0.125, [P, 1]) for b in range(2)]
    gain = [mem.at(f"ret_gain{b}", 187.5 + b * 0.125, [P, 2]) for b in range(2)]
    dmask_h = [mem.at(f"ret_dmask_h{b}", 188 + b * 0.5, [P, P]) for b in range(2)]
    xi_h = [mem.at(f"ret_xi_h{b}", 189 + b * 0.5, [P, P]) for b in range(2)]

    names = both("head_loaded gates_loaded turned kv_copied scores_masked q_scaled out_done state_done stats_done root_done "
                 "normed y_turned y_gated silu_done head_done high_done") + "consts zeta_done vector_step scalar_step "
    banks = [(f"{n}{q}", [P, HALF], F32) for n in ("turn", "score", "out", "y") for q in range(2)]
    with phase(nc, names, banks) as (block, s, ps):
        turn, score, outp, y = ([ps[f"{n}0"], ps[f"{n}1"]] for n in ("turn", "score", "out", "y"))

        def heads(eng, body):
            pairs(eng, RET_H, body)

        def use(p, b, n):
            return NCH * p + (NCH // 2) * b + n // 2

        @block.sync
        def _(sp):
            sp.dma_start(dmask[:], ins["k_dmask"].rearrange("h m c -> m h c")).then_inc(s["consts"], 16)
            sp.dma_start(xi[:], ins["k_xi"]).then_inc(s["consts"], 16)
            sp.dma_start(col[:], ins["k_retcol"]).then_inc(s["consts"], 16)

            def load(p, b):
                h = 2 * p + b
                sp.wait_ge(s[f"head_done{b}"], p)
                sp.dma_start(qT[b][:], projT[bass.ds((RQ + h) * P, P), :]).then_inc(s[f"head_loaded{b}"], 16)
                sp.dma_start(kT[b][:], projT[bass.ds((RK + h) * P, P), :]).then_inc(s[f"head_loaded{b}"], 16)
                sp.dma_start(vT[b][:], projT[bass.ds((RV + 2 * h) * P, 2 * P), :].rearrange("(e p) t -> p e t", p=P)).then_inc(s[f"head_loaded{b}"], 16)
                sp.dma_start(gT[b][:], projT[bass.ds((RG + 2 * h) * P, 2 * P), :].rearrange("(e p) t -> p e t", p=P)).then_inc(s[f"gates_loaded{b}"], 16)

            heads(sp, load)

        @block.tensor
        def _(pe):
            def stage_a(p, b, n):
                q, m = n % 2, use(p, b, n)
                if n == 0:
                    pe.wait_ge(s[f"head_loaded{b}"], 48 * p + 48)
                c = slice(n * P, (n + 1) * P)
                pe.wait_ge(s[f"kv_copied{q}"], m)
                pe.wait_ge(s[f"scores_masked{q}"], m)
                nc.tensor.transpose(turn[q][:, 0:P], kT[b][:, c], ident[:])
                for e in range(2):
                    nc.tensor.transpose(turn[q][:, (1 + e) * P:(2 + e) * P], vT[b][:, e, c], ident[:])
                nc.tensor.matmul(score[q][:, 0:P], kT[b][:, c], qT[b][:, c], start=True, stop=True).then_inc(s[f"turned{q}"], 1)

            def stage_b(p, b, n):
                q, m = n % 2, use(p, b, n)
                pe.wait_ge(s[f"kv_copied{q}"], m + 1)
                pe.wait_ge(s[f"scores_masked{q}"], m + 1)
                pe.wait_ge(s[f"q_scaled{q}"], m + 1)
                pe.wait_ge(s[f"normed{q}"], m)
                pe.wait_ge(s[f"state_done{q}"], m)
                nc.tensor.matmul(outp[q][:, 0:RET_DV], pT[q][:], vn[q][:], start=True, stop=(n == 0))
                if n > 0:
                    pe.wait_ge(s[f"state_done{1 - q}"], use(p, b, n - 1) + 1)
                    nc.tensor.matmul(outp[q][:, 0:RET_DV], qx[q][:], R[q][:], start=False, stop=True)
                nc.tensor.matmul(outp[q][:, RET_DV:2 * RET_DV], kn[q][:], vn[q][:], start=True, stop=True).then_inc(s[f"out_done{q}"], 1)

            def stage_d(p, b, n):
                q, m = n % 2, use(p, b, n)
                pe.wait_ge(s[f"normed{q}"], m + 1)
                pe.wait_ge(s[f"y_gated{q}"], m)
                for e in range(2):
                    last = nc.tensor.transpose(y[q][:, e * P:(e + 1) * P], on[q][:, e * P:(e + 1) * P], ident[:])
                last.then_inc(s[f"y_turned{q}"], 1)

            def head(p, b):
                stage_a(p, b, 0)
                for n in range(NCH):
                    if n + 1 < NCH:
                        stage_a(p, b, n + 1)
                    stage_b(p, b, n)
                    if n > 0:
                        stage_d(p, b, n - 1)
                stage_d(p, b, NCH - 1)

            heads(pe, head)

        @block.scalar
        def _(act):
            act.wait_ge(s["consts"], 48)

            def copies(p, b, n):
                q, m = n % 2, use(p, b, n)
                act.wait_ge(s[f"out_done{q}"], m)
                act.wait_ge(s[f"turned{q}"], m + 1)
                nc.scalar.activation(vn[q][:], turn[q][:, P:3 * P], ACT.Copy).then_inc(s["scalar_step"], 1)
                nc.scalar.activation(kn[q][:], turn[q][:, 0:P], ACT.Identity, scale=zeta[b][:]).then_inc(s[f"kv_copied{q}"], 1)

            def root(p, b, n):
                q, m = n % 2, use(p, b, n)
                act.wait_ge(s[f"stats_done{q}"], m + 1)
                nc.scalar.activation(stats[q][:, 10:11], stats[q][:, 9:10], ACT.Sqrt).then_inc(s[f"root_done{q}"], 1)

            def head(p, b):
                act.wait_ge(s[f"gates_loaded{b}"], 16 * p + 16)
                nc.scalar.activation(gT[b][:], gT[b][:], ACT.Silu).then_inc(s[f"silu_done{b}"], 1)
                act.wait_ge(s[f"zeta_done"], 2 * p + b + 1)
                for n in range(NCH):
                    copies(p, b, n)
                    if n > 0:
                        root(p, b, n - 1)
                root(p, b, NCH - 1)

            heads(act, head)

        @block.gpsimd
        def _(pool):
            pool.wait_ge(s["consts"], 48)

            def head(p, b):
                pool.wait_ge(s[f"head_loaded{b}"], 48 * p + 48)
                for n in range(NCH):
                    q, m = n % 2, use(p, b, n)
                    if n == 0:
                        pool.wait_ge(s["zeta_done"], 2 * p + b + 1)
                    pool.wait_ge(s[f"out_done{q}"], m)
                    nc.gpsimd.tensor_tensor(qx[q][:], qT[b][:, n * P:(n + 1) * P], xi_h[b][:], ALU.mult).then_inc(s[f"q_scaled{q}"], 1)

            heads(pool, head)

        @block.vector
        def _(dve):
            dve.wait_ge(s["consts"], 48)

            def masked(p, b, n):
                q, m = n % 2, use(p, b, n)
                dve.wait_ge(s[f"out_done{q}"], m)
                dve.wait_ge(s[f"turned{q}"], m + 1)
                nc.vector.tensor_tensor(pT[q][:], score[q][:, 0:P], dmask_h[b][:], ALU.mult).then_inc(s[f"scores_masked{q}"], 1)

            def state(p, b, n):
                q, m = n % 2, use(p, b, n)
                dve.wait_ge(s[f"out_done{q}"], m + 1)
                addend = outp[q][:, RET_DV:2 * RET_DV]
                st = stats[q]
                steps = Steps(dve, s["vector_step"], (16 * p + 8 * b + n) * 3)
                steps.link(nc.vector.bn_stats(st[:, 0:6], outp[q][:, 0:RET_DV]))
                if n == 0:
                    nc.vector.tensor_copy(R[1][:], addend).then_inc(s[f"state_done{q}"], 1)
                else:
                    dve.wait_ge(s[f"state_done{1 - q}"], use(p, b, n - 1) + 1)
                    nc.vector.scalar_tensor_tensor(out=R[1 - q][:], in0=R[q][:], scalar=dec[b][:], in1=addend,
                                                   op0=ALU.mult, op1=ALU.add).then_inc(s[f"state_done{q}"], 1)
                steps.link(nc.vector.bn_aggr(st[:, 6:8], st[:, 0:6]))
                steps.link(nc.vector.tensor_scalar(st[:, 8:9], st[:, 7:8], EPS, None, ALU.add))
                nc.vector.reciprocal(st[:, 9:10], st[:, 8:9]).then_inc(s[f"stats_done{q}"], 1)

            def normed(p, b, n):
                q, m = n % 2, use(p, b, n)
                dve.wait_ge(s[f"y_turned{q}"], m)
                dve.wait_ge(s[f"root_done{q}"], m + 1)
                st = stats[q]
                nc.vector.tensor_scalar(on[q][:], outp[q][:, 0:RET_DV], st[:, 6:7], st[:, 10:11], ALU.subtract, ALU.mult).then_inc(s[f"normed{q}"], 1)

            def gated(p, b, n):
                q, m = n % 2, use(p, b, n)
                dve.wait_ge(s[f"y_turned{q}"], m + 1)
                c = slice(n * P, (n + 1) * P)
                for e in range(2):
                    last = nc.vector.scalar_tensor_tensor(out=y32[b][:, e, c], in0=y[q][:, e * P:(e + 1) * P],
                                                          scalar=gain[b][:, e:e + 1], in1=gT[b][:, e, c], op0=ALU.mult, op1=ALU.mult)
                last.then_inc(s[f"y_gated{q}"], 1)

            def head(p, b):
                h = 2 * p + b
                nc.vector.tensor_scalar(zeta[b][:], col[:, bass.ds(h, 1)], 1.0, None, ALU.mult)
                nc.vector.tensor_scalar(dec[b][:], col[:, bass.ds(h + RET_H, 1)], 1.0, None, ALU.mult)
                nc.vector.tensor_scalar(gain[b][:], prm[:, bass.ds(2 * h + PRM["ret_gn_g"], 2)], 1.0, None, ALU.mult)
                nc.vector.tensor_scalar(dmask_h[b][:], dmask[:, bass.ds(h, 1), :].rearrange("m h c -> m (h c)"), 1.0, None, ALU.mult)
                nc.vector.tensor_scalar(xi_h[b][:], xi[:, bass.ds(h, 1), :].rearrange("m h c -> m (h c)"), 1.0, None, ALU.mult).then_inc(s["zeta_done"], 1)
                dve.wait_ge(s["zeta_done"], h + 1)
                dve.wait_ge(s[f"silu_done{b}"], p + 1)
                masked(p, b, 0)
                for n in range(NCH):
                    if n + 1 < NCH:
                        masked(p, b, n + 1)
                    state(p, b, n)
                    if n > 0:
                        normed(p, b, n - 1)
                    if n > 1:
                        gated(p, b, n - 2)
                normed(p, b, NCH - 1)
                gated(p, b, NCH - 2)
                gated(p, b, NCH - 1)
                dve.wait_ge(s["y_gated0"], use(p, b, NCH))
                dve.wait_ge(s["y_gated1"], use(p, b, NCH))
                nc.vector.tensor_scalar(hi[:, bass.ds(2 * h, 2), :], y32[b][:], 1.0, None, ALU.mult).then_inc(s[f"high_done{b}"], 1)
                dve.wait_ge(s[f"high_done{b}"], p + 1)
                nc.vector.tensor_tensor(lo[:, bass.ds(2 * h, 2), :], y32[b][:], hi[:, bass.ds(2 * h, 2), :], ALU.subtract).then_inc(s[f"head_done{b}"], 1)

            heads(dve, head)


def nsa_buffers(mem):
    return dict(
        ksT=mem.at("nsa_ksT", 104, [P, NSA_G, S]),
        kwT=mem.at("nsa_kwT", 112, [P, NSA_G, S]),
        ks_both=mem.at("nsa_ks_both", 164, [P, NSA_G, S], F32R),
        kw_both=mem.at("nsa_kw_both", 172, [P, NSA_G, S], F32R),
        ks_blk=mem.at("nsa_ks_blk", 180, [P, NSA_G, S], F32R),
        vs=mem.at("nsa_vs", 120, [P, NT, P]),
        vw=mem.at("nsa_vw", 124, [P, NT, P]),
        kcT=mem.at("nsa_kcT", 128, [P, NSA_G, NC_PAD]),
        vc=mem.at("nsa_vc", 128.5, [P, NSA_G, NSA_D]),
        gates=mem.at("nsa_gates", 129, [P, NT, N_GATE]),
        slopes=mem.at("nsa_slopes", 130, [P, NSA_H]),
        o=mem.at("nsa_o", 56, [P, NT, NSA_H * NSA_D]),
        dist=mem.at("nsa_dist", 88, [P, 2 * S - P], F32R),
        dwin=mem.at("nsa_dwin", 95.5, [P, WINDOW + P], F32R),
        dcmp=mem.at("nsa_dcmp", 98, [P, NT, NC_PAD], F32R),
        cmask=mem.at("nsa_cmask", 100, [P, NT, NC_PAD]),
    )


def nsa_prepare(nc, mem, env, N, projT, ins):
    LP = CMP_LEN // 2
    prm, ident = env["prm"], env["ident"]
    scale = NSA_D ** -0.5
    w1 = [mem.at(f"cmp_w1{j}", 131 + 16 * j, [P, LP, CMP_HID]) for j in range(2)]
    src = [[mem.at(f"cmp_src{j}{g}", 163 + 8 * j + 4 * g, [P, S]) for g in range(NSA_G)] for j in range(2)]
    shifted = [mem.at(f"cmp_shift{i}", 195 + 4 * i, [P, NSA_G, NC_PAD, CMP_STRIDE // 2]) for i in range(2)]
    w2 = mem.at("cmp_w2", 203, [P, 2, 2, NSA_D])
    pos = mem.at("cmp_pos", 204, [LP, 2, P])
    posT = mem.at("cmp_posT", 205, [P, 2, LP])
    hid = mem.at("cmp_hid", 205.5, [P, 2, NSA_G, NC_PAD])
    kraw = mem.at("nsa_kraw", 40, [P, 2, NSA_G, S])
    tmp = mem.at("nsa_tmp", 80, [P, S])
    names = ("w1a w1b w2_in pos_in src_in kv_in tab_in pos_turned pos_copied shift0 shift1 hidden_done hid_act_done out_done out_copied "
             "vrow_turned vrow_copied gate_done table_done k_done pad_done gate_turned gate_copied vrow_in gate_in vector_step scalar_step")
    banks = [("hid_ps0", [P, 2, NC_PAD], F32), ("hid_ps1", [P, 2, NC_PAD], F32), ("out_ps", [P, 2, NSA_D], F32), ("pos_ps", [P, 2, LP], F32),
             ("vrow_ps", [P, 4, P], F32), ("gate_ps", [P, NT, N_GATE], F32)]
    vrow = mem.at("nsa_vrow", 84, [P, S])
    with phase(nc, names, banks) as (block, s, ps):
        @block.sync
        def _(sp):
            for j, name in enumerate(("cmp_w1_k", "cmp_w1_v")):
                sp.dma_start(w1[j][:], ins[name].rearrange("a (l p) n -> (a p) l n", p=P)).then_inc(s["w1a" if j == 0 else "w1b"], 16)

        @block.scalar
        def _(act):
            for j, name in enumerate(("cmp_pos_k", "cmp_pos_v")):
                act.dma_start(pos[:, j, :], ins[name].rearrange("a (l q) d -> (a l) (q d)", q=2)).then_inc(s["pos_in"], 16)
            for j, t in enumerate((KCR, VCR)):
                for g in range(NSA_G):
                    rows = projT[t * P + g * NSA_D:t * P + (g + 1) * NSA_D, :]
                    act.dma_start(src[j][g][0:NSA_D, :], rows).then_inc(s["src_in"], 16)
                    act.dma_start(src[j][g][NSA_D:P, 0:S - 1], rows[:, 1:S]).then_inc(s["src_in"], 16)
            for j, name in enumerate(("cmp_w2_k", "cmp_w2_v")):
                act.dma_start(w2[:, j], ins[name].rearrange("a (i p) d -> (a p) i d", p=P)).then_inc(s["w2_in"], 16)
            act.dma_start(tmp[0:N_GATE, :], projT[GATE * P:GATE * P + N_GATE, :]).then_inc(s["gate_in"], 16)
            for j, t in enumerate((KS, KW)):
                for g in range(NSA_G):
                    act.dma_start(kraw[0:NSA_D, j, g, :], projT[t * P + g * NSA_D:t * P + (g + 1) * NSA_D, :]).then_inc(s["kv_in"], 16)
            act.dma_start(N["ksT"][NSA_D:NSA_D + N_BLK], ins["k_onehot"]).then_inc(s["tab_in"], 16)
            act.dma_start(N["slopes"][:], ins["k_slopes"]).then_inc(s["tab_in"], 16)
            act.dma_start(N["cmask"][:], ins["k_cmask"]).then_inc(s["tab_in"], 16)
            act.wait_ge(s["gate_in"], 16)
            nc.scalar.activation(tmp[0:N_GATE, :], tmp[0:N_GATE, :], ACT.Sigmoid).then_inc(s["gate_done"], 1)
            for j in range(2):
                act.wait_ge(s["hidden_done"], j + 1)
                if j == 1:
                    act.wait_ge(s["out_done"], 1)
                bias = PRM["cmp_b1_k" if j == 0 else "cmp_b1_v"]
                act.wait_ge(s["pad_done"], 1)
                for i in range(2):
                    for g in range(NSA_G):
                        last = nc.scalar.activation(hid[:, i, g, 0:N_CMP], ps[f"hid_ps{g}"][:, i, 0:N_CMP], ACT.Gelu_apprx_tanh,
                                                    bias=prm[:, bias + i:bias + i + 1])
                last.then_inc(s["hid_act_done"], 1)
                act.wait_ge(s["out_done"], j + 1)
                if j == 0:
                    nc.scalar.activation(N["kcT"][0:NSA_D], ps["out_ps"][0:NSA_D], ACT.Copy, scale=scale).then_inc(s["out_copied"], 1)
                else:
                    nc.scalar.activation(N["vc"][:], ps["out_ps"][:], ACT.Copy).then_inc(s["out_copied"], 1)

        @block.gpsimd
        def _(pool):
            for j, t in enumerate((VS, VW)):
                if j == 1:
                    pool.wait_ge(s["vrow_turned"], 2)
                pool.dma_start(vrow[:], projT[t * P:(t + 1) * P, :]).then_inc(s["vrow_in"], 16)
            for name, dst in (("k_dist", N["dist"]), ("k_dwin", N["dwin"]), ("k_dcmp", N["dcmp"])):
                pool.dma_start(dst[:], ins[name]).then_inc(s["table_done"], 16)
            pool.wait_ge(s["table_done"], 48)

        @block.tensor
        def _(pe):
            pe.wait_ge(s["pos_in"], 32)
            for j in range(2):
                last = nc.tensor.transpose(ps["pos_ps"][:, j, :], pos[:, j, :], ident[0:LP, 0:LP])
            last.then_inc(s["pos_turned"], 1)
            pe.wait_ge(s["gate_done"], 1)
            for i in range(NT):
                last = nc.tensor.transpose(ps["gate_ps"][:, i, :], tmp[0:N_GATE, i * P:(i + 1) * P], ident[0:N_GATE, 0:N_GATE])
            last.then_inc(s["gate_turned"], 1)
            for j in range(2):
                pe.wait_ge(s["vrow_in"], 16 * (j + 1))
                for half in range(2):
                    if 2 * j + half > 0:
                        pe.wait_ge(s["vrow_copied"], 2 * j + half)
                    for i in range(4):
                        c = (half * 4 + i) * P
                        last = nc.tensor.transpose(ps["vrow_ps"][:, i, :], vrow[:, c:c + P], ident[:])
                    last.then_inc(s["vrow_turned"], 1)
            for j in range(2):
                pe.wait_ge(s["w1a" if j == 0 else "w1b"], 16)
                pe.wait_ge(s["shift0"], j + 1)
                pe.wait_ge(s["shift1"], j + 1)
                if j == 1:
                    pe.wait_ge(s["hid_act_done"], 1)
                for i in range(2):
                    for l in range(LP):
                        half, r = divmod(l, LP // 2)
                        for g in range(NSA_G):
                            last = nc.tensor.matmul(ps[f"hid_ps{g}"][:, i, 0:N_CMP], w1[j][:, l, i * P:(i + 1) * P],
                                                    shifted[half][:, g, half:half + N_CMP, r], start=(l == 0), stop=(l == LP - 1))
                last.then_inc(s["hidden_done"], 1)
                pe.wait_ge(s["hid_act_done"], j + 1)
                pe.wait_ge(s["w2_in"], 32)
                if j == 1:
                    pe.wait_ge(s["out_copied"], 1)
                for g in range(NSA_G):
                    for half in range(1 if j == 0 else 2):
                        for i in range(2):
                            out = ps["out_ps"][half * NSA_D:(half + 1) * NSA_D, g, :]
                            if j == 0:
                                last = nc.tensor.matmul(out, w2[:, 0, i, :], hid[:, i, g, :], start=(i == 0), stop=(i == 1))
                            else:
                                last = nc.tensor.matmul(out, hid[:, i, g, :], w2[:, 1, i, :], start=(i == 0), stop=(i == 1))
                last.then_inc(s["out_done"], 1)

        @block.vector
        def _(dve):
            nc.vector.memset(hid[:, :, :, N_CMP:NC_PAD], 0.0).then_inc(s["pad_done"], 1)
            dve.wait_ge(s["pos_turned"], 1)
            nc.vector.tensor_copy(posT[:], ps["pos_ps"][:]).then_inc(s["pos_copied"], 1)
            dve.wait_ge(s["pos_copied"], 1)
            dve.wait_ge(s["src_in"], 16 * 8)

            def shift(j):
                for half in range(2):
                    p = posT[:, j, half * LP // 2:(half + 1) * LP // 2].unsqueeze(1).broadcast_to([P, NC_PAD, LP // 2])
                    for g in range(NSA_G):
                        even = src[j][g][:].rearrange("p (c r q) -> p q c r", r=LP // 2, q=2)[:, 0]
                        last = nc.vector.tensor_tensor(shifted[half][:, g], even, p, ALU.add)
                    last.then_inc(s[f"shift{half}"], 1)

            shift(0)
            dve.wait_ge(s["gate_turned"], 1)
            nc.vector.tensor_copy(N["gates"][:], ps["gate_ps"][:]).then_inc(s["gate_copied"], 1)
            for n in range(4):
                dve.wait_ge(s["vrow_turned"], n + 1)
                dst = (N["vs"], N["vw"])[n // 2]
                nc.vector.tensor_copy(dst[:, (n % 2) * 4:(n % 2) * 4 + 4, :], ps["vrow_ps"][:]).then_inc(s["vrow_copied"], 1)
            dve.wait_ge(s["kv_in"], 64)
            nc.vector.tensor_scalar(N["ksT"][0:NSA_D], kraw[0:NSA_D, 0], scale, None, ALU.mult)
            nc.vector.tensor_scalar(N["kwT"][0:NSA_D], kraw[0:NSA_D, 1], scale, None, ALU.mult)
            dve.wait_ge(s["tab_in"], 48)
            dve.wait_ge(s["hidden_done"], 1)
            shift(1)


def nsa_compressed(nc, mem, env, N, projT, selT, ins):
    ident = env["ident"]
    qc = [mem.at(f"cmpq{b}", 131 + 4 * b, [NSA_D, NSA_H, P]) for b in range(2)]
    slopeI = mem.at("cmp_slopeI", 139, [P, NSA_H, P], F32R)
    e = [mem.at(f"cmp_e{b}", 143 + 2 * b, [P, NSA_H, NC_PAD]) for b in range(2)]
    pT = [mem.at(f"cmp_pT{b}", 147 + 2 * b, [P, 4, P]) for b in range(2)]
    small = mem.at("cmp_small", 151, [P, 4, NSA_H])
    pg = mem.at("cmp_pg", 152, [P, NSA_G, NC_PAD + 4])
    imp = mem.at("cmp_imp", 153, [P, 4, NSA_G, N_BLK])
    above = mem.at("cmp_above", 154, [P, NSA_G, N_BLK, N_BLK])
    equal = mem.at("cmp_equal", 156, [P, NSA_G, N_BLK, N_BLK])
    before = mem.at("cmp_before", 158, [P, N_BLK, N_BLK])
    keep = mem.at("cmp_keep", 159, [P, NT, N_BLK])
    force = mem.at("cmp_force", 159.5, [P, NT, N_BLK])
    selrow = [mem.at(f"cmp_selrow{b}", 160 + b * 0.5, [NSA_G * N_BLK, P]) for b in range(2)]
    names = both("q_in scores_done exp_in exp_done p_done turned p_copied o_done bias_done bias_turned bias_copied bias_stored") \
        + "o_taken tab_in slope_done vector_step setup pool_step"
    banks = [(f"{n}{b}", [P, HALF], F32) for n in ("sc", "pt", "odd") for b in range(2)] + [("bt", [P, 2, P], F32)]
    K = 17
    with phase(nc, names, banks) as (block, s, ps):
        @block.gpsimd
        def _(pool):
            low, raw = slice(0, NSA_D), (N["ksT"], N["kwT"])
            rows = NSA_D + N_BLK
            steps = Steps(pool, s["pool_step"])
            for g in range(NSA_G):
                steps.link(nc.gpsimd.tensor_tensor(N["ks_blk"][0:rows, g], N["ksT"][0:rows, g], mem.one[0:rows].broadcast_to([rows, S]), ALU.mult))
                for j, both_parts in enumerate((N["ks_both"], N["kw_both"])):
                    steps.link(nc.gpsimd.tensor_tensor(both_parts[low, g], raw[j][low, g], mem.one[low].broadcast_to([NSA_D, S]), ALU.mult))
                    steps.link(nc.gpsimd.tensor_tensor(both_parts[NSA_D:P, g], raw[j][low, g], both_parts[low, g], ALU.subtract))

        @block.sync
        def _(sp):
            sp.dma_start(before[:], ins["k_before"]).then_inc(s["tab_in"], 16)
            sp.dma_start(keep[:], ins["k_keep"]).then_inc(s["tab_in"], 16)
            sp.dma_start(force[:], ins["k_force"]).then_inc(s["tab_in"], 16)

            def load(p, b):
                sp.wait_ge(s[f"scores_done{b}"], p)
                q = projT[NQ * P:(NQ + 4) * P, bass.ds((2 * p + b) * P, P)].rearrange("(h d) t -> d h t", d=NSA_D)
                sp.dma_start(qc[b][:], q).then_inc(s[f"q_in{b}"], 16)

            pairs(sp, NT, load)

        @block.tensor
        def _(pe):
            pe.wait_ge(s["slope_done"], 1)

            def scores(p, b):
                i = 2 * p + b
                pe.wait_ge(s[f"q_in{b}"], 16 * p + 16)
                pe.wait_ge(s[f"exp_in{b}"], p)
                for h in range(NSA_H):
                    out = ps[f"sc{b}"][:, h * NC_PAD:(h + 1) * NC_PAD]
                    nc.tensor.matmul(out, qc[b][:, h, :], N["kcT"][0:NSA_D, h // 4, :], start=True, stop=False)
                    last = nc.tensor.matmul(out, slopeI[:, h, :], N["dcmp"][:, bass.ds(i, 1), :].rearrange("p i c -> p (i c)"),
                                            start=False, stop=True)
                last.then_inc(s[f"scores_done{b}"], 1)

            def values(p, b):
                pe.wait_ge(s[f"p_done{b}"], p + 1)
                pe.wait_ge(s[f"p_copied{b}"], p)
                for k in range(4):
                    last = nc.tensor.transpose(ps[f"pt{b}"][:, k * P:(k + 1) * P], e[b][:, 2 * k:2 * k + 2, :].rearrange("p h c -> p (h c)"), ident[:])
                last.then_inc(s[f"turned{b}"], 1)
                pe.wait_ge(s[f"p_copied{b}"], p + 1)
                pe.wait_ge(s["o_taken"], 2 * p + b)
                for h in range(NSA_H):
                    rows = slice((h % 2) * NC_PAD, (h % 2 + 1) * NC_PAD)
                    last = nc.tensor.matmul(ps[f"odd{h % 2}"][:, h // 2 * NSA_D:(h // 2 + 1) * NSA_D], pT[b][rows, h // 2, :], N["vc"][rows, h // 4, :],
                                            start=True, stop=True)
                last.then_inc(s[f"o_done{b}"], 1)
                pe.wait_ge(s[f"bias_done{b}"], p + 1)
                for o in range(2):
                    pe.wait_ge(s[f"bias_copied{o}"], p + (b if o == 0 else 0))
                nc.tensor.transpose(ps["bt"][0:NSA_G * N_BLK, b, :], imp[:, 3].rearrange("p g j -> p (g j)"), ident[:]).then_inc(s[f"bias_turned{b}"], 1)

            def two_tiles(p):
                scores(p, 0)
                scores(p, 1)
                values(p, 0)
                values(p, 1)

            repeat(pe, NT // 2, two_tiles)

        @block.scalar
        def _(act):
            def body(p, b):
                act.wait_ge(s[f"exp_in{b}"], p + 1)
                nc.scalar.activation(e[b][:], e[b][:], ACT.Exp).then_inc(s[f"exp_done{b}"], 1)
                act.wait_ge(s[f"turned{b}"], p + 1)
                act.wait_ge(s[f"o_done{b}"], p)
                nc.scalar.activation(pT[b][:].rearrange("p k t -> p (k t)"), ps[f"pt{b}"][:], ACT.Copy).then_inc(s[f"p_copied{b}"], 1)
                act.wait_ge(s[f"bias_turned{b}"], p + 1)
                act.wait_ge(s[f"bias_stored{b}"], 16 * p)
                nc.scalar.activation(selrow[b][:], ps["bt"][0:NSA_G * N_BLK, b, :], ACT.Copy).then_inc(s[f"bias_copied{b}"], 1)
                act.wait_ge(s[f"bias_copied{b}"], p + 1)
                act.dma_start(selT[:, bass.ds((2 * p + b) * P, P)], selrow[b][:]).then_inc(s[f"bias_stored{b}"], 16)

            pairs(act, NT, body)
            for b in range(2):
                act.wait_ge(s[f"bias_stored{b}"], 16 * (NT // 2))

        @block.vector
        def _(dve):
            dve.wait_ge(s["tab_in"], 48)
            for h in range(NSA_H):
                last = nc.vector.tensor_scalar(slopeI[:, h, :], ident[:], N["slopes"][:, h:h + 1], None, ALU.mult)
            last.then_inc(s["slope_done"], 1)
            nc.vector.memset(pg[:], 0.0).then_inc(s["setup"], 1)
            dve.wait_ge(s["setup"], 1)
            wide = [P, NSA_H, NC_PAD]

            def body(p, b):
                i = 2 * p + b
                steps = Steps(dve, s["vector_step"], i * K)
                sc = ps[f"sc{b}"][:].rearrange("p (h c) -> p h c", c=NC_PAD)
                dve.wait_ge(s[f"scores_done{b}"], p + 1)
                steps.link(nc.vector.tensor_reduce(small[:, 0, :], sc, AX, ALU.max))
                dve.wait_ge(s[f"turned{b}"], p)
                nc.vector.tensor_tensor(e[b][:], sc, small[:, 0, :].unsqueeze(2).broadcast_to(wide), ALU.subtract).then_inc(s[f"exp_in{b}"], 1)
                dve.wait_ge(s[f"exp_done{b}"], p + 1)
                steps.link(nc.vector.tensor_reduce(small[:, 1, :], e[b][:, :, 0:N_CMP], AX, ALU.add))
                steps.link(nc.vector.reciprocal(small[:, 2, :], small[:, 1, :]))
                steps.link(nc.vector.tensor_tensor(e[b][:], e[b][:], small[:, 2, :].unsqueeze(2).broadcast_to(wide), ALU.mult))
                mask = N["cmask"][:, bass.ds(i, 1), :].broadcast_to(wide)
                nc.vector.tensor_tensor(e[b][:], e[b][:], mask, ALU.mult).then_inc(s[f"p_done{b}"], 1)
                dve.wait_ge(s[f"p_done{b}"], p + 1)
                for g in range(NSA_G):
                    steps.do(nc.vector.tensor_reduce(pg[:, g, 4:], e[b][:, 4 * g:4 * g + 4, :].rearrange("p r c -> p c r"), AX, ALU.add))
                steps.wait()
                steps.link(nc.vector.tensor_reduce(imp[:, 0], pg[:, :, 4:].rearrange("p g (j c) -> p g j c", c=4), AX, ALU.add))
                over = pg[:, :, 0:NC_PAD].rearrange("p g (j c) -> p g j c", c=4)[:, :, :, 3]
                steps.link(nc.vector.tensor_tensor(imp[:, 0], imp[:, 0], over, ALU.add))
                per = [P, NSA_G, N_BLK]
                steps.link(nc.vector.tensor_tensor(imp[:, 1], imp[:, 0], keep[:, bass.ds(i, 1), :].broadcast_to(per), ALU.mult))
                steps.link(nc.vector.tensor_tensor(imp[:, 1], imp[:, 1], force[:, bass.ds(i, 1), :].broadcast_to(per), ALU.add))
                for g in range(NSA_G):
                    other = imp[:, 1, g].unsqueeze(1).broadcast_to([P, N_BLK, N_BLK])
                    own = imp[:, 1, g].unsqueeze(2).broadcast_to([P, N_BLK, N_BLK])
                    steps.do(nc.vector.tensor_tensor(above[:, g], other, own, ALU.is_gt))
                    steps.do(nc.vector.tensor_tensor(equal[:, g], other, own, ALU.is_equal))
                steps.wait()
                for g in range(NSA_G):
                    last = nc.vector.tensor_tensor(equal[:, g], equal[:, g], before[:], ALU.mult)
                steps.link(last)
                steps.link(nc.vector.tensor_tensor(above[:], above[:], equal[:], ALU.add))
                steps.link(nc.vector.tensor_reduce(imp[:, 2], above[:], AX, ALU.add))
                for o in range(2):
                    dve.wait_ge(s[f"bias_turned{o}"], p + (b if o == 0 else 0))
                nc.vector.tensor_scalar(imp[:, 3], imp[:, 2], float(SEL_K), NEG, ALU.is_ge, ALU.mult).then_inc(s[f"bias_done{b}"], 1)
                assert steps.n == K, steps.n
                dve.wait_ge(s[f"o_done{b}"], p + 1)
                gates = N["gates"][:, bass.ds(i, 1), 0:NSA_H].rearrange("p i (h o) -> p (i h) o", o=2)
                o = N["o"][:, bass.ds(i, 1), :].rearrange("p i (h o d) -> p (i h) o d", o=2, d=NSA_D)
                for odd in range(2):
                    last = nc.vector.tensor_tensor(o[:, :, odd, :], ps[f"odd{odd}"][:, 0:4 * NSA_D].rearrange("p (h d) -> p h d", d=NSA_D),
                                                   gates[:, :, odd:odd + 1].broadcast_to([P, 4, NSA_D]), ALU.mult)
                last.then_inc(s["o_taken"], 1)

            pairs(dve, NT, body)


def nsa_attend(nc, mem, env, N, projT, selT, ins):
    ident, hi, lo = env["ident"], env["hi"], env["lo"]
    diag = [mem.at(f"att_diag{r}", 158 + 0.5 * r, [P, P]) for r in range(2)]
    qh = [mem.at(f"att_q{b}", 131 + 4 * b, [P, S]) for b in range(2)]
    q_high = [mem.at(f"att_q_high{b}", 188 + 4 * b, [P, S], F32R) for b in range(2)]
    q_low = [mem.at(f"att_q_low{b}", 196 + 4 * b, [P, S], F32R) for b in range(2)]
    slopeI = [mem.at(f"att_slopeI{b}", 139 + 0.5 * b, [P, P], F32R) for b in range(2)]
    prob = [mem.at("att_prob0", 140, [P, S]), mem.at("att_prob1", 144, [P, S])]
    probT = [mem.at("att_probT0", 148, [P, NT, P]), mem.at("att_probT1", 152, [P, NT, P])]
    small = [mem.at(f"att_small{r}", 156 + r, [P, 4]) for r in range(2)]
    names = both("q_in q_split head_scored slope_done scores_done max_done exp_done grouped group_copied diag_done o_done o_read") + "vector_step pool_step"
    banks = [(f"sc{r}", [P, S], F32) for r in range(2)] + [(f"{n}{r}", [P, HALF], F32) for n in ("pt", "ob") for r in range(2)]
    JOBS = [(i, r) for i in range(NT) for r in range(2)]
    first = lambda i, r: 0 if r == 0 else max(0, i - WINDOW // P)
    tiles = lambda i, r: i + 1 - first(i, r)
    GROUPS, before = [], []
    for j, (i, r) in enumerate(JOBS):
        before.append(len(GROUPS))
        for g in range(-(-tiles(i, r) // 4)):
            GROUPS.append((j, 4 * g, min(4, tiles(i, r) - 4 * g)))
    NG = len(GROUPS)
    assert NG % 2 == 0
    with phase(nc, names, banks) as (block, s, ps):
        def heads(eng, body):
            for h in range(NSA_H):
                body(*divmod(h, 2))

        def use(p, b, j):
            return 2 * NT * p + NT * b + j // 2

        def scored(p, b, j):
            if j == len(JOBS) - 1:
                return s[f"head_scored{b}"], p + 1
            if j % 2:
                return s["scores_done1"], 2 * (NT - 1) * p + (NT - 1) * b + j // 2 + 1
            return s["scores_done0"], use(p, b, j) + 1

        def group_use(p, b, n):
            return NG * p + (NG // 2) * b + n // 2

        @block.sync
        def _(sp):
            def load(p, b):
                h = 2 * p + b
                sp.wait_ge(s[f"q_split{b}"], p)
                sp.dma_start(qh[b][0:NSA_D], projT[bass.ds(h * NSA_D + NQ * P, NSA_D), :]).then_inc(s[f"q_in{b}"], 16)
                sp.dma_start(qh[b][NSA_D:NSA_D + N_BLK], selT[bass.ds(p // 2 * N_BLK, N_BLK), :]).then_inc(s[f"q_in{b}"], 16)

            heads(sp, load)

        @block.gpsimd
        def _(pool):
            steps = Steps(pool, s["pool_step"])

            def split(p, b):
                if 2 * p + b > 0:
                    pool.wait_ge(s[f"q_split{1 - b}"], p + b)
                pool.wait_ge(s[f"q_in{b}"], 32 * p + 32)
                pool.wait_ge(s[f"head_scored{b}"], p)
                low, blk = slice(0, NSA_D), slice(NSA_D, NSA_D + N_BLK)
                for half in (slice(0, NSA_D), slice(NSA_D, P)):
                    steps.link(nc.gpsimd.tensor_tensor(q_high[b][half], qh[b][low], mem.one[low].broadcast_to([NSA_D, S]), ALU.mult))
                steps.link(nc.gpsimd.tensor_tensor(q_low[b][blk], qh[b][blk], mem.one[blk].broadcast_to([N_BLK, S]), ALU.mult))
                nc.gpsimd.tensor_tensor(q_low[b][low], qh[b][low], q_high[b][low], ALU.subtract).then_inc(s[f"q_split{b}"], 1)

            heads(pool, split)

        @block.tensor
        def _(pe):
            def scores(p, b, j):
                i, r = JOBS[j]
                m = use(p, b, j)
                if j == 0:
                    pe.wait_ge(s[f"q_split{b}"], p + 1)
                    pe.wait_ge(s[f"slope_done{b}"], p + 1)
                pe.wait_ge(s[f"exp_done{r}"], m)
                n = tiles(i, r) * P
                rows = NSA_D + N_BLK if r == 0 else NSA_D
                both_parts, high = (N["ks_both"], N["ks_blk"]) if r == 0 else (N["kw_both"], N["kw_both"])
                table = N["dist"] if r == 0 else N["dwin"]
                off = (NT - 1 - i) * P if r == 0 else WINDOW + P - n
                for c in range(0, n, HALF):
                    w = min(HALF, n - c)
                    out = ps[f"sc{r}"][:, c:c + w]
                    k = slice(first(i, r) * P + c, first(i, r) * P + c + w)
                    nc.tensor.matmul(out, slopeI[b][:], table[:, off + c:off + c + w], start=True, stop=False)
                    nc.tensor.matmul(out, q_high[b][:, i * P:(i + 1) * P], both_parts[:, p // 2, k], start=False, stop=False)
                    last = nc.tensor.matmul(out, q_low[b][0:rows, i * P:(i + 1) * P], high[0:rows, p // 2, k], start=False, stop=True)
                last.then_inc(scored(p, b, j)[0], 1)

            def turns(p, b, j):
                i, r = JOBS[j]
                pe.wait_ge(s[f"diag_done{r}"], use(p, b, j) + 1)
                for n in range(before[j], NG if j + 1 == len(JOBS) else before[j + 1]):
                    _, t0, nt = GROUPS[n]
                    pe.wait_ge(s[f"group_copied{n % 2}"], group_use(p, b, n))
                    for t in range(nt):
                        last = nc.tensor.matmul(ps[f"pt{n % 2}"][:, t * P:(t + 1) * P], prob[r][:, (t0 + t) * P:(t0 + t + 1) * P], diag[r][:],
                                                start=True, stop=True)
                    last.then_inc(s[f"grouped{n % 2}"], 1)

            def values(p, b, j):
                i, r = JOBS[j]
                for n in range(before[j], NG if j + 1 == len(JOBS) else before[j + 1]):
                    pe.wait_ge(s[f"group_copied{n % 2}"], group_use(p, b, n) + 1)
                h, out = 2 * p + b, ps[f"ob{i % 2}"][b * NSA_D:(b + 1) * NSA_D, 0:P]
                if r == 0:
                    pe.wait_ge(s[f"o_read{i % 2}"], h * (NT // 2) + i // 2)
                    nc.tensor.matmul(out, N["o"][:, i, h * NSA_D:(h + 1) * NSA_D], ident[:], start=True, stop=False)
                v = N["vs"] if r == 0 else N["vw"]
                cols = slice(p // 2 * NSA_D, (p // 2 + 1) * NSA_D)
                for t in range(tiles(i, r)):
                    last = nc.tensor.matmul(out, v[:, first(i, r) + t, cols], probT[r][:, t, :],
                                            start=False, stop=(r == 1 and t == tiles(i, r) - 1))
                last.then_inc(s[f"o_done{r}"], 1)

            def head(p, b):
                scores(p, b, 0)
                for j in range(len(JOBS)):
                    if j + 1 < len(JOBS):
                        scores(p, b, j + 1)
                    turns(p, b, j)
                    if j > 0:
                        values(p, b, j - 1)
                values(p, b, len(JOBS) - 1)

            heads(pe, head)

        def copy_group(eng, p, b, n, op):
            j, t0, nt = GROUPS[n]
            i, r = JOBS[j]
            eng.wait_ge(s[f"grouped{n % 2}"], group_use(p, b, n) + 1)
            if j >= 2:
                eng.wait_ge(s[f"o_done{r}"], use(p, b, j))
            dst = probT[r][:, t0:t0 + nt, :].rearrange("p t c -> p (t c)")
            op(dst, ps[f"pt{n % 2}"][:, 0:nt * P]).then_inc(s[f"group_copied{n % 2}"], 1)

        def groups_of(j, parity):
            return [n for n in range(NG) if GROUPS[n][0] == j and n % 2 == parity]

        @block.scalar
        def _(act):
            def exps(p, b, j):
                i, r = JOBS[j]
                act.wait_ge(s[f"max_done{r}"], use(p, b, j) + 1)
                if j >= 2:
                    n = before[j - 1] - 1
                    act.wait_ge(s[f"grouped{n % 2}"], group_use(p, b, n) + 1)
                else:
                    for parity in range(2):
                        act.wait_ge(s[f"grouped{parity}"], group_use(p, b, 0))
                n = tiles(i, r) * P
                nc.scalar.activation(prob[r][:, 0:n], ps[f"sc{r}"][:, 0:n], ACT.Exp, bias=small[r][:, 0:1],
                                     accum_out=small[r][:, 1:2]).then_inc(s[f"exp_done{r}"], 1)

            def head(p, b):
                exps(p, b, 0)
                for j in range(len(JOBS)):
                    if j + 1 < len(JOBS):
                        exps(p, b, j + 1)
                    for n in groups_of(j, 0):
                        copy_group(act, p, b, n, lambda o, x: nc.scalar.activation(o, x, ACT.Copy))

            heads(act, head)

        @block.vector
        def _(dve):
            def maxima(p, b, j):
                i, r = JOBS[j]
                m = use(p, b, j)
                dve.wait_ge(*scored(p, b, j))
                dve.wait_ge(s[f"exp_done{r}"], m)
                nc.vector.tensor_reduce(small[r][:, 0:1], ps[f"sc{r}"][:, 0:tiles(i, r) * P], AX, ALU.max, negate=True).then_inc(s[f"max_done{r}"], 1)

            steps = Steps(dve, s["vector_step"])

            def weight(p, b, j):
                i, r = JOBS[j]
                dve.wait_ge(s[f"exp_done{r}"], use(p, b, j) + 1)
                steps.link(nc.vector.reciprocal(small[r][:, 2:3], small[r][:, 1:2]))
                gate = (1 + r) * NSA_H + 2 * p + b
                steps.link(nc.vector.tensor_tensor(small[r][:, 3:4], small[r][:, 2:3], N["gates"][:, i, gate:gate + 1], ALU.mult))
                nc.vector.tensor_scalar(diag[r][:], ident[:], small[r][:, 3:4], None, ALU.mult).then_inc(s[f"diag_done{r}"], 1)

            def output(p, b, j):
                i, r = JOBS[j]
                if r == 0:
                    return
                dve.wait_ge(s["o_done1"], use(p, b, j) + 1)
                rows, c = slice(b * NSA_D, (b + 1) * NSA_D), slice(i * P, (i + 1) * P)
                out = ps[f"ob{i % 2}"][rows, 0:P]
                steps.link(nc.vector.tensor_copy(hi[rows, p, c], out))
                nc.vector.tensor_tensor(lo[rows, p, c], out, hi[rows, p, c], ALU.subtract).then_inc(s[f"o_read{i % 2}"], 1)

            def head(p, b):
                nc.vector.tensor_scalar(slopeI[b][:], ident[:], N["slopes"][:, bass.ds(2 * p + b, 1)], None, ALU.mult).then_inc(s[f"slope_done{b}"], 1)
                maxima(p, b, 0)
                for j in range(len(JOBS)):
                    weight(p, b, j)
                    if j + 1 < len(JOBS):
                        maxima(p, b, j + 1)
                    for n in groups_of(j, 1):
                        copy_group(dve, p, b, n, lambda o, x: nc.vector.tensor_copy(o, x))
                    if j > 0:
                        output(p, b, j - 1)
                output(p, b, len(JOBS) - 1)

            heads(dve, head)



def gated_epilogue(nc, mem, name, gate, store=None, other=None, split=None):
    gbuf = [mem.at(f"{name}_gate{b}", 192 + 4 * b, [P, S]) for b in range(2)]
    if store is None:
        mbuf = mem.at(f"{name}_other", 200, [P, S])
    st = [mem.at(f"{name}_stage{b}", (128 if store is not None else 92) + 4 * b, [P, S]) for b in range(2)]
    halves = lambda x: x.rearrange("p (h t) -> p h t", h=NH)

    def epilogue(block, s, acc, ps):
        @block.scalar
        def _(act):
            def body(p, b):
                u = 2 * p + b
                act.wait_ge(s[f"acc_read{b}"], p)
                act.dma_start(gbuf[b][:], gate[bass.ds(u * P, P), :]).then_inc(s[f"loaded{b}"], 16)
                act.wait_ge(s[f"loaded{b}"], 16 * p + 16)
                nc.scalar.activation(gbuf[b][:], gbuf[b][:], ACT.Sigmoid).then_inc(s[f"epilogue_a{b}"], 1)
                if store is not None:
                    act.wait_ge(s[f"acc_read{b}"], p + 1)
                    act.dma_start(store[bass.ds(u * P, P), :], st[b][:]).then_inc(s[f"stored{b}"], 16)
                else:
                    act.wait_ge(s["merged"], u)
                    act.dma_start(mbuf[:], other[bass.ds(u * P, P), :]).then_inc(s[f"stored{b}"], 16)

            pairs(act, KD, body)
            for b in range(2):
                act.wait_ge(s[f"stored{b}"], 16 * (KD // 2))

        @block.vector
        def _(dve):
            def body(p, b):
                u = 2 * p + b
                dve.wait_ge(s[f"products_done{b}"], p + 1)
                if store is not None:
                    dve.wait_ge(s[f"stored{b}"], 16 * p)
                dve.wait_ge(s[f"epilogue_a{b}"], p + 1)
                nc.vector.tensor_tensor(halves(st[b][:]), acc[b][:], halves(gbuf[b][:]), ALU.mult).then_inc(s[f"acc_read{b}"], 1)
                if store is None:
                    m_hi, m_lo = split
                    tile = lambda x: x[:, bass.ds(u, 1), :].rearrange("p k t -> p (k t)")
                    dve.wait_ge(s[f"acc_read{b}"], p + 1)
                    dve.wait_ge(s[f"stored{b}"], 16 * p + 16)
                    nc.vector.tensor_tensor(st[b][:], st[b][:], mbuf[:], ALU.add).then_inc(s["merged"], 1)
                    dve.wait_ge(s["merged"], u + 1)
                    nc.vector.tensor_scalar(tile(m_hi), st[b][:], 1.0, None, ALU.mult).then_inc(s[f"epilogue_b{b}"], 1)
                    dve.wait_ge(s[f"epilogue_b{b}"], p + 1)
                    nc.vector.tensor_tensor(tile(m_lo), st[b][:], tile(m_hi), ALU.subtract).then_inc(s["vector_step"], 1)
                    dve.wait_ge(s["vector_step"], u + 1)

            pairs(dve, KD, body)

    return epilogue


def shift_epilogue(nc, mem, env, name, at, n_units, dst, mu):
    prm = env["prm"]
    st = [mem.at(f"{name}_stage{b}", at + 4 * b, [P, S]) for b in range(2)]
    df = [mem.at(f"{name}_diff{b}", at + 8 + 4 * b, [P, S]) for b in range(2)]

    def epilogue(block, s, acc, ps):
        @block.scalar
        def _(act):
            def body(p, b):
                act.wait_ge(s[f"products_done{b}"], p + 1)
                act.wait_ge(s[f"epilogue_b{b}"], p)
                nc.scalar.activation(st[b][:].rearrange("p (h t) -> p h t", h=NH), acc[b][:], ACT.Copy).then_inc(s[f"acc_read{b}"], 1)
                act.wait_ge(s[f"epilogue_b{b}"], p + 1)
                act.dma_start(dst[bass.ds((2 * p + b) * P, P), :], df[b][:]).then_inc(s[f"stored{b}"], 16)

            pairs(act, n_units, body)
            act.wait_ge(s["stored0"], 16 * ((n_units + 1) // 2))
            act.wait_ge(s["stored1"], 16 * (n_units // 2))

        @block.vector
        def _(dve):
            def body(p, b):
                u = 2 * p + b
                steps = Steps(dve, s["vector_step"], u * 2)
                dve.wait_ge(s[f"stored{b}"], 16 * p)
                dve.wait_ge(s[f"acc_read{b}"], p + 1)
                steps.do(nc.vector.tensor_scalar(df[b][:, 0:1], st[b][:, 0:1], -1.0, None, ALU.mult))
                steps.do(nc.vector.tensor_tensor(df[b][:, 1:S], st[b][:, 0:S - 1], st[b][:, 1:S], ALU.subtract))
                steps.wait()
                nc.vector.scalar_tensor_tensor(out=df[b][:], in0=df[b][:], scalar=prm[:, bass.ds(u + mu, 1)], in1=st[b][:],
                                               op0=ALU.mult, op1=ALU.add).then_inc(s[f"epilogue_b{b}"], 1)

            pairs(dve, n_units, body)

    return epilogue


def norm_and_modulation(nc, mem, env, ins, gain):
    prm, xT = env["prm"], env["xT"]
    W, NB = 4 * P, 6
    raw = [mem.at(f"ada_raw{b}", 104 + 16 * b, [P, KD, W]) for b in range(NB)]
    c_act = mem.at("ada_c", 204, [P, KD])
    part = [mem.at(f"ada_part{b}", 200 + 2 * b, [P, W]) for b in range(2)]
    w = ins["w_ada_2"].rearrange("a (k p) n -> (a p) k n", p=P)
    n = 6 * D // W
    names = " ".join(f"w_in{b}" for b in range(NB)) + " " + both("part_done done read") + "c_done vector_step " + RMS_SEMS
    with phase(nc, names, [(f"ada{b}", [P, W // P], F32) for b in range(2)] + [("tot", [P, NH, HALF], F32)]) as (block, s, ps):
        def tails(rstd, mid):
            def dve_tail(dve):
                for k in range(KD):
                    nc.vector.scalar_tensor_tensor(out=xT[:, k, :], in0=xT[:, k, :], scalar=prm[:, gain + k:gain + k + 1],
                                                   in1=rstd[:], op0=ALU.mult, op1=ALU.mult)

            return None, dve_tail, None

        rms_programs(nc, mem, env, block, s, ps["tot"], "norm_final", 40, tails)

        @block.sync
        def _(sp):
            for u in range(n):
                if u >= NB:
                    sp.wait_ge(s[f"part_done{u % 2}"], (u - NB) // 2 + 1)
                sp.dma_start(raw[u % NB][:], w[:, :, u * W:(u + 1) * W]).then_inc(s[f"w_in{u % NB}"], 16)

        @block.scalar
        def _(act):
            nc.scalar.activation(c_act[:], prm[:, PRM["c_2"]:PRM["c_2"] + KD], ACT.Silu).then_inc(s["c_done"], 1)

        @block.tensor
        def _(pe):
            for u in range(n):
                b = u % 2
                pe.wait_ge(s[f"part_done{b}"], u // 2 + 1)
                if u >= 2:
                    pe.wait_ge(s[f"read{b}"], u // 2)
                for j in range(W // P):
                    last = nc.tensor.matmul(ps[f"ada{b}"][:, j:j + 1], part[b][:, j * P:(j + 1) * P], env["ones"][:, 0:1], start=True, stop=True)
                last.then_inc(s[f"done{b}"], 1)

        @block.vector
        def _(dve):
            st = Steps(dve, s["vector_step"])
            dve.wait_ge(s["c_done"], 1)

            def add_bias(u):
                b, j = u % 2, W // P
                dve.wait_ge(s[f"done{b}"], u // 2 + 1)
                nc.vector.tensor_tensor(prm[:, ADA + u * j:ADA + (u + 1) * j], ps[f"ada{b}"][:],
                                        prm[:, PRM["b_ada_2"] + u * j:PRM["b_ada_2"] + (u + 1) * j], ALU.add).then_inc(s[f"read{b}"], 1)

            for u in range(n):
                b, w_in = u % 2, raw[u % NB]
                dve.wait_ge(s[f"w_in{u % NB}"], 16 * (u // NB) + 16)
                if u >= 2:
                    dve.wait_ge(s[f"done{b}"], u // 2)
                for k in range(KD):
                    c = c_act[:, k:k + 1]
                    if k == 0:
                        last = nc.vector.tensor_scalar(part[b][:], w_in[:, k, :], c, None, ALU.mult)
                    else:
                        last = nc.vector.scalar_tensor_tensor(out=part[b][:], in0=w_in[:, k, :], scalar=c, in1=part[b][:], op0=ALU.mult, op1=ALU.add)
                    if k < KD - 1:
                        st.link(last)
                last.then_inc(s[f"part_done{b}"], 1)
                if u > 0:
                    add_bias(u - 1)
            add_bias(n - 1)
            for b in range(2):
                dve.wait_ge(s[f"read{b}"], n // 2)
            for group in (1, 4):
                c = prm[:, ADA + group * KD:ADA + (group + 1) * KD]
                nc.vector.tensor_scalar(c, c, 1.0, None, ALU.add)


L = 64
RWKV_TILES = 4
VSTEPS = 135
DECAY = float(np.exp(-0.5))


def rwkv(nc, mem, env, zT, ins):
    prm, ident, hi, lo = env["prm"], env["ident"], env["hi"], env["lo"]
    at = iter(range(104, 208, 4))
    big = lambda name: mem.at(f"rw_{name}", next(at), [P, S])
    r, k, v, lw, cs, a, kk, e1, e2, e3, bb, kb, gate, y, rh = map(big, "r k v lw cs a kk e1 e2 e3 bb kb g y rh".split())
    chunk_mask, lora = map(big, "mask lora".split())
    glo = mem.at("rw_glo", 36, [P, S])
    base = next(at)
    GT = mem.at("rw_GT", base + 4, [P, 16, P])
    H = mem.at("rw_H", base + 12, [P, 16, L])
    ST = mem.at("rw_ST", base + 16, [P, 16, L])
    two_of = lambda name, a, b: [mem.at(f"rw_{name}{g}", x, [P, 4, P]) for g, x in enumerate((a, b))]
    e_at, cs_at = 104 + 4 * 7, 104 + 4 * 4
    X0 = two_of("X0_", base + 20, cs_at)
    XA = two_of("XA_", base + 22, cs_at + 2)
    Q = two_of("Q_", base + 24, e_at)
    QT = two_of("QT_", base + 26, e_at + 2)
    Pm = two_of("P_", base + 28, e_at + 4)
    nat = [[mem.at(f"rw_nat{g}{j}", (base, e_at + 6)[g] + 2 * j, [P, 4, P]) for j in range(2)] for g in range(2)]
    Mab, Mak, Mrb, Mrk = (two_of(f"M{n}_", 56 + 2 * i, 88 + 2 * i) for i, n in enumerate(("ab", "ak", "rb", "rk")))
    masks = mem.at("rw_masks", 64, [P, 8, P])
    w2t = mem.at("rw_w2t", 68, [P, P])
    g2t = mem.at("rw_g2t", 68.5, [P, P])
    blockones = mem.at("rw_blockones", 69, [P, P])
    eye2 = mem.at("rw_eye2", 69.5, [P, L])
    cols = mem.at("rw_cols", 70, [P, 16])
    wend = mem.at("rw_wend", 70.5, [P, 16])
    t1 = mem.at("rw_t1", 88, [P, S])
    t2 = mem.at("rw_t2", 92, [P, S])
    t3 = mem.at("rw_t3", 96, [P, S])
    t4 = mem.at("rw_t4", 100, [P, S])
    LEVELS = (2, 4, 8, 16, 32)

    names = ("setup z_in const_in lora_done glo_done turn_done cols_done cols2 "
             "lora_w_mm lora_w_read lora_a_mm lora_a_read lora_g_mm lora_g_read lw_sig a_sig scanned "
             "kk_sq kk_mm kk_root kk_done exp1 exp2 exp3 exp4 prep vector_step bonus_mm bonus_read rtk "
             "nat_turned nat_copied m_done m1_read m2_read q1_turned q1_copied p_mm p_read qq_mm qq_read "
             "x_mm x_read xa_mm xa_read rn_mm rn_read gh_mm gh_read g_fin h_fin s_mm s_done y_mm y_read "
             "mean_mm mean_read var_sq var_mm var_read var_root out_pre high low act_step")
    banks = [("A", [P, NH, HALF], F32), ("B", [P, NH, HALF], F32), ("C", [P, NH, HALF], F32), ("D", [P, NH, HALF], F32)]
    with phase(nc, names, banks) as (block, s, ps):
        A, B, C, Dd = ps["A"], ps["B"], ps["C"], ps["D"]
        two = lambda x: x[:].rearrange("p (h t) -> p h t", h=NH)

        per = dict(z_in=96, lora_w_mm=1, lora_a_mm=1, lora_g_mm=1, lora_w_read=1, lora_a_read=1, lora_g_read=1,
                   scanned=1, kk_sq=1, kk_mm=1, kk_root=1, kk_done=1, exp1=1, exp2=1, exp3=1, exp4=1, prep=1, rtk=1,
                   bonus_mm=1, bonus_read=1, nat_turned=8, nat_copied=8, m_done=8, m1_read=4, m2_read=4, q1_turned=4,
                   q1_copied=4, p_mm=20, p_read=20, qq_mm=20, qq_read=20, x_mm=4, x_read=4, xa_mm=4, xa_read=4, rn_mm=4,
                   rn_read=4, gh_mm=4, gh_read=4, s_mm=16, s_done=16, y_mm=1, y_read=1, mean_mm=1, mean_read=1,
                   var_sq=1, var_mm=1, var_read=1, var_root=1, out_pre=1, high=1, low=1, cols_done=1, cols2=1, turn_done=1)

        def turns(eng, body):
            with eng.Fori(0, RWKV_TILES) as f:
                def wait(name, n):
                    eng.wait_ge(s[name], f * per[name] + n)
                body(f, wait)

        @block.sync
        def _(sp):
            sp.dma_start(lora[:], zT[ZLO * P:(ZLO + 1) * P, :]).then_inc(s["const_in"], 16)
            sp.dma_start(glo[:], zT[ZG * P:(ZG + 1) * P, :]).then_inc(s["const_in"], 16)
            sp.dma_start(chunk_mask[:], ins["k_chunk"]).then_inc(s["const_in"], 16)
            sp.dma_start(masks[:], ins["k_masks"]).then_inc(s["const_in"], 16)
            sp.dma_start(blockones[:], ins["k_blockones"]).then_inc(s["const_in"], 16)
            sp.dma_start(eye2[:], ins["k_eye2"]).then_inc(s["const_in"], 16)

            def body(f):
                for dst, t in ((r, ZR), (k, ZK), (v, ZV)):
                    sp.dma_start(dst[:], zT[bass.ds((f + t) * P, P), :]).then_inc(s["z_in"], 16)
                c = bass.ds(f * P, P)
                sp.dma_start(w2t[0:64, :], ins["rw_w2_2"].rearrange("a k n -> (a k) n")[:, c]).then_inc(s["z_in"], 16)
                sp.dma_start(w2t[64:128, :], ins["rw_a2_2"].rearrange("a k n -> (a k) n")[:, c]).then_inc(s["z_in"], 16)
                sp.dma_start(g2t[:], ins["rw_g2_2"].rearrange("a k n -> (a k) n")[:, c]).then_inc(s["z_in"], 16)

            body(0)
            with sp.Fori(1, RWKV_TILES) as f:
                sp.wait_ge(s["rn_read"], f * per["rn_read"])
                body(f)

        @block.scalar
        def _(act):
            act.wait_ge(s["const_in"], 96)
            nc.scalar.activation(lora[0:64, :], lora[0:64, :], ACT.Tanh).then_inc(s["lora_done"], 1)
            nc.scalar.activation(glo[:], glo[:], ACT.Sigmoid).then_inc(s["lora_done"], 1)

            def body(f, wait):
                wait("cols_done", 1)
                wait("lora_w_mm", 1)
                nc.scalar.activation(two(lw), A[:], ACT.Sigmoid, bias=cols[:, 0:1]).then_inc(s["lora_w_read"], 1)
                wait("lora_a_mm", 1)
                nc.scalar.activation(two(a), B[:], ACT.Sigmoid, bias=cols[:, 1:2]).then_inc(s["lora_a_read"], 1)
                wait("lora_g_mm", 1)
                nc.scalar.activation(two(gate), C[:], ACT.Copy).then_inc(s["lora_g_read"], 1)
                wait("kk_mm", 1)
                nc.scalar.activation(two(t1), Dd[:], ACT.Sqrt).then_inc(s["kk_root"], 1)
                wait("scanned", 1)
                nc.scalar.activation(e1[:], cs[:], ACT.Exp).then_inc(s["exp1"], 1)
                nc.scalar.activation(e2[:], cs[:], ACT.Exp, scale=-1.0).then_inc(s["exp2"], 1)
                nc.scalar.activation(t2[:], t2[:], ACT.Exp).then_inc(s["exp3"], 1)
                nc.scalar.activation(e3[:], e3[:], ACT.Exp).then_inc(s["exp4"], 1)
                for n2 in range(2):
                    for g in range(2):
                        for j in range(2):
                            wait("nat_turned", 4 * n2 + 2 * g + j + 1)
                            nc.scalar.activation(nat[g][j][:].rearrange("p i c -> p (i c)"), C[:, j, :], ACT.Copy).then_inc(s["nat_copied"], 1)
                    for g in range(2):
                        wait("q1_turned", 2 * n2 + g + 1)
                        nc.scalar.activation(Q[g][:].rearrange("p x c -> p (x c)"), (C, Dd)[g][:, 0, :], ACT.Copy).then_inc(s["q1_copied"], 1)
                    for g in range(2):
                        wait("x_mm", 2 * n2 + g + 1)
                        for x in range(4):
                            j, h = divmod(x, 2)
                            ao, no = (0, L) if h == 0 else (L, 0)
                            nc.scalar.activation(X0[g][:, x, ao:ao + L], nat[g][j][:, 0, h * L:(h + 1) * L], ACT.Copy)
                            last = nc.scalar.activation(X0[g][:, x, no:no + L], (Dd, C)[g][:, 0, x * L:(x + 1) * L], ACT.Copy)
                        last.then_inc(s["x_read"], 1)
                    for g in range(2):
                        wait("xa_mm", 2 * n2 + g + 1)
                        nc.scalar.activation(XA[g][:].rearrange("p x c -> p (x c)"), (Dd, C)[g][:, 1, :], ACT.Copy).then_inc(s["xa_read"], 1)
                wait("var_mm", 1)
                nc.scalar.activation(two(t1), B[:], ACT.Sqrt, bias=cols[:, 9:10], scale=1.0 / L).then_inc(s["var_root"], 1)

            turns(act, body)

        @block.tensor
        def _(pe):
            pe.wait_ge(s["lora_done"], 2)

            def body(f, wait):
                wait("z_in", 96)
                for t in range(NH):
                    c = slice(t * HALF, (t + 1) * HALF)
                    last = nc.tensor.matmul(A[:, t, :], w2t[0:64, :], lora[0:64, c], start=True, stop=True)
                last.then_inc(s["lora_w_mm"], 1)
                for t in range(NH):
                    c = slice(t * HALF, (t + 1) * HALF)
                    last = nc.tensor.matmul(B[:, t, :], w2t[64:128, :], lora[64:128, c], start=True, stop=True)
                last.then_inc(s["lora_a_mm"], 1)
                for t in range(NH):
                    c = slice(t * HALF, (t + 1) * HALF)
                    last = nc.tensor.matmul(C[:, t, :], g2t[:], glo[:, c], start=True, stop=True)
                last.then_inc(s["lora_g_mm"], 1)
                wait("kk_sq", 1)
                for t in range(NH):
                    c = slice(t * HALF, (t + 1) * HALF)
                    last = nc.tensor.matmul(Dd[:, t, :], blockones[:], t1[:, c], start=True, stop=True)
                last.then_inc(s["kk_mm"], 1)
                wait("rtk", 1)
                wait("lora_w_read", 1)
                for t in range(NH):
                    c = slice(t * HALF, (t + 1) * HALF)
                    last = nc.tensor.matmul(A[:, t, :], blockones[:], t3[:, c], start=True, stop=True)
                last.then_inc(s["bonus_mm"], 1)
                wait("prep", 1)
                wait("lora_g_read", 1)
                wait("lora_a_read", 1)
                wait("kk_root", 1)
                wait("bonus_read", 1)
                for n2 in range(2):
                    for g in range(2):
                        n = 2 * n2 + g
                        for j in range(2):
                            if g == 0 and n2 > 0 and j == 0:
                                wait("xa_read", 2 * n2)
                                wait("qq_read", 10 * n2)
                            if g == 1:
                                wait("nat_copied", 4 * n2 + 1 + j)
                            c = slice((2 * n + j) * P, (2 * n + j + 1) * P)
                            for i, x in enumerate((kk, bb, kb, v)):
                                last = nc.tensor.transpose(C[:, j, i * P:(i + 1) * P], x[:, c], ident[:])
                            last.then_inc(s["nat_turned"], 1)
                        for m, (left, right) in enumerate(((a, kk), (lw, kk), (a, r), (lw, r))):
                            if m == 0 and g == 1:
                                wait("m1_read", n)
                            if m == 0 and g == 0 and n2 > 0:
                                wait("gh_read", n)
                            if m == 2 and g == 1:
                                wait("m2_read", n)
                            if m == 2 and g == 0 and n2 > 0:
                                wait("rn_read", n)
                            bank = A if m < 2 else B
                            for j in range(2):
                                c = slice((2 * n + j) * P, (2 * n + j + 1) * P)
                                for h in range(2):
                                    rows = slice(h * L, (h + 1) * L)
                                    col = ((m % 2) * 2 + j) * P
                                    last = nc.tensor.matmul(bank[:, h, col:col + P], left[rows, c], right[rows, c], start=True, stop=True)
                            if m % 2:
                                last.then_inc(s["m_done"], 1)
                    wait("nat_copied", 4 * n2 + 4)
                    for g in range(2):
                        wait("m1_read", 2 * n2 + g + 1)
                        for x in range(4):
                            last = nc.tensor.transpose((C, Dd)[g][:, 0, x * P:(x + 1) * P], QT[g][:, x, :], ident[:])
                        last.then_inc(s["q1_turned"], 1)
                    wait("m2_read", 2 * n2 + 2)
                    for i in range(len(LEVELS)):
                        for g in range(2):
                            lv = 10 * n2 + 2 * i + g
                            if i == 0:
                                wait("q1_copied", 2 * n2 + g + 1)
                            else:
                                wait("qq_read", lv - 1)
                            for x in range(4):
                                last = nc.tensor.matmul((A, B)[g][:, 0, x * P:(x + 1) * P], Mab[g][:, x, :], Q[g][:, x, :], start=True, stop=True)
                            last.then_inc(s["p_mm"], 1)
                        for g in range(2):
                            lv = 10 * n2 + 2 * i + g
                            wait("p_read", lv + 1)
                            for x in range(4):
                                if i < len(LEVELS) - 1:
                                    nc.tensor.matmul((A, B)[g][:, 1, x * P:(x + 1) * P], QT[g][:, x, :], Pm[g][:, x, :], start=True, stop=True)
                                last = nc.tensor.matmul((C, Dd)[g][:, 1, x * P:(x + 1) * P], Pm[g][:, x, :], QT[g][:, x, :], start=True, stop=True)
                            last.then_inc(s["qq_mm"], 1)
                    for g in range(2):
                        for x in range(4):
                            j, h = divmod(x, 2)
                            last = nc.tensor.matmul((Dd, C)[g][:, 0, x * L:(x + 1) * L], Mak[g][:, x, :], nat[g][j][:, 3, h * L:(h + 1) * L], start=True, stop=True)
                        last.then_inc(s["x_mm"], 1)
                    wait("qq_read", 10 * n2 + 10)
                    for g in range(2):
                        wait("x_read", 2 * n2 + g + 1)
                        for x in range(4):
                            last = nc.tensor.matmul((Dd, C)[g][:, 1, x * P:(x + 1) * P], QT[g][:, x, :], X0[g][:, x, :], start=True, stop=True)
                        last.then_inc(s["xa_mm"], 1)
                    for g in range(2):
                        wait("xa_read", 2 * n2 + g + 1)
                        for x in range(4):
                            j, h = divmod(x, 2)
                            no = L if h == 0 else 0
                            c = slice(x * P, (x + 1) * P)
                            if g == 1 and x == 3:
                                wait("gh_read", 2 * n2 + 1)
                            nc.tensor.matmul(B[:, g, c], XA[g][:, x, :], Mrb[g][:, x, :], start=True, stop=False, skip_group_check=True)
                            last = nc.tensor.matmul(B[no:no + L, g, c], nat[g][j][:, 3, h * L:(h + 1) * L], Mrk[g][:, x, :], start=False, stop=True,
                                                    skip_group_check=True)
                        last.then_inc(s["rn_mm"], 1)
                        for x in range(4):
                            j, h = divmod(x, 2)
                            ao, no = (0, L) if h == 0 else (L, 0)
                            orow = slice(h * L, (h + 1) * L)
                            for q in range(2):
                                rows = slice(q * L, (q + 1) * L)
                                hc = slice(h * L, (h + 1) * L)
                                g_out = A[orow, q, j * L:(j + 1) * L]
                                h_out = A[orow, q, (2 + j) * L:(3 + j) * L]
                                nc.tensor.matmul(g_out, XA[g][rows, x, ao:ao + L], nat[g][j][rows, 1, hc], start=True, stop=True)
                                nc.tensor.matmul(h_out, nat[g][j][rows, 1, hc], XA[g][rows, x, no:no + L], start=True, stop=False)
                                last = nc.tensor.matmul(h_out, nat[g][j][rows, 2, hc], nat[g][j][rows, 3, hc], start=False, stop=True)
                        last.then_inc(s["gh_mm"], 1)
                wait("gh_read", 4)
                wait("rn_read", 4)
                for c in range(16):
                    wait("s_done", c + 1)
                    nc.tensor.matmul(Dd[:, 0, (c % 2) * L:(c % 2 + 1) * L], GT[:, c, :], ST[:, c, :], start=True, stop=True)\
                        .then_inc(s["s_mm"], 1)
                    for h in range(2):
                        rows = slice(h * L, (h + 1) * L)
                        last = nc.tensor.matmul(B[rows, c // 8, (c % 8) * L:(c % 8 + 1) * L], ST[rows, c, :], rh[rows, c * L:(c + 1) * L],
                                                start=True, stop=True)
                last.then_inc(s["y_mm"], 1)
                wait("y_read", 1)
                for t in range(NH):
                    c = slice(t * HALF, (t + 1) * HALF)
                    last = nc.tensor.matmul(A[:, t, :], blockones[:], y[:, c], start=True, stop=True)
                last.then_inc(s["mean_mm"], 1)
                wait("var_sq", 1)
                for t in range(NH):
                    c = slice(t * HALF, (t + 1) * HALF)
                    last = nc.tensor.matmul(B[:, t, :], blockones[:], t2[:, c], start=True, stop=True)
                last.then_inc(s["var_mm"], 1)
                wait("var_root", 1)

            turns(pe, body)

        @block.vector
        def _(dve):
            dve.wait_ge(s["const_in"], 96)
            nc.vector.memset(GT[:], 0.0).then_inc(s["setup"], 1)
            dve.wait_ge(s["setup"], 1)
            K = VSTEPS

            def body(f, wait):
                st = Steps(dve, s["vector_step"], f * K)
                tt = lambda o, x, yv, op: nc.vector.tensor_tensor(o, x, yv, op)
                ts = lambda o, x, s1, s2, o0, o1=ALU.bypass: nc.vector.tensor_scalar(o, x, s1, s2, o0, o1)
                for i, n in enumerate(("rw_w0_2", "rw_a0_2", "rw_k_k_2", "rw_k_a_2", None, "rw_r_k_2", "rw_lnx_w_2", "rw_lnx_b_2")):
                    if n:
                        st.do(ts(cols[:, i:i + 1], prm[:, bass.ds(f + PRM[n], 1)], 1.0, None, ALU.mult))
                st.do(nc.vector.memset(cols[:, 9:10], 64e-5))
                st.wait()
                ts(cols[:, 4:5], cols[:, 3:4], -1.0, 1.0, ALU.mult, ALU.add).then_inc(s["cols_done"], 1)
                wait("cols_done", 1)
                wait("z_in", 96)
                st.link(ts(kk[:], k[:], cols[:, 2:3], None, ALU.mult))
                tt(t1[:], kk[:], kk[:], ALU.mult).then_inc(s["kk_sq"], 1)
                wait("lora_w_read", 1)
                st.link(ts(lw[:], lw[:], -DECAY, None, ALU.mult))
                st.link(nc.vector.tensor_tensor_scan(cs[:], chunk_mask[:], lw[:], 0.0, ALU.mult, ALU.add))
                st.do(tt(t2[:], cs[:], lw[:], ALU.subtract))
                ch = lambda x: x[:].rearrange("p (c t) -> p c t", t=L)
                tt(ch(e3), ch(cs)[:, :, L - 1:L].broadcast_to([P, S // L, L]), ch(cs), ALU.subtract).then_inc(s["scanned"], 1)
                wait("lora_a_read", 1)
                st.link(ts(t3[:], a[:], cols[:, 3:4], cols[:, 4:5], ALU.mult, ALU.add))
                st.link(tt(k[:], k[:], t3[:], ALU.mult))
                nc.vector.scalar_tensor_tensor(out=t3[:], in0=r[:], scalar=cols[:, 5:6], in1=k[:], op0=ALU.mult, op1=ALU.mult)\
                    .then_inc(s["rtk"], 1)
                wait("kk_root", 1)
                st.link(ts(t1[:], t1[:], 1e-12, None, ALU.max))
                st.link(nc.vector.reciprocal(t1[:], t1[:]))
                st.link(tt(kk[:], kk[:], t1[:], ALU.mult))
                st.link(tt(a[:], kk[:], a[:], ALU.mult))
                wait("exp4", 1)
                st.do(tt(bb[:], a[:], e3[:], ALU.mult))
                st.do(tt(kb[:], k[:], e3[:], ALU.mult))
                st.wait()
                st.do(tt(a[:], a[:], e2[:], ALU.mult))
                st.do(tt(lw[:], k[:], e2[:], ALU.mult))
                st.do(nc.vector.scalar_tensor_tensor(out=kk[:], in0=kk[:], scalar=-1.0, in1=t2[:], op0=ALU.mult, op1=ALU.mult))
                st.do(tt(r[:], r[:], e1[:], ALU.mult))
                nc.vector.tensor_copy(wend[:], ch(e1)[:, :, L - 1]).then_inc(s["prep"], 1)
                wait("bonus_mm", 1)
                tt(two(t4), A[:], two(v), ALU.mult).then_inc(s["bonus_read"], 1)
                src = lambda bank, m: bank[:, :, 2 * m * P:(2 * m + 2) * P].rearrange("p h (j t) -> p j h t", t=P)
                dst = lambda x: x[:].rearrange("p (j h) t -> p j h t", h=2)
                mk = lambda i: masks[:, i, :].unsqueeze(1).broadcast_to([P, 4, P])
                for n2 in range(2):
                    for g in range(2):
                        n = 2 * n2 + g
                        wait("m_done", 2 * n + 1)
                        for j in range(2):
                            for (o, m, i) in ((Mab, 0, 0), (Mak, 1, 0)):
                                st.do(tt(dst(o[g])[:, j], src(A, m)[:, j], masks[:, i, :].unsqueeze(1).broadcast_to([P, 2, P]), ALU.mult))
                        st.wait()
                        st.link(tt(QT[g][:], Mab[g][:], mk(2), ALU.mult))
                        tt(QT[g][:], QT[g][:], ident[:].unsqueeze(1).broadcast_to([P, 4, P]), ALU.add).then_inc(s["m1_read"], 1)
                        wait("m_done", 2 * n + 2)
                        for j in range(2):
                            for (o, m, i) in ((Mrb, 0, 1), (Mrk, 1, 1)):
                                last = tt(dst(o[g])[:, j], src(B, m)[:, j], masks[:, i, :].unsqueeze(1).broadcast_to([P, 2, P]), ALU.mult)
                                if (j, m) != (1, 1):
                                    st.do(last)
                        last.then_inc(s["m2_read"], 1)
                    for i in range(len(LEVELS)):
                        for g in range(2):
                            lv = 10 * n2 + 2 * i + g
                            wait("p_mm", lv + 1)
                            if i == 0:
                                wait("q1_copied", 2 * n2 + g + 1)
                            tt(Pm[g][:], (A, B)[g][:, 0, :].rearrange("p (x t) -> p x t", t=P), mk(3 + i), ALU.mult).then_inc(s["p_read"], 1)
                        for g in range(2):
                            lv = 10 * n2 + 2 * i + g
                            wait("qq_mm", lv + 1)
                            if i < len(LEVELS) - 1:
                                st.do(tt(Q[g][:], Q[g][:], (A, B)[g][:, 1, :].rearrange("p (x t) -> p x t", t=P), ALU.add))
                            tt(QT[g][:], QT[g][:], (C, Dd)[g][:, 1, :].rearrange("p (x t) -> p x t", t=P), ALU.add).then_inc(s["qq_read"], 1)
                    for g in range(2):
                        n = 2 * n2 + g
                        wait("rn_mm", n + 1)
                        for h in range(2):
                            rows, other = slice(h * L, (h + 1) * L), slice((1 - h) * L, (2 - h) * L)
                            c = slice(2 * n * P, (2 * n + 2) * P)
                            pair = lambda x: x.rearrange("p (j t) -> p j t", t=P)
                            b3 = B[:, g, :].rearrange("p (j h t) -> p h j t", h=2, t=P)
                            st.do(tt(pair(rh[rows, c]), b3[rows, h], pair(r[rows, c]), ALU.add))
                            last = nc.vector.tensor_copy(pair(y[rows, c]), b3[other, h])
                            if h == 0:
                                st.do(last)
                        last.then_inc(s["rn_read"], 1)
                        wait("gh_mm", n + 1)
                        for j in range(2):
                            for q in range(2):
                                c = 4 * n + 2 * j + q
                                for h in range(2):
                                    rows = slice(h * L, (h + 1) * L)
                                    st.do(nc.vector.scalar_tensor_tensor(out=GT[rows, c, rows], in0=eye2[rows, :], scalar=wend[rows, c:c + 1],
                                                                         in1=A[rows, q, j * L:(j + 1) * L], op0=ALU.mult, op1=ALU.add))
                                last = nc.vector.tensor_copy(H[:, c, :], A[:, q, (2 + j) * L:(3 + j) * L])
                                if (j, q) != (1, 1):
                                    st.do(last)
                        last.then_inc(s["gh_read"], 1)
                wait("gh_read", 4)
                nc.vector.memset(ST[:, 0, :], 0.0).then_inc(s["s_done"], 1)
                for c in range(15):
                    wait("s_mm", c + 1)
                    tt(ST[:, c + 1, :], Dd[:, 0, (c % 2) * L:(c % 2 + 1) * L], H[:, c, :], ALU.add).then_inc(s["s_done"], 1)
                wait("y_mm", 1)
                tt(two(y), two(y), B[:], ALU.add).then_inc(s["y_read"], 1)
                wait("mean_mm", 1)
                st.link(ts(two(t1), A[:], 1.0 / L, None, ALU.mult))
                st.link(tt(y[:], y[:], t1[:], ALU.subtract))
                tt(t2[:], y[:], y[:], ALU.mult).then_inc(s["var_sq"], 1)
                wait("var_root", 1)
                st.link(nc.vector.reciprocal(t1[:], t1[:]))
                st.link(tt(y[:], y[:], t1[:], ALU.mult))
                st.link(ts(y[:], y[:], cols[:, 6:7], cols[:, 7:8], ALU.mult, ALU.add))
                st.link(tt(y[:], y[:], t4[:], ALU.add))
                tt(y[:], y[:], gate[:], ALU.mult).then_inc(s["out_pre"], 1)
                wait("out_pre", 1)
                tile = lambda x: x[:, bass.ds(f, 1), :].rearrange("p k t -> p (k t)")
                st.link(ts(tile(hi), y[:], 1.0, None, ALU.mult))
                tt(tile(lo), y[:], tile(hi), ALU.subtract).then_inc(s["turn_done"], 1)
                wait("turn_done", 1)
                assert st.n == VSTEPS, st.n

            turns(dve, body)


S5_G, S5_P, S5_C = 32, 64, 16
GP = S5_G // 2
SEG, LEN = 8, 16
STEP = 8
NCK = S // STEP


def s5_buffers(mem):
    return dict(
        vin=mem.at("s5_vin", 104, [P, GP, 2, P]),
        wc=mem.at("s5_wc", 120, [P, 2, GP, STEP + 1, S5_C]),
        toep=mem.at("s5_toep", 138, [P, S5_G, P]),
        pw=mem.at("s5_pw", 154, [P, 2, GP, STEP + 1]),
        u8=mem.at("s5_u8", 155.5, [P, S5_G, NCK]),
    )


def s5_setup(nc, mem, env, B5, uperm, ins):
    ident = env["ident"]
    vin, wc, toep, pw, u8 = (B5[n] for n in ("vin", "wc", "toep", "pw", "u8"))
    rows = mem.at("s5_rows", 200, [GP, 3, P])
    dt_row = mem.at("s5_dt_row", 201.5, [GP, 2])
    d_row = mem.at("s5_d_row", 201.75, [S5_G, S5_C])
    crow = mem.at("s5_crow", 202, [P, 2, 4, P])
    ab = mem.at("s5_ab", 175, [P, 32, GP])
    braw = mem.at("s5_b", 177, [P, 2, GP, S5_C])
    bbar = mem.at("s5_bbar", 179, [P, 2, GP, S5_C])
    cT = mem.at("s5_cT", 181, [P, 2, GP, S5_C])
    powr = mem.at("s5_powr", 183, [P, 2, GP, STEP])
    wb = mem.at("s5_wb", 184, [P, 2, GP, STEP, S5_C])
    tmp = mem.at("s5_tmp", 56, [P, GP, STEP + 1, S5_C])
    kall = mem.at("s5_kall", 88, [S5_C, S5_G, STEP, S5_C])
    dsk = mem.at("s5_dsk", 65, [S5_C, S5_G])
    eyed = mem.at("s5_eyed", 66, [S5_C, S5_G, S5_C])
    names = "dt_in dt_row_done turned_in params_in b_in u_in rows_turned rows_copied step trig0 trig1 exp_dt exp_mag wb_done wc_done turned0 turned1 vin_copied0 vin_copied1 c_turned k_mm k_copied k_skip toep_zero banded ramp"
    banks = [("r", [P, 3, GP], F32), ("d", [S5_C, S5_G], F32), ("c", [P, 2, 4, P], F32), ("t0", [P, 4, P], F32), ("t1", [P, 4, P], F32),
             ("k0", [S5_C, 4, P], F32), ("k1", [S5_C, 4, P], F32)]
    dre, dim, dt, x, th, n_, rr, cosv, sinv, mag, pr, den, cre, cim, tA, tB, tC = range(17)
    col = lambda i: ab[:, i, :]
    with phase(nc, names, banks) as (block, s, ps):
        @block.sync
        def _(sp):
            for i, name in enumerate(("s5_a_re_2", "s5_a_im_2")):
                sp.dma_start(rows[:, i, :], ins[name].rearrange("a (g o) p -> (a g) (o p)", o=2)).then_inc(s["params_in"], 16)
            sp.dma_start(dt_row[:], ins["s5_log_dt_2"].rearrange("a (g o) -> (a g) o", o=2)).then_inc(s["dt_in"], 16)
            sp.dma_start(d_row[:], ins["s5_d_2"].rearrange("a g c -> (a g) c")).then_inc(s["params_in"], 16)
            for i, name in enumerate(("s5_c_re_2", "s5_c_im_2")):
                cv = ins[name].rearrange("a (b g) c p -> (a g c) b p", b=4)
                for half in range(2):
                    sp.dma_start(crow[:, i, :, half * S5_P:(half + 1) * S5_P], cv).then_inc(s["params_in"], 16)
            for i, name in enumerate(("s5_b_re_2", "s5_b_im_2")):
                sp.dma_start(braw[:, i], ins[name].rearrange("a (g o) p c -> (a o p) g c", o=2)).then_inc(s["b_in"], 16)
            for j in range(STEP):
                sp.dma_start(u8[j * S5_C:(j + 1) * S5_C], uperm[:, j, :].rearrange("(g c) m -> c g m", c=S5_C)).then_inc(s["u_in"], 16)
            sp.wait_ge(s["k_skip"], 1)
            sp.wait_ge(s["toep_zero"], 1)
            for j in range(STEP):
                sp.dma_start(toep[j * S5_C:(j + 1) * S5_C, :, j * S5_C:].rearrange("p g (i c) -> p g i c", c=S5_C),
                             kall[:, :, 0:STEP - j, :]).then_inc(s["banded"], 16)
            sp.wait_ge(s["banded"], 16 * STEP)
            sp.wait_ge(s["u_in"], 16 * STEP)

        @block.gpsimd
        def _(pool):
            nc.gpsimd.memset(toep[:], 0.0).then_inc(s["toep_zero"], 1)

        @block.scalar
        def _(act):
            act.wait_ge(s["turned_in"], 1)
            nc.scalar.activation(col(dt), col(dt), ACT.Exp).then_inc(s["exp_dt"], 1)
            act.wait_ge(s["ramp"], 1)
            nc.scalar.activation(col(mag), col(x), ACT.Exp).then_inc(s["exp_mag"], 1)
            act.wait_ge(s["ramp"], 2)
            nc.scalar.activation(col(sinv), col(rr), ACT.Sin).then_inc(s["trig0"], 1)
            act.wait_ge(s["ramp"], 3)
            nc.scalar.activation(col(cosv), col(tC), ACT.Sin).then_inc(s["trig1"], 1)
            for gq in range(8):
                b = gq % 2
                act.wait_ge(s[f"turned{b}"], gq // 2 + 1)
                nc.scalar.activation(vin[:, 2 * gq:2 * gq + 2].rearrange("p g r c -> p (g r) c"), ps[f"t{b}"][:], ACT.Copy).then_inc(s[f"vin_copied{b}"], 1)

        @block.tensor
        def _(pe):
            pe.wait_ge(s["params_in"], 16 * 7)
            pe.wait_ge(s["dt_row_done"], 1)
            nc.tensor.transpose(ps["d"][:], d_row[:], ident[0:S5_G, 0:S5_G])
            for i in range(3):
                nc.tensor.transpose(ps["r"][:, i, :], rows[:, i, :], ident[0:GP, 0:GP])
            for i in range(2):
                for e in range(4):
                    last = nc.tensor.transpose(ps["c"][:, i, e, :], crow[:, i, e, :], ident[:])
            last.then_inc(s["rows_turned"], 1)
            pe.wait_ge(s["wb_done"], 1)
            for gq in range(8):
                b = gq % 2
                pe.wait_ge(s[f"vin_copied{b}"], gq // 2)
                for q in range(4):
                    gp, ri = 2 * gq + q // 2, q % 2
                    last = nc.tensor.transpose(ps[f"t{b}"][:, q, :], wb[:, ri, gp].rearrange("p j c -> p (j c)"), ident[:])
                last.then_inc(s[f"turned{b}"], 1)
            pe.wait_ge(s["wc_done"], 1)
            for gq in range(4):
                pe.wait_ge(s["k_copied"], gq)
                for q in range(4):
                    gp = 4 * gq + q
                    for ri in range(2):
                        for o in range(2):
                            rws = slice(o * S5_P, (o + 1) * S5_P)
                            last = nc.tensor.matmul(ps[f"k{o}"][:, q, :], wb[rws, ri, gp, STEP - 1, :],
                                                    wc[rws, ri, gp, 0:STEP, :].rearrange("p m c -> p (m c)"), start=(ri == 0), stop=(ri == 1))
                last.then_inc(s["k_mm"], 1)

        @block.vector
        def _(dve):
            st = Steps(dve, s["step"])
            tt = lambda o, xx, yv, op: st.link(nc.vector.tensor_tensor(o, xx, yv, op))
            ts = lambda o, xx, s1, s2, o0, o1=ALU.bypass: st.link(nc.vector.tensor_scalar(o, xx, s1, s2, o0, o1))
            dve.wait_ge(s["dt_in"], 16)
            nc.vector.tensor_copy(rows[:, 2, :].rearrange("g (o p) -> g o p", o=2), dt_row[:].unsqueeze(2).broadcast_to([GP, 2, S5_P]))\
                .then_inc(s["dt_row_done"], 1)
            dve.wait_ge(s["rows_turned"], 1)
            st.do(nc.vector.tensor_copy(dsk[:], ps["d"][:]))
            nc.vector.tensor_copy(ab[:, dre:dt + 1, :], ps["r"][:]).then_inc(s["turned_in"], 1)
            dve.wait_ge(s["turned_in"], 1)
            for ri in range(2):
                for o in range(2):
                    half = slice(o * S5_P, (o + 1) * S5_P)
                    src = ps["c"][half, ri].rearrange("p e (g o c) -> p (e g) o c", o=2, c=S5_C)[:, :, o]
                    st.do(nc.vector.tensor_copy(cT[half, ri], src))
            st.wait()
            dve.wait_ge(s["exp_dt"], 1)
            tt(col(th), col(dt), col(dim), ALU.mult)
            nc.vector.tensor_tensor(col(x), col(dt), col(dre), ALU.mult).then_inc(s["ramp"], 1)
            ROUND = 12582912.0
            ts(col(n_), col(th), float(0.5 / np.pi), ROUND, ALU.mult, ALU.add)
            ts(col(n_), col(n_), ROUND, None, ALU.subtract)
            c1 = 6.28125
            c2 = float(np.float32(2 * np.pi - c1))
            c3 = float(2 * np.pi - c1 - c2)
            stt = lambda o, i0, sc, i1: st.link(nc.vector.scalar_tensor_tensor(out=o, in0=i0, scalar=sc, in1=i1, op0=ALU.mult, op1=ALU.add))
            stt(col(rr), col(n_), -c1, col(th))
            stt(col(rr), col(n_), -c2, col(rr))
            stt(col(rr), col(n_), -c3, col(rr))
            nc.vector.tensor_scalar(col(rr), col(rr), 3.1415925, -3.1415925, ALU.min, ALU.max).then_inc(s["ramp"], 1)
            dve.wait_ge(s["ramp"], 2)
            ts(col(tB), col(rr), -1.0, None, ALU.mult)
            tt(col(tC), col(rr), col(tB), ALU.max)
            nc.vector.tensor_scalar(col(tC), col(tC), -1.0, float(np.pi / 2), ALU.mult, ALU.add).then_inc(s["ramp"], 1)
            dve.wait_ge(s["trig1"], 1)
            dve.wait_ge(s["trig0"], 1)
            dve.wait_ge(s["exp_mag"], 1)
            P0 = lambda ri, m: pw[:, ri, :, m]
            st.do(nc.vector.memset(pw[:, 0, :, 0], 1.0))
            st.do(nc.vector.memset(pw[:, 1, :, 0], 0.0))
            tt(P0(0, 1), col(mag), col(cosv), ALU.mult)
            tt(P0(1, 1), col(mag), col(sinv), ALU.mult)
            ts(col(pr), P0(0, 1), -1.0, None, ALU.add)
            tt(col(tA), col(dre), col(dre), ALU.mult)
            tt(col(tB), col(dim), col(dim), ALU.mult)
            tt(col(den), col(tA), col(tB), ALU.add)
            st.link(nc.vector.reciprocal(col(den), col(den)))
            tt(col(tA), col(pr), col(dre), ALU.mult)
            tt(col(tB), P0(1, 1), col(dim), ALU.mult)
            tt(col(cre), col(tA), col(tB), ALU.add)
            tt(col(cre), col(cre), col(den), ALU.mult)
            tt(col(tA), P0(1, 1), col(dre), ALU.mult)
            tt(col(tB), col(pr), col(dim), ALU.mult)
            tt(col(cim), col(tA), col(tB), ALU.subtract)
            tt(col(cim), col(cim), col(den), ALU.mult)
            dve.wait_ge(s["b_in"], 32)

            def complex_product(o_re, o_im, xr, xi, yr, yi, t, minus_im=False, done=None):
                tt(o_re, xr, yr, ALU.mult)
                tt(t, xi, yi, ALU.mult)
                tt(o_re, o_re, t, ALU.subtract)
                tt(o_im, xr, yi, ALU.mult)
                tt(t, xi, yr, ALU.mult)
                if minus_im:
                    last = nc.vector.scalar_tensor_tensor(out=o_im, in0=o_im, scalar=-1.0, in1=t, op0=ALU.mult, op1=ALU.subtract)
                else:
                    last = nc.vector.tensor_tensor(o_im, o_im, t, ALU.add)
                if done:
                    last.then_inc(s[done], 1)
                else:
                    st.link(last)

            wide = lambda v: v.unsqueeze(2).broadcast_to([P, GP, S5_C])
            complex_product(bbar[:, 0], bbar[:, 1], wide(col(cre)), wide(col(cim)), braw[:, 0], braw[:, 1], tmp[:, :, 0, :])
            for m in range(2, STEP + 1):
                complex_product(P0(0, m), P0(1, m), P0(0, 1), P0(1, 1), P0(0, m - 1), P0(1, m - 1), col(tC))
            for j in range(STEP):
                st.do(nc.vector.tensor_copy(powr[:, :, :, j], pw[:, :, :, STEP - 1 - j]))
            st.wait()
            full = [P, GP, STEP, S5_C]
            pf = lambda ri: powr[:, ri].unsqueeze(3).broadcast_to(full)
            bf = lambda ri: bbar[:, ri].unsqueeze(2).broadcast_to(full)
            complex_product(wb[:, 0], wb[:, 1], pf(0), pf(1), bf(0), bf(1), tmp[:, :, 0:STEP, :], done="wb_done")
            full9 = [P, GP, STEP + 1, S5_C]
            pf9 = lambda ri: pw[:, ri].unsqueeze(3).broadcast_to(full9)
            cf9 = lambda ri: cT[:, ri].unsqueeze(2).broadcast_to(full9)
            complex_product(wc[:, 0], wc[:, 1], pf9(0), pf9(1), cf9(0), cf9(1), tmp[:], minus_im=True, done="wc_done")
            st.link(nc.vector.tensor_tensor(eyed[:], ident[0:S5_C, 0:S5_C].unsqueeze(1).broadcast_to([S5_C, S5_G, S5_C]),
                                            dsk[:].unsqueeze(2).broadcast_to([S5_C, S5_G, S5_C]), ALU.mult))
            for gq in range(4):
                dve.wait_ge(s["k_mm"], gq + 1)
                for o in range(2):
                    dst = kall[:, 8 * gq:8 * gq + 8].rearrange("p (g o) m c -> p o g (m c)", o=2)[:, o]
                    last = nc.vector.tensor_copy(dst, ps[f"k{o}"][:])
                last.then_inc(s["k_copied"], 1)
            dve.wait_ge(s["k_copied"], 4)
            nc.vector.tensor_tensor(kall[:, :, 0, :], kall[:, :, 0, :], eyed[:], ALU.add).then_inc(s["k_skip"], 1)


def s5_run(nc, mem, env, B5, yperm):
    vin, wc, toep, pw, u8 = (B5[n] for n in ("vin", "wc", "toep", "pw", "u8"))
    z = mem.at("s5_z", 172, [P, 2, GP, NCK])
    sp_ = mem.at("s5_s", 56, [P, NCK, 2, GP])
    sT = mem.at("s5_sT", 188, [P, 2, GP, NCK])
    trans = mem.at("s5_trans", 88, [P, 2, 2, 2, GP])
    t = [mem.at(f"s5_tmp{i}", 89 + i, [P, SEG, 2, GP]) for i in range(3)]
    power = mem.at("s5_power", 96, [P, 2, LEN + 1, GP])
    start = mem.at("s5_start", 99, [P, SEG, 2, GP])
    ct = mem.at("s5_ct", 100, [P, LEN // 2, GP])
    full = [mem.at(f"s5_full{i}", 172 + 8 * i, [P, SEG, LEN, GP]) for i in range(2)]
    y8 = mem.at("s5_y8", 92, [P, 2, 4, NCK])
    names = "z_mm0 z_mm1 z_read0 z_read1 step scanned turned " + both("y_mm y_read y_stored")
    banks = [("z0", [P, 4, P], F32), ("z1", [P, 4, P], F32), ("y0", [P, 4, P], F32), ("y1", [P, 4, P], F32)]
    with phase(nc, names, banks) as (block, s, ps):
        @block.tensor
        def _(pe):
            for gp in range(GP):
                b = gp // 2 % 2
                if gp % 2 == 0:
                    pe.wait_ge(s[f"z_read{b}"], gp // 4)
                for ri in range(2):
                    for o in range(2):
                        last = nc.tensor.matmul(ps[f"z{b}"][o * S5_P:(o + 1) * S5_P, (gp % 2) * 2 + ri, :],
                                                vin[:, gp, ri, o * S5_P:(o + 1) * S5_P], u8[:, 2 * gp + o, :], start=True, stop=True)
                if gp % 2:
                    last.then_inc(s[f"z_mm{b}"], 1)
            pe.wait_ge(s["turned"], 1)
            for h in range(GP // 4):
                for o in range(2):
                    rws = slice(o * S5_P, (o + 1) * S5_P)
                    pe.wait_ge(s[f"y_read{o}"], h)
                    for q in range(4):
                        gp = 4 * h + q
                        out = ps[f"y{o}"][:, q, :]
                        nc.tensor.matmul(out, toep[:, 2 * gp + o, :], u8[:, 2 * gp + o, :], start=True, stop=False)
                        for ri in range(2):
                            last = nc.tensor.matmul(out, wc[rws, ri, gp, 1:STEP + 1, :].rearrange("p m c -> p (m c)"),
                                                    sT[rws, ri, gp, :], start=False, stop=(ri == 1))
                    last.then_inc(s[f"y_mm{o}"], 1)

        @block.scalar
        def _(act):
            rows = yperm.rearrange("(g o c) j m -> o j c g m", o=2, c=S5_C)
            for h in range(GP // 4):
                for o in range(2):
                    act.wait_ge(s[f"y_mm{o}"], h + 1)
                    if h > 0:
                        act.wait_ge(s[f"y_stored{o}"], 16 * STEP * h)
                    nc.scalar.activation(y8[:, o], ps[f"y{o}"][:], ACT.Copy).then_inc(s[f"y_read{o}"], 1)
                    act.wait_ge(s[f"y_read{o}"], h + 1)
                    for i in range(STEP):
                        act.dma_start(rows[o, i, :, 4 * h:4 * h + 4], y8[i * S5_C:(i + 1) * S5_C, o]).then_inc(s[f"y_stored{o}"], 16)
            for b in range(2):
                act.wait_ge(s[f"y_stored{b}"], 16 * STEP * 4)

        @block.vector
        def _(dve):
            st = Steps(dve, s["step"])
            tt = lambda o, x, y, op: nc.vector.tensor_tensor(o, x, y, op)

            def complex_product(o_re, o_im, xr, xi, yr, yi, tmp):
                st.do(tt(o_re, xr, yr, ALU.mult))
                st.link(tt(tmp, xi, yi, ALU.mult))
                st.do(tt(o_re, o_re, tmp, ALU.subtract))
                st.do(tt(o_im, xr, yi, ALU.mult))
                st.wait()
                st.link(tt(tmp, xi, yr, ALU.mult))
                st.link(tt(o_im, o_im, tmp, ALU.add))

            for ri in range(2):
                st.do(nc.vector.tensor_copy(power[:, ri, 1, :], pw[:, ri, :, STEP]))
                st.do(nc.vector.memset(power[:, ri, 0, :], 1.0 - ri))
            st.wait()
            known = 1
            while known < LEN:
                top = lambda ri: power[:, ri, known:known + 1, :].broadcast_to([P, known, GP])
                complex_product(*(power[:, ri, known + 1:2 * known + 1, :] for ri in range(2)),
                                *(power[:, ri, 1:known + 1, :] for ri in range(2)), top(0), top(1), ct[:, 0:known, :])
                known *= 2
            for i, e in enumerate((1, LEN)):
                for ri in range(2):
                    st.do(nc.vector.tensor_copy(trans[:, i, 0, ri, :], power[:, 0, e, :]))
                st.do(nc.vector.tensor_scalar(trans[:, i, 1, 0, :], power[:, 1, e, :], -1.0, None, ALU.mult))
                st.do(nc.vector.tensor_copy(trans[:, i, 1, 1, :], power[:, 1, e, :]))
            for gh in range(8):
                b = gh % 2
                dve.wait_ge(s[f"z_mm{b}"], gh // 2 + 1)
                dst = z[:, :, 2 * gh:2 * gh + 2, :].rearrange("p r g m -> p g r m")
                src = ps[f"z{b}"][:].rearrange("p (g r) m -> p g r m", r=2)
                nc.vector.tensor_copy(dst[:, 0], src[:, 0])
                nc.vector.tensor_copy(dst[:, 1], src[:, 1]).then_inc(s[f"z_read{b}"], 1)
            dve.wait_ge(s["z_read0"], 4)
            dve.wait_ge(s["z_read1"], 4)
            st.wait()

            def step(new, now, add, i):
                n = now.shape[1]
                wide = lambda v: v.unsqueeze(1).broadcast_to([P, n, *v.shape[1:]])
                a, b, c = (x[:, 0:n] for x in t)
                st.do(tt(a, now, wide(trans[:, i, 0]), ALU.mult))
                for ri in range(2):
                    st.do(tt(b[:, :, ri], now[:, :, 1 - ri], wide(trans[:, i, 1, ri]), ALU.mult))
                st.wait()
                st.link(tt(c, a, b, ALU.add))
                st.link(tt(new, c, add, ALU.add))

            local = sp_[:].rearrange("p (s i) r g -> p i s r g", i=LEN)
            zi = z[:].rearrange("p r g (s i) -> p i s r g", i=LEN)
            st.do(nc.vector.memset(local[:, 0], 0.0))
            st.do(nc.vector.memset(start[:, 0], 0.0))
            st.link(nc.vector.tensor_copy(local[:, 1], zi[:, 0]))
            for i in range(1, LEN - 1):
                step(local[:, i + 1], local[:, i], zi[:, i], 0)
            step(zi[:, 0], local[:, LEN - 1], zi[:, LEN - 1], 0)
            for g in range(SEG - 1):
                step(start[:, g + 1:g + 2], start[:, g:g + 1], z[:, :, :, g * LEN:g * LEN + 1].rearrange("p r g m -> p m r g"), 1)
            shape = [P, SEG, LEN, GP]
            pb = lambda ri: power[:, ri, 0:LEN, :].unsqueeze(1).broadcast_to(shape)
            sb = lambda ri: start[:, :, ri].unsqueeze(2).broadcast_to(shape)
            for ri in range(2):
                st.do(tt(full[0][:], pb(0), sb(ri), ALU.mult))
                st.link(tt(full[1][:], pb(1), sb(1 - ri), ALU.mult))
                st.link(tt(full[0][:], full[0][:], full[1][:], ALU.add if ri else ALU.subtract))
                last = tt(sT[:, ri].rearrange("p g (s i) -> p s i g", i=LEN), full[0][:],
                          sp_[:, :, ri].rearrange("p (s i) g -> p s i g", i=LEN), ALU.add)
                if ri == 0:
                    st.link(last)
            last.then_inc(s["turned"], 1)


def s5_gate(nc, mem, env, yperm, ins, cat):
    prm, ones = env["prm"], env["ones"]
    zz = mem.at("glu_zz", 136, [P, 4, S])
    z_hi = mem.at("glu_zhi", 152, [P, 4, S], F32R)
    z_lo = mem.at("glu_zlo", 168, [P, 4, S], F32R)
    yin = [mem.at(f"glu_in{b}", 184 + 4 * b, [P, STEP, NCK]) for b in range(2)]
    hi, lo = cat
    with phase(nc, both("y_in done") + "gelu_done high_done low_done", []) as (block, s, ps):
        @block.sync
        def _(sp):
            for k in range(4):
                b = k % 2
                if k >= 2:
                    sp.wait_ge(s["gelu_done"], k - 1)
                sp.dma_start(yin[b][:], yperm[k * P:(k + 1) * P]).then_inc(s[f"y_in{b}"], 16)

        @block.scalar
        def _(act):
            for k in range(4):
                b = k % 2
                act.wait_ge(s[f"y_in{b}"], 16 * (k // 2 + 1))
                nc.scalar.activation(zz[:, k, :].rearrange("p (m j) -> p m j", j=STEP), yin[b][:].rearrange("p j m -> p m j"),
                                     ACT.Gelu_apprx_tanh).then_inc(s["gelu_done"], 1)
                act.wait_ge(s["gelu_done"], k + 1)
                nc.scalar.activation(z_hi[:, k, :], zz[:, k, :], ACT.Copy).then_inc(s["high_done"], 1)

        @block.vector
        def _(dve):
            for k in range(4):
                dve.wait_ge(s["high_done"], k + 1)
                nc.vector.tensor_tensor(z_lo[:, k, :], zz[:, k, :], z_hi[:, k, :], ALU.subtract)

    gout = [mem.at(f"glu_sig{b}", 184 + 4 * b, [P, S]) for b in range(2)]

    def epilogue(block, s, acc, ps):
        @block.scalar
        def _(act):
            for u in range(4):
                p, b = divmod(u, 2)
                act.wait_ge(s[f"products_done{b}"], p + 1)
                act.wait_ge(s[f"epilogue_b{b}"], p)
                c = PRM["s5_b_glu_2"] + u
                nc.scalar.activation(gout[b][:].rearrange("p (h t) -> p h t", h=NH), acc[b][:], ACT.Sigmoid, bias=prm[:, c:c + 1])\
                    .then_inc(s[f"acc_read{b}"], 1)

        @block.vector
        def _(dve):
            for u in range(4):
                p, b = divmod(u, 2)
                dve.wait_ge(s[f"acc_read{b}"], p + 1)
                nc.vector.tensor_tensor(zz[:, u, :], zz[:, u, :], gout[b][:], ALU.mult).then_inc(s[f"epilogue_b{b}"], 1)

    gemm(nc, mem, "glu", 4, 4, columns(ins["s5_w_glu_2"], 4), (z_hi, z_lo), epilogue, 104)

    sq = mem.at("glu_sq", 152, [P, S])
    sums = mem.at("glu_sums", 156, [P, S])
    rs = mem.at("glu_rs", 160, [P, S])
    with phase(nc, "step summed total inverse root scaled high", [("tot", [P, NH, HALF], F32)]) as (block, s, ps):
        @block.vector
        def _(dve):
            st = Steps(dve, s["step"])
            st.link(nc.vector.tensor_tensor(sums[:], zz[:, 0, :], zz[:, 0, :], ALU.mult))
            for k in range(1, 4):
                st.link(nc.vector.tensor_tensor(sq[:], zz[:, k, :], zz[:, k, :], ALU.mult))
                last = nc.vector.tensor_tensor(sums[:], sums[:], sq[:], ALU.add)
                if k < 3:
                    st.link(last)
            last.then_inc(s["summed"], 1)
            dve.wait_ge(s["total"], 1)
            st.link(nc.vector.tensor_scalar(rs[:], ps["tot"][:].rearrange("p h t -> p (h t)"), 1.0 / 512, EPS, ALU.mult, ALU.add))
            nc.vector.reciprocal(rs[:], rs[:]).then_inc(s["inverse"], 1)
            dve.wait_ge(s["root"], 1)
            for k in range(4):
                c = PRM["s5_gain_2"] + k
                nc.vector.scalar_tensor_tensor(out=zz[:, k, :], in0=zz[:, k, :], scalar=prm[:, c:c + 1], in1=rs[:],
                                               op0=ALU.mult, op1=ALU.mult).then_inc(s["scaled"], 1)
                dve.wait_ge(s["high"], k + 1)
                nc.vector.tensor_tensor(lo[:, 4 + k, :], zz[:, k, :], hi[:, 4 + k, :], ALU.subtract)

        @block.tensor
        def _(pe):
            pe.wait_ge(s["summed"], 1)
            for h in range(NH):
                last = nc.tensor.matmul(ps["tot"][:, h, :], ones[:], sums[:, h * HALF:(h + 1) * HALF], start=True, stop=True)
            last.then_inc(s["total"], 1)

        @block.scalar
        def _(act):
            act.wait_ge(s["inverse"], 1)
            nc.scalar.activation(rs[:], rs[:], ACT.Sqrt).then_inc(s["root"], 1)
            for k in range(4):
                act.wait_ge(s["scaled"], k + 1)
                nc.scalar.activation(hi[:, 4 + k, :], zz[:, k, :], ACT.Copy).then_inc(s["high"], 1)


def s5(nc, mem, env, uperm, yperm, ins, cat):
    B5 = s5_buffers(mem)
    s5_setup(nc, mem, env, B5, uperm, ins)
    s5_run(nc, mem, env, B5, yperm)
    s5_gate(nc, mem, env, yperm, ins, cat)


def constants():
    f = np.float32
    c = {"k_ident": np.eye(P, dtype=f)}
    h = np.arange(RET_H, dtype=f)
    lg = np.log1p(-np.exp2(-5.0 - h)).astype(f)
    pos = np.arange(P, dtype=f)
    diff = pos[None, :] - pos[:, None]
    scale = f(RET_DK) ** f(-0.5)
    dm = np.where(diff >= 0, np.exp(lg[:, None, None] * np.maximum(diff, 0.0)), 0.0)
    c["k_dmask"] = (dm * scale).astype(f)
    xi = np.exp(lg[:, None] * (pos + 1.0)).astype(f)
    c["k_xi"] = np.broadcast_to(xi[None], (P, RET_H, P)).copy()
    zeta = np.exp(lg[:, None] * (P - 1 - pos)) * scale
    dec = np.broadcast_to(np.exp(lg * P)[:, None], (RET_H, P))
    c["k_retcol"] = np.concatenate([zeta, dec]).T.astype(f).copy()
    t = np.arange(S)
    onehot = (t[None, :] // 64 == np.arange(N_BLK)[:, None]).astype(f)
    c["k_onehot"] = np.stack([onehot] * NSA_G, 1)
    c["k_slopes"] = np.broadcast_to(np.exp2(-(np.arange(NSA_H, dtype=f) + 1)), (P, NSA_H)).astype(f).copy()
    q = np.arange(P)[:, None]
    d = q + (S - P) - np.arange(2 * S - P)[None, :]
    c["k_dist"] = np.where(d >= 0, -d, NEG).astype(f)
    d = q + WINDOW - np.arange(WINDOW + P)[None, :]
    c["k_dwin"] = np.where((d >= 0) & (d < WINDOW), -d, NEG).astype(f)
    tok = (np.arange(NT)[None, :] * P + q)[:, :, None]
    blk = np.arange(NC_PAD)[None, None, :]
    d = tok - (blk * CMP_STRIDE + CMP_LEN - 1)
    ok = (d >= 0) & (blk < N_CMP)
    c["k_dcmp"] = np.where(ok, -d, NEG).astype(f)
    c["k_cmask"] = ok.astype(f)
    j = np.arange(N_BLK)
    c["k_before"] = np.broadcast_to((j[None, :] < j[:, None]).astype(f), (P, N_BLK, N_BLK)).copy()
    cur, jj = tok // 64, j[None, None, :]
    always = (jj == 0) | (jj == cur) | (jj == cur - 1)
    c["k_keep"] = (~always & (jj <= cur)).astype(f)
    c["k_force"] = np.where(jj > cur, -FORCE, np.where(always, FORCE, 0.0)).astype(f)
    return c


def rwkv_constants():
    f = np.float32
    c = {}
    c["k_chunk"] = np.broadcast_to((np.arange(S) % 64 != 0).astype(f), (P, S)).copy()
    i, t = np.arange(P)[:, None], np.arange(P)[None, :]
    same = i // 64 == t // 64
    m = [same & (i < t), same & (i <= t), same & (i // 2 == t // 2) & (i < t)]
    for sz in (2, 4, 8, 16, 32):
        m.append((i // (2 * sz) == t // (2 * sz)) & (i % (2 * sz) >= sz) & (t % (2 * sz) < sz))
    c["k_masks"] = np.stack(m, 1).astype(f)
    c["k_blockones"] = same.astype(f)
    c["k_eye2"] = np.tile(np.eye(64, dtype=f), (2, 1))
    return c


def build(nc, ins, out):
    mem = Memory(nc)
    env = dict(
        xT=mem.at("xT", 0, [P, KD, S]),
        prm=mem.at("prm", 32, [P, PRM_COLS]),
        ident=mem.at("ident", 34, [P, P]),
        ones=mem.at("ones", 35, [P, P]),
        hi=mem.at("h_hi", 40, [P, KD, S], F32R),
        lo=mem.at("h_lo", 72, [P, KD, S], F32R),
    )
    mem.one = env["ones"][:, 0:1]
    h = (env["hi"], env["lo"])
    scratch = lambda name, shape: nc.dram_tensor(name, shape, F32, kind="Internal").ap()
    projT = scratch("projT", [N_PROJ * P, S])
    proj2T = scratch("proj2T", [N_PROJ2 * P, S])
    yaT = scratch("yaT", [D, S])
    selT = scratch("selT", [NSA_G * N_BLK, S])
    uperm = scratch("uperm", [HALF, STEP, NCK])
    yperm = scratch("yperm", [HALF, STEP, NCK])

    load_parameters(nc, mem, env, ins)
    w_in = ins["w_in"].rearrange("a (k p) n -> (a p) k n", p=P)
    gemm(nc, mem, "proj", N_PROJ, KD, lambda u, shift: w_in[:, :, bass.ds(u * P + shift, P)], h,
         store_epilogue(nc, mem, "proj", 128, N_PROJ, projT), 104,
         norm=SplitNorm(nc, mem, env, "norm_mix", gain=PRM["norm_mix"]), later=(GA // 2, N_GATE, GATE_COL - GATE * P))
    retention(nc, mem, env, projT, ins)
    gemm(nc, mem, "ret_out", KD, KD, columns(ins["w_ret_o"], KD), h,
         gated_epilogue(nc, mem, "ret_out", projT[GA * P:(GA + KD) * P, :], store=yaT), 104)
    N = nsa_buffers(mem)
    nsa_prepare(nc, mem, env, N, projT, ins)
    nsa_compressed(nc, mem, env, N, projT, selT, ins)
    nsa_attend(nc, mem, env, N, projT, selT, ins)
    merged = (mem.at("merged_hi", 128, [P, KD, S], F32R), mem.at("merged_lo", 160, [P, KD, S], F32R))
    gemm(nc, mem, "nsa_out", KD, 4, columns(ins["w_nsa_o"], 4), h,
         gated_epilogue(nc, mem, "nsa_out", projT[GB * P:(GB + KD) * P, :], other=yaT, split=merged), 104, extra="merged ")
    residual_gemm(nc, mem, env, "mix_out", columns(ins["w_out"], KD), merged, KD)
    up = ins["w_up"].rearrange("a (k p) n -> (a p) k n", p=P)
    rows = lambda w: (lambda c: w.rearrange("a (c j p) n -> c (a p) j n", p=P, j=2)[bass.ds(c, 1)].rearrange("c p j n -> (c p) j n"))
    feed_forward(nc, mem, env, "ffn", lambda i, f: up[:, :, bass.ds(f * P + i * FT * P, P)], rows(ins["w_down"]), "conv",
                 SplitNorm(nc, mem, env, "norm_ffn", gain=PRM["norm_ffn"]))

    norm_and_modulation(nc, mem, env, ins, PRM["norm_final"])
    w_in2 = ins["w_in_2"].rearrange("a (k p) n -> (a p) k n", p=P)
    gemm(nc, mem, "proj2_z", UU, KD, lambda u: w_in2[:, :, bass.ds(u * P, P)], h,
         shift_epilogue(nc, mem, env, "proj2_z", 128, UU, proj2T, PRM["mu_shift_2"]), 104,
         norm=SplitNorm(nc, mem, env, "norm_mix2", scale=ADA + 8, shift=ADA))
    gemm(nc, mem, "proj2_u", N_PROJ2 - UU, KD, lambda u: w_in2[:, :, bass.ds((UU + u) * P, P)], h,
         store_epilogue(nc, mem, "proj2_u", 128, N_PROJ2 - UU, uperm.rearrange("r j m -> r (j m)"), STEP), 104)
    rwkv(nc, mem, env, proj2T, ins)
    s5(nc, mem, env, uperm, yperm, ins, h)
    residual_gemm(nc, mem, env, "mix2_out", columns(ins["w_out_2"], KD), h, KD, gate=ADA + 16)
    up2 = [ins[n].rearrange("a (k p) n -> (a p) k n", p=P) for n in ("ffn_w_gate_2", "ffn_w_up_2")]
    feed_forward(nc, mem, env, "ffn2", lambda i, f: up2[i][:, :, bass.ds(f * P, P)], rows(ins["ffn_w_down_2"]), "silu",
                 SplitNorm(nc, mem, env, "norm_ffn2", scale=ADA + 32, shift=ADA + 24), gate=ADA + 40)
    norm_out(nc, mem, env, "final", PRM["final_gain_2"], out)


def kernel(**inputs):
    import concourse.bacc as _bacc
    from concourse.bass_utils import run_bass_kernel_spmd as _run

    nc = _bacc.Bacc("TRN2", target_bir_lowering=False, num_devices=1)
    arrays = {name: np.ascontiguousarray(a) for name, a in inputs.items()}
    arrays.update(constants())
    arrays.update(rwkv_constants())
    args = {name: nc.dram_tensor(name, a.shape, mybir.dt.from_np(a.dtype), kind="ExternalInput").ap() for name, a in arrays.items()}
    out = nc.dram_tensor("out", (1, S, D), F32, kind="ExternalOutput").ap()
    build(nc, args, out)
    r = _run(nc, [arrays], core_ids=[0])
    return r.results[0]["out"]
```
